# Optimizing a Trainium2 kernel written in Bass

```python
import math
import jax, jax.numpy as jnp
from jax import lax
import numpy as np

D_MODEL = 1024
BATCH = 1
SEQ = 256
DEPTH = 2

N_HEADS = 16
HEAD_DIM = D_MODEL // N_HEADS
D_FF = 4 * D_MODEL
N_MIXERS = 2
N_A_LAYERS = (DEPTH + 1) // 2
N_B_LAYERS = DEPTH // 2
NUM_BUCKETS = 32
MAX_DISTANCE = 128
MOBA_BLOCK = 256
MOBA_TOPK = 3
MOBA_Q_CHUNK = 64
DSA_Q_LORA = 256
DSA_KV_LORA = 256
IDX_HEADS = 8
IDX_DIM = 64
DSA_TOPK_MAX = 256
DSA_Q_CHUNK = 128
DSA_IN_DIM = DSA_Q_LORA + DSA_KV_LORA + IDX_DIM + IDX_HEADS
EPS = 1e-6
NEG = -1e30


def rms_norm(x, g):
    x32 = x.astype(jnp.float32)
    y = x32 * lax.rsqrt(jnp.mean(x32 * x32, axis=-1, keepdims=True) + EPS)
    return y.astype(x.dtype) * g

def rel_bucket(dist):
    n = jnp.maximum(dist, 0)
    exact = NUM_BUCKETS // 2
    nf = jnp.maximum(n, 1).astype(jnp.float32)
    large = exact + (jnp.log(nf / exact) / math.log(MAX_DISTANCE / exact) * (NUM_BUCKETS - exact)).astype(jnp.int32)
    large = jnp.minimum(large, NUM_BUCKETS - 1)
    return jnp.where(n < exact, n, large)

def moba_attention(h, w_qkv, w_o, bias_table):
    B, S, _ = h.shape
    H, Dh, BLK, QC = N_HEADS, HEAD_DIM, MOBA_BLOCK, MOBA_Q_CHUNK
    q, k, v = jnp.split(h @ w_qkv, 3, axis=-1)
    q = q.reshape(B, S, H, Dh).transpose(0, 2, 1, 3)
    k = k.reshape(B, S, H, Dh).transpose(0, 2, 1, 3)
    v = v.reshape(B, S, H, Dh).transpose(0, 2, 1, 3)
    n_blk = -(-S // BLK)
    pad = ((0, 0), (0, 0), (0, n_blk * BLK - S), (0, 0))
    kb = jnp.pad(k, pad).reshape(B, H, n_blk, BLK, Dh)
    vb = jnp.pad(v, pad).reshape(B, H, n_blk, BLK, Dh)
    k_mean = jnp.mean(kb.astype(jnp.float32), axis=3)
    gate = jnp.einsum('bhsd,bhnd->bhsn', q.astype(jnp.float32), k_mean)
    n_past = jnp.arange(S) // BLK
    past = jnp.arange(n_blk)[None, :] < n_past[:, None]
    gate = jnp.where(past[None, None], gate, NEG)
    k_sel = max(1, min(MOBA_TOPK, n_blk - 1))
    _, sel = lax.top_k(gate, k_sel)
    sel = sel.astype(jnp.int32)

    n_ch = S // QC

    def to_chunks(a):
        a = a.reshape(B, H, n_ch, QC, *a.shape[3:])
        a = jnp.moveaxis(a, 2, 1)
        return a.reshape(B * n_ch, H, QC, *a.shape[4:])

    q_c, sel_c = to_chunks(q), to_chunks(sel)
    b_idx = jnp.repeat(jnp.arange(B, dtype=jnp.int32), n_ch)
    c_idx = jnp.tile(jnp.arange(n_ch, dtype=jnp.int32), B)
    head_ids = jnp.arange(H)
    scale = HEAD_DIM ** -0.5

    def step(args):
        qc, selc, b, c = args
        t = c * QC + jnp.arange(QC, dtype=jnp.int32)
        j_own = (c * QC) // BLK
        kbb = lax.dynamic_index_in_dim(kb, b, 0, keepdims=False)
        vbb = lax.dynamic_index_in_dim(vb, b, 0, keepdims=False)
        k_g = kbb[head_ids[:, None, None], selc]
        v_g = vbb[head_ids[:, None, None], selc]
        k_own = lax.dynamic_index_in_dim(kbb, j_own, 1, keepdims=False)
        v_own = lax.dynamic_index_in_dim(vbb, j_own, 1, keepdims=False)
        qf = qc.astype(jnp.float32)
        l_sel = jnp.einsum('hqd,hqnjd->hqnj', qf, k_g.astype(jnp.float32)) * scale
        pos_sel = selc[..., None] * BLK + jnp.arange(BLK, dtype=jnp.int32)
        b_sel = bias_table[rel_bucket(t[None, :, None, None] - pos_sel), head_ids[:, None, None, None]].astype(jnp.float32)
        slot_ok = jnp.arange(k_sel)[None, :] < (t // BLK)[:, None]
        l_sel = jnp.where(slot_ok[None, :, :, None], l_sel + b_sel, NEG).reshape(H, QC, k_sel * BLK)
        l_own = jnp.einsum('hqd,hkd->hqk', qf, k_own.astype(jnp.float32)) * scale
        d_own = t[:, None] - (j_own * BLK + jnp.arange(BLK, dtype=jnp.int32))[None, :]
        b_own = jnp.moveaxis(bias_table[rel_bucket(d_own)].astype(jnp.float32), -1, 0)
        l_own = jnp.where((d_own >= 0)[None], l_own + b_own, NEG)
        p = jax.nn.softmax(jnp.concatenate([l_sel, l_own], axis=-1), axis=-1)
        p_sel = p[..., :k_sel * BLK].reshape(H, QC, k_sel, BLK)
        p_own = p[..., k_sel * BLK:]
        o = (jnp.einsum('hqnj,hqnjd->hqd', p_sel, v_g.astype(jnp.float32))
             + jnp.einsum('hqk,hkd->hqd', p_own, v_own.astype(jnp.float32)))
        return o.astype(qc.dtype)

    o = lax.map(step, (q_c, sel_c, b_idx, c_idx))
    o = o.reshape(B, n_ch, H, QC, Dh).transpose(0, 1, 3, 2, 4).reshape(B, S, H * Dh)
    return o @ w_o

def dsa_attention(h, w_in, g_q, g_kv, w_uq, w_qi, w_uk, w_uv, w_o, bias_table):
    B, S, _ = h.shape
    H, Dh, QC = N_HEADS, HEAD_DIM, DSA_Q_CHUNK
    proj = h @ w_in
    c_q, c_kv, k_idx, w_idx = jnp.split(proj, [DSA_Q_LORA, DSA_Q_LORA + DSA_KV_LORA, DSA_Q_LORA + DSA_KV_LORA + IDX_DIM], axis=-1)
    c_q = rms_norm(c_q, g_q)
    c_kv = rms_norm(c_kv, g_kv)
    q_nope = (c_q @ w_uq).reshape(B, S, H, Dh)
    q_idx = (c_q @ w_qi).reshape(B, S, IDX_HEADS, IDX_DIM)
    w_idx = w_idx.astype(jnp.float32) * (IDX_HEADS ** -0.5 * IDX_DIM ** -0.5)
    top_k = min(DSA_TOPK_MAX, S // 4)
    n_ch = S // QC

    def to_chunks(a):
        return jnp.moveaxis(a.reshape(B, n_ch, QC, *a.shape[2:]), 1, 0)

    k_idx32 = k_idx.astype(jnp.float32)
    key_pos = jnp.arange(S, dtype=jnp.int32)
    b_ids = jnp.arange(B)[:, None, None]
    scale = HEAD_DIM ** -0.5

    def step(args):
        qn, qi, wi, c = args
        t = c * QC + jnp.arange(QC, dtype=jnp.int32)
        rel = jax.nn.relu(jnp.einsum('bqhd,bsd->bqhs', qi.astype(jnp.float32), k_idx32))
        score = jnp.einsum('bqh,bqhs->bqs', wi, rel)
        score = jnp.where((key_pos[None, :] <= t[:, None])[None], score, NEG)
        _, idx = lax.top_k(score, top_k)
        valid = idx <= t[None, :, None]
        c_sel = c_kv[b_ids, idx].astype(jnp.float32)
        q_lat = jnp.einsum('bqhd,hdc->bqhc', qn.astype(jnp.float32), w_uk.astype(jnp.float32))
        logits = jnp.einsum('bqhc,bqkc->bhqk', q_lat, c_sel) * scale
        bias = jnp.moveaxis(bias_table[rel_bucket(t[None, :, None] - idx)].astype(jnp.float32), -1, 1)
        logits = jnp.where(valid[:, None], logits + bias, NEG)
        p = jax.nn.softmax(logits, axis=-1)
        o_lat = jnp.einsum('bhqk,bqkc->bqhc', p, c_sel)
        o = jnp.einsum('bqhc,hcd->bqhd', o_lat, w_uv.astype(jnp.float32))
        return o.astype(qn.dtype)

    o = lax.map(step, (to_chunks(q_nope), to_chunks(q_idx), to_chunks(w_idx), jnp.arange(n_ch, dtype=jnp.int32)))
    o = jnp.moveaxis(o, 0, 1).reshape(B, S, H * Dh)
    return o @ w_o

def sq_relu_mlp(h, w_up, w_down):
    return jnp.square(jax.nn.relu(h @ w_up)) @ w_down

def first_inputs(seed: int = 0) -> dict:
    key = jax.random.key(seed)
    ks = jax.random.split(key, 20)
    D, H, Dh = D_MODEL, N_HEADS, HEAD_DIM
    nrm = lambda k, shape, s: jax.random.normal(k, shape, jnp.float32) * s
    gain = lambda k, shape: 1.0 + 0.05 * jax.random.normal(k, shape, jnp.float32)
    return {
        "x": nrm(ks[0], (BATCH, SEQ, D), 1.0),
        "rel_bias": nrm(ks[1], (NUM_BUCKETS, H), 0.2),
        "ln_attn": gain(ks[2], (DEPTH, D)),
        "ln_mlp": gain(ks[3], (DEPTH, D)),
        "moba_w_qkv": nrm(ks[4], (N_A_LAYERS, D, 3 * D), D ** -0.5),
        "moba_w_o": nrm(ks[5], (N_A_LAYERS, D, D), D ** -0.5),
        "dsa_w_in": nrm(ks[6], (N_B_LAYERS, D, DSA_IN_DIM), D ** -0.5),
        "dsa_g_q": gain(ks[7], (N_B_LAYERS, DSA_Q_LORA)),
        "dsa_g_kv": gain(ks[8], (N_B_LAYERS, DSA_KV_LORA)),
        "dsa_w_uq": nrm(ks[9], (N_B_LAYERS, DSA_Q_LORA, H * Dh), DSA_Q_LORA ** -0.5),
        "dsa_w_qi": nrm(ks[10], (N_B_LAYERS, DSA_Q_LORA, IDX_HEADS * IDX_DIM), DSA_Q_LORA ** -0.5),
        "dsa_w_uk": nrm(ks[11], (N_B_LAYERS, H, Dh, DSA_KV_LORA), DSA_KV_LORA ** -0.5),
        "dsa_w_uv": nrm(ks[12], (N_B_LAYERS, H, DSA_KV_LORA, Dh), DSA_KV_LORA ** -0.5),
        "dsa_w_o": nrm(ks[13], (N_B_LAYERS, H * Dh, D), (H * Dh) ** -0.5),
        "mlp_w_up": nrm(ks[14], (DEPTH, D, D_FF), D ** -0.5),
        "mlp_w_down": nrm(ks[15], (DEPTH, D_FF, D), 0.5 * D_FF ** -0.5),
        "final_norm": gain(ks[16], (D,)),
    }

def first_block(x, rel_bias, ln_attn, ln_mlp, moba_w_qkv, moba_w_o, dsa_w_in, dsa_g_q, dsa_g_kv,
              dsa_w_uq, dsa_w_qi, dsa_w_uk, dsa_w_uv, dsa_w_o, mlp_w_up, mlp_w_down, final_norm):
    for i in range(DEPTH):
        hn = rms_norm(x, ln_attn[i])
        j = i // N_MIXERS
        if i % N_MIXERS == 0:
            x = x + moba_attention(hn, moba_w_qkv[j], moba_w_o[j], rel_bias)
        else:
            x = x + dsa_attention(hn, dsa_w_in[j], dsa_g_q[j], dsa_g_kv[j], dsa_w_uq[j], dsa_w_qi[j],
                                  dsa_w_uk[j], dsa_w_uv[j], dsa_w_o[j], rel_bias)
        x = x + sq_relu_mlp(rms_norm(x, ln_mlp[i]), mlp_w_up[i], mlp_w_down[i])
    return rms_norm(x, final_norm)


N_CONV_LAYERS = DEPTH // 2
N_ATTN_LAYERS = DEPTH - N_CONV_LAYERS
CONV_WIDTH = 3
HEAD_DIM_2 = 64
N_HEADS_2 = D_MODEL // HEAD_DIM_2
BRANCHES = ((128, 1), (512, 4), (2048, 16))
N_BRANCHES = len(BRANCHES)
Q_WIDTH = N_BRANCHES * N_HEADS_2 * HEAD_DIM_2
D_FF_2 = -(-8 * D_MODEL // (3 * 256)) * 256
ROPE_THETA = 10000.0
RMS_EPS = 1e-6
NEG_INF = -1e30


def rms_norm_2(x, g):
    xf = x.astype(jnp.float32)
    y = xf * lax.rsqrt(jnp.mean(xf * xf, axis=-1, keepdims=True) + RMS_EPS)
    return (y * g.astype(jnp.float32)).astype(x.dtype)

def rope(t, positions):
    half = HEAD_DIM_2 // 2
    inv_freq = ROPE_THETA ** (-jnp.arange(half, dtype=jnp.float32) / half)
    ang = positions.astype(jnp.float32)[..., None] * inv_freq
    cos = jnp.cos(ang)[:, :, None, :]
    sin = jnp.sin(ang)[:, :, None, :]
    t1 = t[..., :half].astype(jnp.float32)
    t2 = t[..., half:].astype(jnp.float32)
    out = jnp.concatenate([t1 * cos - t2 * sin, t2 * cos + t1 * sin], axis=-1)
    return out.astype(t.dtype)

def short_conv_mixer(x, w_in, conv_w, w_out):
    b_gate, c_gate, h = jnp.split(x @ w_in, 3, axis=-1)
    u = c_gate * h
    rhs = conv_w[:, None, :].astype(u.dtype)
    conv = lax.conv_general_dilated(
        u, rhs, window_strides=(1,), padding=[(CONV_WIDTH - 1, 0)],
        dimension_numbers=("NWC", "WIO", "NWC"), feature_group_count=u.shape[-1])
    return (b_gate * conv) @ w_out

def swiglu(x, w_gate_up, w_down):
    g, u = jnp.split(x @ w_gate_up, 2, axis=-1)
    return (jax.nn.silu(g) * u) @ w_down

def dilated_branch(q, k, v, window, dilation):
    band = window // dilation
    B, S, H, Dh = q.shape
    chunk = dilation * band
    Sp = -(-S // chunk) * chunk
    nb = Sp // chunk
    pad = ((0, 0), (0, Sp - S), (0, 0), (0, 0))

    def to_blocks(t):
        t = jnp.pad(t, pad).reshape(B, nb, band, dilation, H, Dh)
        return t.transpose(0, 3, 4, 1, 2, 5)

    def with_prev(t):
        prev = jnp.pad(t, ((0, 0), (0, 0), (0, 0), (1, 0), (0, 0), (0, 0)))[:, :, :, :-1]
        return jnp.concatenate([prev, t], axis=4)

    qb = to_blocks(q * (HEAD_DIM_2 ** -0.5))
    kk = with_prev(to_blocks(k))
    vv = with_prev(to_blocks(v))
    s = jnp.einsum("brhnqd,brhnkd->brhnqk", qb, kk).astype(jnp.float32)
    qi = jnp.arange(band)[:, None]
    kj = jnp.arange(2 * band)[None, :]
    dist = qi + band - kj
    in_band = (dist >= 0) & (dist <= band)
    has_prev = (kj >= band)[None] | (jnp.arange(nb)[:, None, None] > 0)
    mask = in_band[None] & has_prev
    s = jnp.where(mask, s, NEG_INF)
    m = jnp.max(s, axis=-1)
    p = jnp.exp(s - m[..., None])
    l = jnp.sum(p, axis=-1)
    o = jnp.einsum("brhnqk,brhnkd->brhnqd", p, vv.astype(jnp.float32)) / l[..., None]
    lse = m + jnp.log(l)
    o = o.transpose(0, 3, 4, 1, 2, 5).reshape(B, Sp, H, Dh)[:, :S]
    lse = lse.transpose(0, 3, 4, 1, 2).reshape(B, Sp, H)[:, :S]
    return o, lse

def dilated_attention_mixer(x, positions, k_sh, v_sh, w_q, w_o):
    B, S, _ = x.shape
    q = (x @ w_q).reshape(B, S, N_BRANCHES * N_HEADS_2, HEAD_DIM_2)
    q = rope(q, positions).reshape(B, S, N_BRANCHES, N_HEADS_2, HEAD_DIM_2)
    outs, lses = [], []
    for g, (window, dilation) in enumerate(BRANCHES):
        o, lse = dilated_branch(q[:, :, g], k_sh[:, :, g], v_sh[:, :, g], window, dilation)
        outs.append(o)
        lses.append(lse)
    wts = jax.nn.softmax(jnp.stack(lses, axis=0), axis=0)
    o = jnp.einsum("gbsh,gbshd->bshd", wts, jnp.stack(outs, axis=0))
    return o.astype(x.dtype).reshape(B, S, N_HEADS_2 * HEAD_DIM_2) @ w_o

def shared_kv(h, positions, kv_norm, w_kv):
    B, S, _ = h.shape
    kv = (rms_norm_2(h, kv_norm) @ w_kv).reshape(B, S, 2, N_BRANCHES * N_HEADS_2, HEAD_DIM_2)
    k = rope(kv[:, :, 0], positions).reshape(B, S, N_BRANCHES, N_HEADS_2, HEAD_DIM_2)
    v = kv[:, :, 1].reshape(B, S, N_BRANCHES, N_HEADS_2, HEAD_DIM_2)
    return k, v

def second_inputs(seed: int = 0) -> dict:
    key = jax.random.key(seed)
    ks = jax.random.split(key, 20)
    f32 = jnp.float32

    def w(k, shape, fan_in):
        return jax.random.normal(k, shape, f32) * (fan_in ** -0.5)

    def gain(k, shape):
        return 1.0 + 0.05 * jax.random.normal(k, shape, f32)

    x = jax.random.normal(ks[0], (BATCH, SEQ, D_MODEL), f32)
    offset = jax.random.randint(ks[1], (BATCH, 1), 0, 4096, dtype=jnp.int32)
    positions = offset + jnp.arange(SEQ, dtype=jnp.int32)[None, :]
    nA, nB = N_CONV_LAYERS, N_ATTN_LAYERS
    return {
        "x": x,
        "positions": positions,
        "mix_norm_pre": gain(ks[2], (DEPTH, D_MODEL)),
        "mix_norm_post": gain(ks[3], (DEPTH, D_MODEL)),
        "ffn_norm_pre": gain(ks[4], (DEPTH, D_MODEL)),
        "ffn_norm_post": gain(ks[5], (DEPTH, D_MODEL)),
        "ffn_w_gate_up": w(ks[6], (DEPTH, D_MODEL, 2 * D_FF_2), D_MODEL),
        "ffn_w_down": w(ks[7], (DEPTH, D_FF_2, D_MODEL), D_FF_2),
        "conv_w_in": w(ks[8], (nA, D_MODEL, 3 * D_MODEL), D_MODEL),
        "conv_w": w(ks[9], (nA, CONV_WIDTH, D_MODEL), CONV_WIDTH),
        "conv_w_out": w(ks[10], (nA, D_MODEL, D_MODEL), D_MODEL),
        "kv_norm": gain(ks[11], (D_MODEL,)),
        "w_kv": w(ks[12], (D_MODEL, 2 * Q_WIDTH), D_MODEL),
        "w_q": w(ks[13], (nB, D_MODEL, Q_WIDTH), D_MODEL),
        "w_o": w(ks[14], (nB, N_HEADS_2 * HEAD_DIM_2, D_MODEL), N_HEADS_2 * HEAD_DIM_2),
    }

def second_block(x, positions, mix_norm_pre, mix_norm_post, ffn_norm_pre, ffn_norm_post,
              ffn_w_gate_up, ffn_w_down, conv_w_in, conv_w, conv_w_out,
              kv_norm, w_kv, w_q, w_o):
    h = x
    for layer in range(DEPTH):
        if layer == N_CONV_LAYERS:
            k_sh, v_sh = shared_kv(h, positions, kv_norm, w_kv)
        hn = rms_norm_2(h, mix_norm_pre[layer])
        if layer < N_CONV_LAYERS:
            y = short_conv_mixer(hn, conv_w_in[layer], conv_w[layer], conv_w_out[layer])
        else:
            j = layer - N_CONV_LAYERS
            y = dilated_attention_mixer(hn, positions, k_sh, v_sh, w_q[j], w_o[j])
        h = h + rms_norm_2(y, mix_norm_post[layer])
        f = swiglu(rms_norm_2(h, ffn_norm_pre[layer]), ffn_w_gate_up[layer], ffn_w_down[layer])
        h = h + rms_norm_2(f, ffn_norm_post[layer])
    return h


def setup_inputs(seed=0):
    out = dict(first_inputs(seed))
    for name, value in second_inputs(seed + 1).items():
        if name != "x":
            out[name + "_2"] = value
    return out


def reference(
    x, rel_bias, ln_attn, ln_mlp, moba_w_qkv, moba_w_o, dsa_w_in, dsa_g_q, dsa_g_kv, dsa_w_uq,
    dsa_w_qi, dsa_w_uk, dsa_w_uv, dsa_w_o, mlp_w_up, mlp_w_down, final_norm, positions_2,
    mix_norm_pre_2, mix_norm_post_2, ffn_norm_pre_2, ffn_norm_post_2, ffn_w_gate_up_2,
    ffn_w_down_2, conv_w_in_2, conv_w_2, conv_w_out_2, kv_norm_2, w_kv_2, w_q_2, w_o_2,
):
    x = first_block(
        x, rel_bias, ln_attn, ln_mlp, moba_w_qkv, moba_w_o, dsa_w_in, dsa_g_q, dsa_g_kv,
        dsa_w_uq, dsa_w_qi, dsa_w_uk, dsa_w_uv, dsa_w_o, mlp_w_up, mlp_w_down, final_norm,
    )
    return second_block(
        x, positions_2, mix_norm_pre_2, mix_norm_post_2, ffn_norm_pre_2, ffn_norm_post_2,
        ffn_w_gate_up_2, ffn_w_down_2, conv_w_in_2, conv_w_2, conv_w_out_2, kv_norm_2, w_kv_2,
        w_q_2, w_o_2,
    )


_drawn_inputs = setup_inputs


def setup_inputs(seed=0):
    import zlib

    import numpy as np

    out = dict(_drawn_inputs(seed))
    spreads = {}
    factors = {}
    for name, (base, spread) in spreads.items():
        noise = np.random.default_rng([zlib.crc32(name.encode()), seed]).standard_normal(out[name].shape)
        drawn = base * np.exp(spread * noise) if base else spread * noise
        out[name] = __import__('jax').numpy.asarray(drawn.astype(out[name].dtype))
    for name, factor in factors.items():
        out[name] = (out[name] * factor).astype(out[name].dtype)
    return out
```

```python
from contextlib import ExitStack

import numpy as np

import concourse.bass as bass
from concourse import mybir

F32 = mybir.dt.float32
F32R = mybir.dt.float32r
I32 = mybir.dt.int32
ALU = mybir.AluOpType
ACT = mybir.ActivationFunctionType
AX = mybir.AxisListType

P = 128
SEQ = 256
QT = SEQ // P
D = 1024
KT = D // P
HEADS = 16
DH = 64
FF = 4096
FF2 = 2816
HID_TILES = FF // P
HID2_TILES = FF2 // P
BUCKETS = 32
MAX_DISTANCE = 128
IDX_HEADS = 8
LORA = 256
TOPK = 64
BRANCHES = ((128, 1), (512, 4), (2048, 16))
NB = len(BRANCHES)
QW = NB * HEADS * DH
EPS = 1e-6
NEG = -1e30
TAKEN = -3e38
SCALE = DH ** -0.5
IDX_SCALE = IDX_HEADS ** -0.5 * DH ** -0.5
CAUSAL = P + SEQ

CW = 2048
RAW_SLOTS = 4
SPLIT_SLOTS = 2
LIN_BANKS = 2

QUARTERS = {HID_TILES: ((0, 8), (8, 8), (16, 8), (24, 8)), HID2_TILES: ((0, 6), (6, 6), (12, 5), (17, 5))}


class Stage:

    def __init__(self, name, kind, chunks, banks, contraction=KT):
        self.name, self.kind, self.chunks, self.banks, self.contraction = name, kind, chunks, banks, contraction
        self.quartered = contraction != KT
        self.unroll = 8 if self.quartered else 4


STAGES = [
    Stage("moba_qk", "scale", 8, 8),
    Stage("moba_v", "token", 4, 4),
    Stage("moba_o", "residual", 4, 4),
    Stage("up_0", "relu", 16, 16),
    Stage("down_0", "residual", 16, 4, HID_TILES),
    Stage("dsa_in", "dsa_in", 3, 4),
    Stage("dsa_low", "dsa_low", 4, 14),
    Stage("dsa_o", "residual", 4, 4),
    Stage("up_1", "relu", 16, 16),
    Stage("down_1", "residual", 16, 4, HID_TILES),
    Stage("conv_ch", "conv", 8, 8),
    Stage("conv_b", "gate", 4, 4),
    Stage("conv_out", "post", 4, 4),
    Stage("gate_up_0", "swiglu", 22, 22),
    Stage("ffn_down_0", "post", 16, 4, HID2_TILES),
    Stage("dil_k", "rope", 12, 12),
    Stage("dil_v", "token", 12, 12),
    Stage("dil_q", "rope", 12, 12),
    Stage("dil_o", "post", 4, 4),
    Stage("gate_up_1", "swiglu", 22, 22),
    Stage("ffn_down_1", "post", 16, 4, HID2_TILES),
]
CHUNKS = 0
_banks = 0
for _n, _s in enumerate(STAGES):
    _s.n, _s.base, _s.bank_base = _n, CHUNKS, _banks
    CHUNKS += _s.chunks
    _banks += _s.banks
BY_NAME = {s.name: s for s in STAGES}


OPERANDS = [("moba_qk", KT), ("moba_o", KT), ("up_0", KT), ("down_0", FF // 256), ("dsa_in", KT), ("dsa_low", 4),
            ("dsa_o", KT), ("up_1", KT), ("down_1", FF // 256), ("conv_ch", KT), ("conv_out", KT), ("gate_up_0", KT),
            ("ffn_down_0", HID2_TILES), ("dil_k", KT), ("dil_q", KT), ("dil_o", KT), ("gate_up_1", KT),
            ("ffn_down_1", HID2_TILES)]
OP_BEFORE = {name: sum(n for _, n in OPERANDS[:m]) for m, (name, _) in enumerate(OPERANDS)}
ATTENTION_FOR = ["moba_o", "dsa_o", "dil_o"]


def banks_before(stage, *kinds):
    return sum(s.banks for s in STAGES[:stage.n] if s.kind in kinds)


def in_loop(eng, stage, step):
    full = stage.chunks // stage.unroll
    looped = full - 1 if stage is STAGES[-1] else full
    if looped > 1:
        with eng.Fori(0, looped) as i:
            for u in range(stage.unroll):
                step(i, u)
    else:
        for u in range(looped * stage.unroll):
            step(0, u)
    for c in range(looped * stage.unroll, stage.chunks):
        step(c // stage.unroll, c % stage.unroll)


class Own:

    def __init__(self, eng, sem):
        self.eng, self.sem, self.n = eng, sem, 0

    def link(self, ins):
        self.n += 1
        ins.then_inc(self.sem, 1)
        self.eng.wait_ge(self.sem, self.n)


GAINS = ["ln_attn_0", "ln_mlp_0", "ln_attn_1", "ln_mlp_1", "final", "mix_pre_0", "mix_post_0", "ffn_pre_0",
         "ffn_post_0", "kv", "mix_pre_1", "mix_post_1", "ffn_pre_1", "ffn_post_1"]
GAIN_AT = {g: KT * n for n, g in enumerate(GAINS)}
LATENT_GAIN_AT = KT * len(GAINS)
CONV_AT = LATENT_GAIN_AT + 2 * (LORA // P)
GAIN_COLS = CONV_AT + KT * 3

C_MASK = 0
C_CAUSAL = C_MASK + NB * CAUSAL
C_IDENT = C_CAUSAL + CAUSAL
C_FREQ = C_IDENT + P
C_SIGN = C_FREQ + 1
CONST_COLS = C_SIGN + 1


def build(nc, stream, x_in, gains_in, table_in, pos_in, const_in, onehot_in, negmask_in, toeplitz, out):
    with ExitStack() as ctx:
        ctx.enter_context(nc.allow_non_contiguous_dma("small constants"))
        place = [-(-nc.sbuf_base // 64) * 64]

        def at(name, shape, dt, offset):
            return nc.alloc_sbuf_tensor_at(name, shape, dt, offset=offset)

        def sb(name, shape, dt=F32):
            offset = place[0]
            place[0] += -(-int(np.prod(shape[1:])) * 4 // 32) * 32
            return at(name, shape, dt, offset)

        def sem(name):
            return nc.alloc_semaphore(name)

        raw = sb("raw", [P, RAW_SLOTS, CW])
        whi = sb("whi", [P, SPLIT_SLOTS, CW], F32R)
        wlo = sb("wlo", [P, SPLIT_SLOTS, CW], F32R)
        x = sb("x", [P, KT, SEQ])
        ahi = sb("ahi", [P, KT, SEQ], F32R)
        alo = sb("alo", [P, KT, SEQ], F32R)
        region = place[0]
        place[0] += NB * KT * SEQ * 4 * 3
        bhi = at("bhi", [P, HID_TILES, SEQ], F32R, region)
        blo = at("blo", [P, HID_TILES, SEQ], F32R, region + HID_TILES * SEQ * 4)
        one = KT * SEQ * 4
        qk1 = at("qk1", [P, 2 * KT, SEQ], F32, region)
        q1, k1 = qk1[:, 0:KT, :], qk1[:, KT:2 * KT, :]
        v1 = at("v1", [P, QT, D], F32, region + 2 * one)
        bias = at("bias", [P, HEADS, CAUSAL], F32, region + 3 * one)
        free1 = region + 3 * one + HEADS * CAUSAL * 4
        topmask = at("topmask", [P, CAUSAL], F32, free1)
        q_idx = at("q_idx", [P, 4, SEQ], F32, free1 + 2048)
        k_idx = at("k_idx", [P, SEQ], F32, free1 + 2048 + 4096)
        score = at("score", [P, CAUSAL], F32, free1 + 2048 + 4096 + 1024)
        relu_s = at("relu_s", [P, 2, CAUSAL], F32, free1 + 2048 + 4096 + 1024 + 2048)
        z_q = at("z_q", [P, 2, SEQ], F32, free1 + 13312)
        z_kv = at("z_kv", [P, 2, SEQ], F32, free1 + 13312 + 2048)
        masked_bias = at("masked_bias", [P, 4, CAUSAL], F32, free1 + 17408)
        q3 = at("q3", [P, NB * KT, SEQ], F32, region)
        k3 = at("k3", [P, NB * KT, SEQ], F32, region + NB * one)
        v3 = at("v3", [P, QT, QW], F32, region + 2 * NB * one)
        gated = at("gated", [P, KT, SEQ + 2], F32, region)
        conv = at("conv", [P, KT, SEQ], F32, region + KT * (SEQ + 2) * 4 + 64)
        shared = place[0]
        place[0] += 3 * 2 * NB * SEQ * 4 + 2 * SEQ * 4
        y = at("y", [P, KT, SEQ], F32, shared)
        sq = at("sq", [P, KT, SEQ], F32, shared + one)
        q_pair = at("q_pair", [P, 2, NB, SEQ], F32, shared)
        k_pair = at("k_pair", [P, 2, NB, SEQ], F32, shared + 2 * NB * SEQ * 4)
        v_pair = at("v_pair", [P, 2, NB * QT, P], F32, shared + 4 * NB * SEQ * 4)
        o_pair = at("o_pair", [P, 2, QT * P], F32, shared + 6 * NB * SEQ * 4)
        logits3 = sb("logits3", [P, 2, NB * CAUSAL])
        logits = at("logits", [P, 4, CAUSAL], F32, place[0] - 2 * NB * CAUSAL * 4)
        pt = sb("pt", [P, NB, CAUSAL])
        z = at("z", [P, 2, SEQ], F32, place[0] - NB * CAUSAL * 4)
        zz = at("zz", [P, 2, SEQ], F32, place[0] - NB * CAUSAL * 4 + 2048)
        ssum = at("ssum", [P, 2, SEQ], F32, place[0] - 3 * NB * CAUSAL * 4)
        std = at("std", [P, 2, SEQ], F32, place[0] - 3 * NB * CAUSAL * 4 + 2048)
        masks3 = sb("masks3", [P, NB, CAUSAL])
        causal = sb("causal", [P, CAUSAL])
        consts = sb("consts", [P, CONST_COLS - C_IDENT])
        gains = sb("gains", [P, GAIN_COLS])
        rstd = sb("rstd", [P, 2, SEQ])
        rcol = sb("rcol", [P, QT])
        cos_r = sb("cos_r", [P, SEQ])
        sin_r = sb("sin_r", [P, SEQ])
        cos_t = sb("cos_t", [P, SEQ])
        sin_t = sb("sin_t", [P, SEQ])
        ones = sb("ones", [P, P])
        eps = sb("eps", [P, 1])
        w_idx = sb("w_idx", [P, QT, IDX_HEADS])
        neg_max = sb("neg_max", [P, 4, QT])
        row_sum = sb("row_sum", [P, 4, QT])
        inv_sum = sb("inv_sum", [P, 4, QT])
        best = sb("best", [P, QT, 8])
        assert place[0] <= nc.sbuf_usable_end, place[0] - nc.sbuf_usable_end
        onehot = at("onehot", [BUCKETS, CAUSAL], F32, shared)
        table = at("table", [BUCKETS, HEADS], F32, shared + 2048)
        negmask = at("negmask", [HEADS, CAUSAL], F32, shared + 4096)
        by_dist = at("by_dist", [HEADS, CAUSAL], F32, shared + 6144)
        pos_i = at("pos_i", [P, SEQ], I32, shared + 8192)
        angle = at("angle", [P, SEQ], F32, shared + 9216)
        turns = at("turns", [P, SEQ], F32, shared + 10240)
        shifted = at("shifted", [P, SEQ], F32, shared + 11264)
        ident = consts[:, 0:P]

        bank = nc.alloc_psum_tensor("bank", [P, 8, 512], F32)
        S_BANKS, PT_BANKS, O_BANKS = (0, 1, 2, 3), (4, 5), (6, 7)
        STAT = 7

        raw_landed = [sem(f"raw_landed{n}") for n in range(RAW_SLOTS)]
        hi_split = sem("hi_split")
        lo_split = sem("lo_split")
        chunk_used = sem("chunk_used")
        low_bank = sem("low_bank")
        bank_read = sem("bank_read")
        x_landed = sem("x_landed")
        const_landed = sem("const_landed")
        table_landed = sem("table_landed")
        dist_stored = sem("dist_stored")
        bias_landed = sem("bias_landed")
        ones_set = sem("ones_set")
        dist_ready = sem("dist_ready")
        dist_done = sem("dist_done")
        act_hi = sem("act_hi")
        op_ready = sem("op_ready")
        squares = sem("squares")
        sums = sem("sums")
        totals = sem("totals")
        roots = sem("roots")
        rstd_ready = sem("rstd_ready")
        col_ready = sem("col_ready")
        rcol_ready = sem("rcol_ready")
        dve_step = sem("dve_step")
        act_step = sem("act_step")
        h_ready = sem("h_ready")
        e_ready = sem("e_ready")
        y_ready = sem("y_ready")
        yhi_ready = sem("yhi_ready")
        gate_ready = sem("gate_ready")
        tap_ready = sem("tap_ready")
        conv_ready = sem("conv_ready")
        rot_ready = sem("rot_ready")
        rope_cos = sem("rope_cos")
        rope_sin = sem("rope_sin")
        angles = sem("angles")
        sines = sem("sines")
        x_done = sem("x_done")
        qk_staged = sem("qk_staged")
        v_staged = sem("v_staged")
        topped = sem("topped")
        topmask_ready = sem("topmask_ready")
        s_ready = sem("s_ready")
        l_ready = sem("l_ready")
        m_ready = sem("m_ready")
        p_ready = sem("p_ready")
        i_ready = sem("i_ready")
        t_ready = sem("t_ready")
        tc_ready = sem("tc_ready")
        o_ready = sem("o_ready")
        on_ready = sem("on_ready")
        ot_ready = sem("ot_ready")
        ohi_ready = sem("ohi_ready")
        idx_ready = sem("idx_ready")
        idx_relu = sem("idx_relu")
        idx_used = sem("idx_used")
        stored = sem("stored")

        def chunk_slot(stage, u):
            return (stage.base + u) % SPLIT_SLOTS

        def lin_bank(stage, local):
            return (stage.bank_base + local) % LIN_BANKS

        def local_bank(stage, i, u):
            return (i * 2 + u // 4) if stage.quartered else i * stage.unroll + u

        def static_bank(stage, u):
            return lin_bank(stage, u // 4 if stage.quartered else u)


        AHEAD = {False: 3, True: 2}

        def in_steps(eng, step, steps, first=8):
            for u in range(first):
                step(0, u)
            with eng.Fori(0, 2) as i:
                for u in range(first, first + 4):
                    step(i, u)
            for u in range(first + 8, steps):
                step(0, u)

        block = ctx.enter_context(nc.Block())

        @block.sync
        def _(sp):
            sp.dma_start(x[:, :, :], x_in).then_inc(x_landed, 16)
            for stage in STAGES:
                width = 6 * 2 * P if stage.contraction == HID2_TILES else CW

                def load(i, u, stage=stage, width=width):
                    g = stage.base + u
                    s = g % RAW_SLOTS
                    c = i * stage.unroll + stage.base + u
                    if g >= RAW_SLOTS:
                        sp.wait_ge(lo_split, i * stage.unroll + (g - RAW_SLOTS + 1))
                    sp.dma_start(raw[:, s, 0:width], stream[c, :, 0:width]).then_inc(raw_landed[s], 16)

                if stage.base == 0:
                    for u in range(4):
                        load(0, u)
                    for u in range(4, stage.chunks):
                        load(0, u)
                else:
                    in_loop(sp, stage, load)
            sp.wait_ge(x_done, 5)
            sp.dma_start(out, x[:, :, :]).then_inc(stored, 16)
            sp.wait_ge(stored, 16)

        @block.tensor
        def _(pe):
            n_stat = [0]

            def fmm(out_ap, stat, mov, first, last):
                return nc.tensor.matmul(out_ap, stat, mov, start=first, stop=last, skip_group_check=True)

            def features(b, slot, col, a_hi, a_lo, k0, nk, first, last, waits=None):
                for k in range(nk):
                    if waits is not None:
                        pe.wait_ge(op_ready, waits + k + 1)
                    for n in range(2):
                        c = col(k, n)
                        o = bank[:, b, n * SEQ:(n + 1) * SEQ]
                        w_h, w_l = whi[:, slot, c:c + P], wlo[:, slot, c:c + P]
                        fmm(o, w_h, a_hi[:, k0 + k, :], first and k == 0 and n == 0, False)
                        fmm(o, w_h, a_lo[:, k0 + k, :], False, False)
                        ins = fmm(o, w_l, a_hi[:, k0 + k, :], False, last and k == nk - 1)
                return ins

            def tokens(b, slot, col, width, k0, nk, out_width=SEQ):
                for k in range(nk):
                    c = col(k)
                    for t in range(QT):
                        o = bank[:, b, t * out_width:t * out_width + width]
                        rows = slice(t * P, (t + 1) * P)
                        w_h, w_l = whi[:, slot, c:c + width], wlo[:, slot, c:c + width]
                        fmm(o, ahi[:, k0 + k, rows], w_h, k == 0 and t == 0, False)
                        fmm(o, alo[:, k0 + k, rows], w_h, False, False)
                        ins = fmm(o, ahi[:, k0 + k, rows], w_l, False, k == nk - 1)
                return ins

            def weights_ready(stage, i, u):
                pe.wait_ge(lo_split, i * stage.unroll + (stage.base + u + 1))

            def bank_free(stage, i, local):
                j = stage.bank_base + local
                if j >= LIN_BANKS:
                    per = 2 if stage.quartered else stage.unroll
                    pe.wait_ge(bank_read, i * per + (j - LIN_BANKS + 1))

            def product(stage, operand_base):
                def step(i, u):
                    weights_ready(stage, i, u)
                    local = u // 4 if stage.quartered else u
                    if not stage.quartered or u % 4 == 0:
                        bank_free(stage, i, local)
                    b, slot = static_bank(stage, u), chunk_slot(stage, u)
                    if stage.quartered:
                        k0, nk = QUARTERS[stage.contraction][u % 4]
                        need = (k0 + nk) // 2 if stage.contraction == HID_TILES else k0 + nk
                        pe.wait_ge(op_ready, operand_base + need)
                        ins = features(b, slot, lambda k, n: (2 * k + n) * P, bhi, blo, k0, nk, u % 4 == 0,
                                       u % 4 == 3)
                    elif stage.kind == "token":
                        ins = tokens(b, slot, lambda k: 2 * k * P, 2 * P, 0, KT)
                    else:
                        ins = features(b, slot, lambda k, n: (2 * k + n) * P, ahi, alo, 0, KT, True, True,
                                       waits=operand_base if u == 0 else None)
                    ins.then_inc(chunk_used, 1)
                in_loop(pe, stage, step)

            def statistics(width=SEQ):
                n_stat[0] += 1
                pe.wait_ge(sums, n_stat[0])
                nc.tensor.matmul(bank[:, STAT, 0:width], ones[:, :], ssum[:, :, :].rearrange("p a t -> p (a t)")[:, 0:width],
                                 start=True, stop=True).then_inc(totals, 1)

            def columns(source):
                pe.wait_ge(rstd_ready, n_stat[0])
                for t in range(QT):
                    ins = nc.tensor.matmul(bank[:, STAT, t:t + 1], rstd[0:1, source, t * P:(t + 1) * P], ones[0:1, 0:1],
                                           start=(t == 0), stop=(t == 1), skip_group_check=True)
                ins.then_inc(col_ready, 1)

            def attention(run, branches):
                base, wide = HEADS * run, branches > 1
                ahead = AHEAD[wide]
                pairs = base // 2
                s_banks, pt_banks = ((0, 1, 2), (3, 4, 5)) if wide else (S_BANKS, PT_BANKS)

                def step(i, u):
                    h = u - ahead
                    if 0 <= h < HEADS:
                        pe.wait_ge(p_ready, i * 4 + (base + h + 1))
                        held = base + h if wide else base + h - 1
                        if held > 0:
                            pe.wait_ge(tc_ready, i * 4 + held)
                        for g in range(branches):
                            b = pt_banks[g] if wide else pt_banks[h % 2]
                            src = logits3[:, h % 2, g * CAUSAL:(g + 1) * CAUSAL] if wide else logits[:, h % 4, :]
                            for c in range(3):
                                cols = slice(c * P, (c + 1) * P)
                                ins = nc.tensor.transpose(bank[:, b, cols], src[:, cols], ident)
                        ins.then_inc(t_ready, 1)
                    if u < HEADS:
                        slot, odd = (u // 2) % 2, u % 2
                        rows = slice(odd * DH, odd * DH + DH)
                        if not odd:
                            pe.wait_ge(qk_staged, i * 4 + (2 * pairs + (u // 2 + 1) * 2))
                        need = base + u if wide else base + u + 1 - len(s_banks)
                        if need > 0:
                            pe.wait_ge(l_ready, i * 4 + need)
                        for g in range(branches):
                            b = s_banks[g] if wide else s_banks[u % 4]
                            nc.tensor.matmul(bank[:, b, 0:P], q_pair[rows, slot, g, 0:P], k_pair[rows, slot, g, 0:P],
                                             start=True, stop=True, skip_group_check=True)
                            ins = nc.tensor.matmul(bank[:, b, P:CAUSAL], q_pair[rows, slot, g, P:SEQ],
                                                   k_pair[rows, slot, g, :], start=True, stop=True, skip_group_check=True)
                        ins.then_inc(s_ready, 1)
                    if 0 <= h < HEADS:
                        b = O_BANKS[(h // 2) % 2]
                        odd = h % 2
                        pe.wait_ge(tc_ready, i * 4 + (base + h + 1))
                        if not odd:
                            pe.wait_ge(v_staged, i * 2 + (pairs + h // 2 + 1))
                        if not odd and h >= 4:
                            pe.wait_ge(op_ready, i * 2 + (OP_BEFORE[ATTENTION_FOR[run]] + h // 2 - 1))
                        for q in range(QT):
                            o = bank[:, b, q * P + odd * DH:q * P + odd * DH + DH]
                            terms = [(g, c) for g in range(branches) for c in range(q + 1)]
                            for n, (g, c) in enumerate(terms):
                                at_col = (q + c) * P
                                src = (pt[:, g, at_col:at_col + P] if wide else pt[:, h % 2, at_col:at_col + P])
                                v = v_pair[:, (h // 2) % 2, g * QT + c, odd * DH:odd * DH + DH]
                                ins = nc.tensor.matmul(o, src, v, start=(n == 0),
                                                       stop=(n == len(terms) - 1), skip_group_check=True)
                        ins.then_inc(o_ready, 1)
                    if h >= 2 and h % 2 == 0:
                        t = h // 2 - 1
                        pe.wait_ge(on_ready, i * 2 + (pairs + t + 1))
                        for q in range(QT):
                            ins = nc.tensor.transpose(bank[:, O_BANKS[t % 2], SEQ + q * P:SEQ + (q + 1) * P],
                                                      o_pair[:, t % 2, q * P:(q + 1) * P], ident)
                        ins.then_inc(ot_ready, 1)

                in_steps(pe, step, HEADS + ahead + 2)

            pe.wait_ge(table_landed, 48)
            pe.wait_ge(ones_set, 2)
            nc.tensor.matmul(bank[0:HEADS, 0, 0:CAUSAL], table[:, :], onehot[:, :], start=True, stop=True)\
              .then_inc(dist_ready, 1)
            pe.wait_ge(dist_done, 1)

            def low_rank():
                stage = BY_NAME["dsa_low"]
                j = 0
                for c in range(4):
                    weights_ready(stage, 0, c)
                    for pair in range(2 if c == 0 else 4):
                        if pair == 0 and c == 0:
                            pe.wait_ge(op_ready, OP_BEFORE["dsa_low"] + 4)
                        bank_free(stage, 0, j)
                        b, slot = lin_bank(stage, j), chunk_slot(stage, c)
                        if c == 3:
                            ins = tokens(b, slot, lambda k: k * 1024 + pair * 256, 256, 2, 2)
                        else:
                            ins = features(b, slot, lambda k, n: k * 1024 + pair * 256 + n * P, ahi, alo,
                                           2 if c == 2 else 0, 2, True, True)
                        last = pair == (1 if c == 0 else 3)
                        ins.then_inc(chunk_used if last else low_bank, 1)
                        j += 1
                    if c == 0:
                        columns_kv()
                        index_scores()

            def columns_kv():
                for t in range(QT):
                    ins = nc.tensor.matmul(bank[:, STAT, t:t + 1], rstd[0:1, 1, t * P:(t + 1) * P], ones[0:1, 0:1],
                                           start=(t == 0), stop=(t == 1), skip_group_check=True)
                ins.then_inc(col_ready, 1)

            def index_scores():
                stage = BY_NAME["dsa_low"]
                pe.wait_ge(bank_read, stage.bank_base + 2)
                for h in range(IDX_HEADS):
                    rows = slice((h % 2) * DH, (h % 2) * DH + DH)
                    b = 2 + h % 4
                    if h >= 4:
                        pe.wait_ge(idx_relu, h - 3)
                    nc.tensor.matmul(bank[:, b, 0:P], q_idx[rows, h // 2, 0:P], k_idx[rows, 0:P],
                                     start=True, stop=True, skip_group_check=True)
                    nc.tensor.matmul(bank[:, b, P:CAUSAL], q_idx[rows, h // 2, P:SEQ], k_idx[rows, :],
                                     start=True, stop=True, skip_group_check=True).then_inc(idx_ready, 1)

            def dsa_in():
                stage = BY_NAME["dsa_in"]
                for c in range(2):
                    weights_ready(stage, 0, c)
                    bank_free(stage, 0, c)
                    features(lin_bank(stage, c), chunk_slot(stage, c), lambda k, n: (2 * k + n) * P, ahi, alo, 0, KT,
                             True, True, waits=OP_BEFORE["dsa_in"] if c == 0 else None).then_inc(chunk_used, 1)
                weights_ready(stage, 0, 2)
                bank_free(stage, 0, 2)
                slot, b = chunk_slot(stage, 2), lin_bank(stage, 2)
                for k in range(KT):
                    c = 2 * k * P
                    fmm(bank[:, b, 0:SEQ], whi[:, slot, c:c + P], ahi[:, k, :], k == 0, False)
                    fmm(bank[:, b, 0:SEQ], whi[:, slot, c:c + P], alo[:, k, :], False, False)
                    ins = fmm(bank[:, b, 0:SEQ], wlo[:, slot, c:c + P], ahi[:, k, :], False, k == KT - 1)
                ins.then_inc(low_bank, 1)
                bank_free(stage, 0, 3)
                tokens(lin_bank(stage, 3), slot, lambda k: (2 * k + 1) * P, IDX_HEADS, 0, KT, IDX_HEADS)\
                    .then_inc(chunk_used, 1)

            statistics()
            columns(0)
            product(BY_NAME["moba_qk"], OP_BEFORE["moba_qk"])
            product(BY_NAME["moba_v"], 0)
            attention(0, 1)
            product(BY_NAME["moba_o"], OP_BEFORE["moba_o"])
            for n in range(2):
                if n == 1:
                    statistics()
                    columns(0)
                    dsa_in()
                    statistics(2 * SEQ)
                    pe.wait_ge(rstd_ready, n_stat[0])
                    low_rank()
                    attention(1, 1)
                    product(BY_NAME["dsa_o"], OP_BEFORE["dsa_o"])
                statistics()
                product(BY_NAME[f"up_{n}"], OP_BEFORE[f"up_{n}"])
                product(BY_NAME[f"down_{n}"], OP_BEFORE[f"down_{n}"])
            statistics()
            statistics()
            product(BY_NAME["conv_ch"], OP_BEFORE["conv_ch"])
            product(BY_NAME["conv_b"], OP_BEFORE["conv_ch"])
            product(BY_NAME["conv_out"], OP_BEFORE["conv_out"])
            statistics()
            for n in range(2):
                if n == 1:
                    statistics()
                    columns(0)
                    product(BY_NAME["dil_k"], OP_BEFORE["dil_k"])
                    product(BY_NAME["dil_v"], 0)
                    product(BY_NAME["dil_q"], OP_BEFORE["dil_q"])
                    attention(2, NB)
                    product(BY_NAME["dil_o"], OP_BEFORE["dil_o"])
                    statistics()
                statistics()
                product(BY_NAME[f"gate_up_{n}"], OP_BEFORE[f"gate_up_{n}"])
                product(BY_NAME[f"ffn_down_{n}"], OP_BEFORE[f"ffn_down_{n}"])
                statistics()

        @block.scalar
        def _(act):
            n_sq = [0]

            def split(stage, i, u):
                g = stage.base + u + SPLIT_SLOTS
                if stage is STAGES[-1] and isinstance(i, int) and i * stage.unroll + g >= CHUNKS:
                    return
                per = stage.unroll // RAW_SLOTS
                s = g % RAW_SLOTS
                act.wait_ge(raw_landed[s], (i * per + (g // RAW_SLOTS + 1)) * 16)
                act.wait_ge(chunk_used, i * stage.unroll + (g - 1))
                nc.scalar.activation(whi[:, g % SPLIT_SLOTS, :], raw[:, s, :], ACT.Copy).then_inc(hi_split, 1)

            def first_split():
                for g in range(SPLIT_SLOTS):
                    act.wait_ge(raw_landed[g], 16)
                    nc.scalar.activation(whi[:, g, :], raw[:, g, :], ACT.Copy).then_inc(hi_split, 1)

            def square(src, n=KT):
                nc.scalar.activation(sq[:, 0:n, :], src, ACT.Square).then_inc(squares, 1)
                n_sq[0] += 1

            def root(over, width=SEQ):
                act.wait_ge(totals, n_sq[0])
                nc.scalar.activation(std[:, :, :].rearrange("p a t -> p (a t)")[:, 0:width], bank[:, STAT, 0:width],
                                     ACT.Sqrt, bias=eps[:, 0:1], scale=1.0 / over).then_inc(roots, 1)

            def high_operand(gain):
                for k in range(KT):
                    nc.scalar.activation(ahi[:, k, :], x[:, k, :], ACT.Copy,
                                         scale=gains[:, gain + k:gain + k + 1]).then_inc(act_hi, 1)

            def norm_operand(gain):
                square(x[:, :, :])
                high_operand(GAIN_AT[gain])
                root(D)

            def through(stage, step=None):
                def body(i, u):
                    split(stage, i, u)
                    if step is not None:
                        step(i, u)
                in_loop(act, stage, body)

            def relu_stage(stage):
                before = banks_before(stage, "relu", "swiglu")

                def step(i, u):
                    j = i * stage.unroll + u
                    act.wait_ge(bank_read, i * stage.unroll + (stage.bank_base + u + 1))
                    nc.scalar.activation(zz[:, :, :], z[:, :, :], ACT.Square).then_inc(e_ready, 1)
                    act.wait_ge(e_ready, i * stage.unroll + (before + u + 1))
                    nc.scalar.activation(bhi[:, bass.ds(j * 2, 2), :], zz[:, :, :], ACT.Copy).then_inc(h_ready, 1)
                through(stage, step)

            def swiglu_stage(stage):
                before = banks_before(stage, "relu", "swiglu")

                def step(i, u):
                    act.wait_ge(bank_read, i * stage.unroll + (stage.bank_base + u + 1))
                    nc.scalar.activation(zz[:, 0, :], z[:, 0, :], ACT.Silu).then_inc(h_ready, 1)
                through(stage, step)

            def rope_stage(stage):
                before = banks_before(stage, "rope")

                def step(i, u):
                    b = static_bank(stage, u)
                    act.wait_ge(rope_cos, i * stage.unroll + (before + u + 1))
                    act.wait_ge(bank_read, i * stage.unroll + (stage.bank_base + u))
                    for d in range(4):
                        s = d ^ 1
                        ins = nc.scalar.activation(zz[d * 32:(d + 1) * 32, :, :].rearrange("p a t -> p (a t)"),
                                                   bank[s * 32:(s + 1) * 32, b, :], ACT.Copy)
                    ins.then_inc(rot_ready, 1)
                through(stage, step)

            def attention(run, branches):
                base, wide = HEADS * run, branches > 1
                ahead = AHEAD[wide]

                def step(i, u):
                    h = u - ahead
                    if h >= 3 and h % 2 == 1:
                        t = (h - 3) // 2
                        act.wait_ge(ot_ready, i * 2 + (base // 2 + t + 1))
                        nc.scalar.activation(ahi[:, bass.ds(i * 2 + t, 1), :],
                                             bank[:, O_BANKS[t % 2]:O_BANKS[t % 2] + 1, SEQ:2 * SEQ], ACT.Copy)\
                          .then_inc(ohi_ready, 1)
                    if 0 <= h < HEADS:
                        act.wait_ge(t_ready, i * 4 + (base + h + 1))
                        held = base + h if wide else base + h - 1
                        if held > 0:
                            act.wait_ge(o_ready, i * 4 + held)
                        if wide:
                            ins = nc.scalar.activation(pt[:, :, :], bank[:, 3:6, 0:CAUSAL], ACT.Copy)
                        else:
                            ins = nc.scalar.activation(pt[:, h % 2, :], bank[:, PT_BANKS[h % 2], 0:CAUSAL], ACT.Copy)
                        ins.then_inc(tc_ready, 1)
                    if u < HEADS:
                        s = u % 4
                        act.wait_ge(m_ready, i * 4 + (base + u + 1))
                        if wide:
                            l = logits3[:, u % 2, :].rearrange("p (g c) -> p g c", g=NB)
                            first, second = l[:, :, 0:P], l[:, :, P:CAUSAL]
                        else:
                            first, second = logits[:, s, 0:P], logits[:, s, P:CAUSAL]
                        nc.scalar.activation(first, first, ACT.Exp, bias=neg_max[:, s, 0:1],
                                             accum_out=row_sum[:, s, 0:1])
                        nc.scalar.activation(second, second, ACT.Exp, bias=neg_max[:, s, 1:2],
                                             accum_out=row_sum[:, s, 1:2]).then_inc(p_ready, 1)

                in_steps(act, step, HEADS + ahead + 2)

            act.dma_start(gains[:, :], gains_in).then_inc(const_landed, 16)
            act.dma_start(consts[:, :], const_in[:, C_IDENT:CONST_COLS]).then_inc(const_landed, 16)
            act.dma_start(masks3[:, :, :], const_in[:, 0:C_CAUSAL].rearrange("p (g c) -> p g c", g=NB))\
               .then_inc(const_landed, 16)
            act.dma_start(causal[:, :], const_in[:, C_CAUSAL:C_IDENT]).then_inc(const_landed, 16)
            act.dma_start(pos_i[:, :], bass.AP(tensor=pos_in.tensor, offset=0, ap=[[0, P], [1, SEQ]]))\
               .then_inc(const_landed, 16)
            act.wait_ge(x_landed, 16)
            act.wait_ge(const_landed, 80)
            for n, dst in enumerate((sin_t, cos_t)):
                act.wait_ge(angles, n + 1)
                nc.scalar.activation(dst[:, :], angle[:, :] if n == 0 else shifted[:, :], ACT.Sin).then_inc(sines, 1)
            first_split()
            act.wait_ge(sines, 2)
            act.wait_ge(ones_set, 2)
            norm_operand("ln_attn_0")
            through(BY_NAME["moba_qk"])
            through(BY_NAME["moba_v"])
            attention(0, 1)
            through(BY_NAME["moba_o"])
            for n in range(2):
                if n == 1:
                    act.wait_ge(bank_read, BY_NAME["dsa_in"].bank_base)
                    norm_operand("ln_attn_1")
                    through(BY_NAME["dsa_in"])
                    act.wait_ge(bank_read, BY_NAME["dsa_low"].bank_base)
                    nc.scalar.activation(sq[:, 0:2, :], z_q[:, :, :], ACT.Square)
                    nc.scalar.activation(sq[:, 2:4, :], z_kv[:, :, :], ACT.Square).then_inc(squares, 1)
                    n_sq[0] += 1
                    for k in range(2):
                        for src, at_tile in ((z_q, 0), (z_kv, 2)):
                            g = LATENT_GAIN_AT + at_tile + k
                            nc.scalar.activation(ahi[:, at_tile + k, :], src[:, k, :], ACT.Copy,
                                                 scale=gains[:, g:g + 1]).then_inc(act_hi, 1)
                    root(LORA, 2 * SEQ)
                    for u in range(4):
                        split(BY_NAME["dsa_low"], 0, u)
                        if u == 0:
                            for h in range(IDX_HEADS):
                                act.wait_ge(idx_ready, h + 1)
                                if h >= 2:
                                    act.wait_ge(idx_used, h - 1)
                                nc.scalar.activation(relu_s[:, h % 2, :], bank[:, 2 + h % 4, 0:CAUSAL], ACT.Relu)\
                                  .then_inc(idx_relu, 1)
                    attention(1, 1)
                    through(BY_NAME["dsa_o"])
                act.wait_ge(bank_read, BY_NAME[f"up_{n}"].bank_base)
                norm_operand(f"ln_mlp_{n}")
                relu_stage(BY_NAME[f"up_{n}"])
                through(BY_NAME[f"down_{n}"])
            act.wait_ge(bank_read, BY_NAME["conv_ch"].bank_base)
            square(x[:, :, :])
            root(D)
            act.wait_ge(x_done, 1)
            norm_operand("mix_pre_0")
            through(BY_NAME["conv_ch"])
            through(BY_NAME["conv_b"])
            through(BY_NAME["conv_out"])
            act.wait_ge(bank_read, BY_NAME["gate_up_0"].bank_base)
            square(y[:, :, :])
            root(D)
            done = 2
            for n in range(2):
                if n == 1:
                    act.wait_ge(x_done, done)
                    done += 1
                    norm_operand("kv")
                    rope_stage(BY_NAME["dil_k"])
                    through(BY_NAME["dil_v"])
                    act.wait_ge(chunk_used, BY_NAME["dil_q"].base)
                    high_operand(GAIN_AT["mix_pre_1"])
                    rope_stage(BY_NAME["dil_q"])
                    attention(2, NB)
                    through(BY_NAME["dil_o"])
                    act.wait_ge(bank_read, BY_NAME["gate_up_1"].bank_base)
                    square(y[:, :, :])
                    root(D)
                act.wait_ge(x_done, done)
                done += 1
                norm_operand(f"ffn_pre_{n}")
                swiglu_stage(BY_NAME[f"gate_up_{n}"])
                through(BY_NAME[f"ffn_down_{n}"])
                down = BY_NAME[f"ffn_down_{n}"]
                act.wait_ge(bank_read, down.bank_base + down.banks)
                square(y[:, :, :])
                root(D)

        @block.gpsimd
        def _(pool):
            G = nc.gpsimd

            def store_bias():
                whole = by_dist[:, :]
                for lo, hi, offset in ((0, P, 2 * P - 1), (P, CAUSAL, P - 1)):
                    src = bass.AP(tensor=whole.tensor, offset=offset, ap=[list(whole.ap[0]), [-1, P], [1, hi - lo]])
                    pool.dma_start(toeplitz[:, :, lo:hi], src).then_inc(dist_stored, 16)

            def load_bias():
                pool.dma_start(bias[:, :, :], toeplitz.rearrange("h p c -> p h c")).then_inc(bias_landed, 16)

            def attention(run, branches, masked=False):
                base, wide = HEADS * run, branches > 1
                if wide:
                    q_of, k_of = (a[:, :, :].rearrange("p (g k) t -> p g k t", g=NB) for a in (q3, k3))
                else:
                    q_of, k_of = q1.unsqueeze(1), k1.unsqueeze(1)

                def stage_qk(i, t):
                    slot = t % 2
                    for src, dst in ((q_of, q_pair), (k_of, k_pair)):
                        G.tensor_copy(dst[:, slot, 0:branches, :].unsqueeze(2), src[:, :, bass.ds(i * 2 + t, 1), :])\
                         .then_inc(qk_staged, 1)

                def step(i, u):
                    if masked and u < HEADS:
                        if u >= 4:
                            pool.wait_ge(l_ready, i * 4 + (base + u - 3))
                        G.tensor_tensor(masked_bias[:, u % 4, :], bias[:, bass.ds(i * 4 + u, 1), :].squeeze(1),
                                        topmask[:, :], ALU.add).then_inc(topped, 1)
                    if u % 2 and u < HEADS - 1:
                        t = u // 2
                        if base + 2 * t > 0:
                            pool.wait_ge(s_ready, i * 4 + (base + 2 * t))
                        stage_qk(i, t + 1)

                stage_qk(0, 0)
                if masked:
                    pool.wait_ge(topmask_ready, 1)
                in_steps(pool, step, HEADS, first=4)

            pool.dma_start(table[:, :], table_in).then_inc(table_landed, 16)
            pool.dma_start(onehot[:, :], onehot_in).then_inc(table_landed, 16)
            pool.dma_start(negmask[:, :], negmask_in).then_inc(table_landed, 16)
            pool.wait_ge(dist_done, 1)
            store_bias()
            pool.wait_ge(dist_stored, 32)
            load_bias()
            pool.wait_ge(bank_read, BY_NAME["moba_o"].bank_base)
            attention(0, 1)
            pool.wait_ge(bank_read, BY_NAME["dsa_in"].bank_base)
            load_bias()
            pool.wait_ge(bias_landed, 32)
            pool.wait_ge(bank_read, BY_NAME["dsa_o"].bank_base)
            attention(1, 1, masked=True)
            pool.wait_ge(bank_read, BY_NAME["dil_o"].bank_base)
            attention(2, NB)

        @block.vector
        def _(dve):
            own = Own(dve, dve_step)
            n_norm = [0]
            n_hi = [0]
            V = nc.vector

            def plain(ap):
                return ap.bitcast(F32)

            def split(stage, i, u):
                g = stage.base + u + SPLIT_SLOTS
                if stage is STAGES[-1] and isinstance(i, int) and i * stage.unroll + g >= CHUNKS:
                    return
                dve.wait_ge(hi_split, i * stage.unroll + (g + 1))
                s = g % SPLIT_SLOTS
                V.tensor_tensor(wlo[:, s, :], raw[:, g % RAW_SLOTS, :], plain(whi[:, s, :]), ALU.subtract)\
                 .then_inc(lo_split, 1)

            def first_split():
                for g in range(SPLIT_SLOTS):
                    dve.wait_ge(hi_split, g + 1)
                    V.tensor_tensor(wlo[:, g, :], raw[:, g, :], plain(whi[:, g, :]), ALU.subtract).then_inc(lo_split, 1)

            def sum_squares(n=KT):
                n_norm[0] += 1
                dve.wait_ge(squares, n_norm[0])
                V.tensor_reduce(ssum[:, 0, :], sq[:, 0:n, :].rearrange("p k t -> p t k"), AX.X, ALU.add).then_inc(sums, 1)

            def inverse_root(width=SEQ):
                dve.wait_ge(roots, n_norm[0])
                V.reciprocal(rstd[:, :, :].rearrange("p a t -> p (a t)")[:, 0:width],
                             std[:, :, :].rearrange("p a t -> p (a t)")[:, 0:width]).then_inc(rstd_ready, 1)
                dve.wait_ge(rstd_ready, n_norm[0])

            def low_operand(src, gain):
                for k in range(KT):
                    n_hi[0] += 1
                    dve.wait_ge(act_hi, n_hi[0])
                    V.scalar_tensor_tensor(alo[:, k, :], src[:, k, :], gains[:, gain + k:gain + k + 1],
                                           plain(ahi[:, k, :]), ALU.mult, ALU.subtract).then_inc(op_ready, 1)

            def norm_operand(gain):
                sum_squares()
                low_operand(x, GAIN_AT[gain])
                inverse_root()

            def token_scale(n):
                dve.wait_ge(col_ready, n)
                V.tensor_copy(rcol[:, :], bank[:, STAT, 0:QT]).then_inc(rcol_ready, 1)
                dve.wait_ge(rcol_ready, n)

            def both(ap):
                return ap.unsqueeze(1).to_broadcast([P, 2, SEQ])

            def through(stage, step, tail=None):
                def body(i, u):
                    done = not stage.quartered or u % 4 == 3
                    if done:
                        dve.wait_ge(chunk_used, i * stage.unroll + (stage.base + u + 1))
                        local = u // 4 if stage.quartered else u
                        per = 2 if stage.quartered else stage.unroll
                        b = bank[:, lin_bank(stage, local), :].rearrange("p (a t) -> p a t", a=2)
                        step(i, u, i * per + local, b)
                    split(stage, i, u)
                    if done and tail is not None:
                        tail(i, u, i * per + local, b)
                in_loop(dve, stage, body)

            def scaled_into(dst):
                def step(i, u, j, b):
                    V.tensor_tensor(dst[:, bass.ds(j * 2, 2), :], b, both(rstd[:, 0, :]), ALU.mult).then_inc(bank_read, 1)
                return step

            def tokens_into(v, width):
                def step(i, u, j, b):
                    for t in range(QT):
                        ins = V.tensor_scalar(v[:, t, bass.ds(j * 256, 256)], b[:, t, :], rcol[:, t:t + 1], None, ALU.mult)
                    ins.then_inc(bank_read, 1)
                return step

            def residual(i, u, j, b):
                d = x[:, bass.ds(j * 2, 2), :]
                V.tensor_tensor(d, b, d, ALU.add).then_inc(bank_read, 1)

            def before_norm(i, u, j, b):
                V.tensor_copy(y[:, bass.ds(j * 2, 2), :], b).then_inc(bank_read, 1)

            def relu_stage(stage):
                before = banks_before(stage, "relu", "swiglu")

                def step(i, u, j, b):
                    V.scalar_tensor_tensor(z[:, :, :], b, 0.0, both(rstd[:, 0, :]), ALU.max, ALU.mult)\
                     .then_inc(bank_read, 1)

                def tail(i, u, j, b):
                    dve.wait_ge(h_ready, i * stage.unroll + (before + u + 1))
                    V.tensor_tensor(blo[:, bass.ds(j * 2, 2), :], zz[:, :, :], plain(bhi[:, bass.ds(j * 2, 2), :]),
                                    ALU.subtract).then_inc(op_ready, 1)
                return step, tail

            def swiglu_stage(stage):
                before = banks_before(stage, "relu", "swiglu")
                first = banks_before(stage, "swiglu")
                operands = OP_BEFORE[STAGES[stage.n + 1].name]

                def step(i, u, j, b):
                    dve.wait_ge(op_ready, i * stage.unroll + (operands + u))
                    V.tensor_tensor(z[:, :, :], b, both(rstd[:, 0, :]), ALU.mult).then_inc(bank_read, 1)

                def tail(i, u, j, b):
                    n = i * stage.unroll + (first + u + 1)
                    dve.wait_ge(h_ready, i * stage.unroll + (before + u + 1))
                    V.tensor_tensor(zz[:, 1:2, :], zz[:, 0:1, :], z[:, 1:2, :], ALU.mult).then_inc(y_ready, 1)
                    dve.wait_ge(y_ready, n)
                    V.tensor_copy(bhi[:, bass.ds(j, 1), :], zz[:, 1:2, :]).then_inc(yhi_ready, 1)
                    dve.wait_ge(yhi_ready, n)
                    V.tensor_tensor(blo[:, bass.ds(j, 1), :], zz[:, 1:2, :], plain(bhi[:, bass.ds(j, 1), :]),
                                    ALU.subtract).then_inc(op_ready, 1)
                return step, tail

            def rope_stage(stage, dst):
                before = banks_before(stage, "rope")

                def step(i, u, j, b):
                    dve.wait_ge(bank_read, i * stage.unroll + (stage.bank_base + u))
                    V.tensor_tensor(z[:, :, :], b, both(cos_r[:, :]), ALU.mult).then_inc(rope_cos, 1)

                def tail(i, u, j, b):
                    n = i * stage.unroll + (before + u + 1)
                    dve.wait_ge(rot_ready, n)
                    V.tensor_tensor(zz[:, :, :], zz[:, :, :], both(sin_r[:, :]), ALU.mult).then_inc(rope_sin, 1)
                    dve.wait_ge(rope_sin, n)
                    dve.wait_ge(rope_cos, n)
                    V.tensor_tensor(dst[:, bass.ds(j * 2, 2), :], z[:, :, :], zz[:, :, :], ALU.add).then_inc(bank_read, 1)
                return step, tail

            def attention(run, branches, masked=False):
                base, wide = HEADS * run, branches > 1
                ahead = AHEAD[wide]
                pairs = base // 2

                if wide:
                    v_of = v3[:, :, :].rearrange("p q (g n) -> p g q n", g=NB)
                else:
                    v_of = v1[:, :, :].unsqueeze(1)

                def stage_v(i, t):
                    dst = v_pair[:, t % 2, 0:branches * QT, :].rearrange("p (g q) n -> p g q n", q=QT)
                    V.tensor_copy(dst, v_of[:, :, :, bass.ds((i * 2 + t) * P, P)]).then_inc(v_staged, 1)

                for t in range(2):
                    stage_v(0, t)

                def step(i, u):
                    s = u % 4
                    if u < HEADS:
                        dve.wait_ge(s_ready, i * 4 + (base + u + 1))
                        if wide:
                            l = logits3[:, u % 2, :].rearrange("p (g c) -> p g c", g=NB)
                            V.scalar_tensor_tensor(l, bank[:, 0:3, 0:CAUSAL], SCALE, masks3[:, :, :],
                                                   ALU.mult, ALU.add).then_inc(l_ready, 1)
                            first, second, axes = l[:, :, 0:P], l[:, :, P:CAUSAL], AX.XY
                        else:
                            l = logits[:, s, :]
                            if masked:
                                dve.wait_ge(topped, i * 4 + (u + 1))
                                b = masked_bias[:, s, :]
                            else:
                                b = bias[:, bass.ds(i * 4 + u, 1), :].squeeze(1)
                            V.scalar_tensor_tensor(l, bank[:, S_BANKS[s], 0:CAUSAL], SCALE, b,
                                                   ALU.mult, ALU.add).then_inc(l_ready, 1)
                            first, second, axes = l[:, 0:P], l[:, P:CAUSAL], AX.X
                        dve.wait_ge(l_ready, i * 4 + (base + u + 1))
                        V.tensor_reduce(neg_max[:, s, 0:1], first, axes, ALU.max, negate=True)
                        V.tensor_reduce(neg_max[:, s, 1:2], second, axes, ALU.max, negate=True).then_inc(m_ready, 1)
                    if 1 <= u <= HEADS:
                        dve.wait_ge(p_ready, i * 4 + (base + u))
                        V.reciprocal(inv_sum[:, (u - 1) % 4, :], row_sum[:, (u - 1) % 4, :]).then_inc(i_ready, 1)
                    h = u - ahead
                    if h >= 3 and h % 2 == 1:
                        t = (h - 3) // 2
                        dve.wait_ge(ohi_ready, i * 2 + (pairs + t + 1))
                        V.tensor_tensor(alo[:, bass.ds(i * 2 + t, 1), :],
                                        bank[:, O_BANKS[t % 2]:O_BANKS[t % 2] + 1, SEQ:2 * SEQ],
                                        plain(ahi[:, bass.ds(i * 2 + t, 1), :]), ALU.subtract).then_inc(op_ready, 1)
                    if 1 <= h < HEADS and h % 2 == 1:
                        t = h // 2
                        dve.wait_ge(o_ready, i * 4 + (base + h + 1))
                        dve.wait_ge(i_ready, i * 4 + (base + h + 1))
                        if t >= 2:
                            dve.wait_ge(ot_ready, i * 2 + (pairs + t - 1))
                        inv = inv_sum[:, (h - 1) % 4:(h - 1) % 4 + 2, :].rearrange("p h q -> p q h")
                        V.tensor_tensor(o_pair[:, t % 2, :].rearrange("p (q h d) -> p q h d", q=QT, h=2),
                                        bank[:, O_BANKS[t % 2], 0:SEQ].rearrange("p (q h d) -> p q h d", q=QT, h=2),
                                        inv.unsqueeze(3).to_broadcast([P, QT, 2, DH]), ALU.mult).then_inc(on_ready, 1)
                        if h < HEADS - 4:
                            stage_v(i, t + 2)

                in_steps(dve, step, HEADS + ahead + 2, first=ahead + 5)

            def add_normed(gain):
                sum_squares()
                inverse_root()
                own.link(V.tensor_tensor(y[:, :, :], y[:, :, :], rstd[:, 0:1, :].to_broadcast([P, KT, SEQ]), ALU.mult))
                for k in range(KT):
                    g = GAIN_AT[gain] + k
                    ins = V.scalar_tensor_tensor(x[:, k, :], y[:, k, :], gains[:, g:g + 1], x[:, k, :], ALU.mult, ALU.add)
                ins.then_inc(x_done, 1)
                x_count[0] += 1
                dve.wait_ge(x_done, x_count[0])

            def top_keys():
                own.link(V.tensor_tensor(score[:, :], score[:, :], causal[:, :], ALU.add))
                halves = ((0, slice(0, P)), (1, slice(P, CAUSAL)))
                for _ in range(TOPK // 8):
                    for t, cols in halves:
                        ins = V.max(best[:, t, :], score[:, cols])
                    own.link(ins)
                    for t, cols in halves:
                        ins = V.match_replace(score[:, cols], best[:, t, :], score[:, cols], TAKEN)
                    own.link(ins)
                V.tensor_scalar(topmask[:, :], score[:, :], TAKEN / 2, NEG, ALU.is_gt, ALU.mult).then_inc(topmask_ready, 1)

            x_count = [0]
            V.memset(ones[:, :], 1.0).then_inc(ones_set, 1)
            V.memset(eps[:, :], EPS).then_inc(ones_set, 1)
            dve.wait_ge(dist_ready, 1)
            V.tensor_tensor(by_dist[:, :], bank[0:HEADS, 0, 0:CAUSAL], negmask[:, :], ALU.add).then_inc(dist_done, 1)
            dve.wait_ge(const_landed, 80)
            own.link(V.tensor_copy(angle[:, :], pos_i[:, :]))
            own.link(V.tensor_scalar(angle[:, :], angle[:, :], consts[:, C_FREQ - C_IDENT:C_FREQ - C_IDENT + 1], None,
                                     ALU.mult))
            magic = 12582912.0
            own.link(V.tensor_scalar(turns[:, :], angle[:, :], 1.0 / (2 * np.pi), magic, ALU.mult, ALU.add))
            own.link(V.tensor_scalar(turns[:, :], turns[:, :], -magic, None, ALU.add))
            two_pi = 2 * np.pi
            part1 = 6.28125
            part2 = float(np.round((two_pi - part1) * 2 ** 21) / 2 ** 21)
            part3 = float(two_pi - part1 - part2)
            for part in (part1, part2, part3):
                own.link(V.scalar_tensor_tensor(angle[:, :], turns[:, :], -part, angle[:, :], ALU.mult, ALU.add))
            edge = 3.1415925
            own.link(V.tensor_scalar(shifted[:, :], angle[:, :], float(np.pi / 2), None, ALU.add))
            own.link(V.tensor_scalar(turns[:, :], shifted[:, :], float(np.pi), -two_pi, ALU.is_gt, ALU.mult))
            own.link(V.tensor_tensor(shifted[:, :], shifted[:, :], turns[:, :], ALU.add))
            V.tensor_scalar(angle[:, :], angle[:, :], -edge, edge, ALU.max, ALU.min).then_inc(angles, 1)
            V.tensor_scalar(shifted[:, :], shifted[:, :], -edge, edge, ALU.max, ALU.min).then_inc(angles, 1)
            dve.wait_ge(sines, 2)
            own.link(V.tensor_scalar(sin_t[:, :], sin_t[:, :], consts[:, C_SIGN - C_IDENT:C_SIGN - C_IDENT + 1], None,
                                     ALU.mult))
            first_split()
            norm_operand("ln_attn_0")
            token_scale(1)

            through(BY_NAME["moba_qk"], scaled_into(qk1))
            through(BY_NAME["moba_v"], tokens_into(v1, D))
            dve.wait_ge(bias_landed, 16)
            attention(0, 1)
            through(BY_NAME["moba_o"], residual)
            for n in range(2):
                if n == 1:
                    norm_operand("ln_attn_1")
                    token_scale(2)
                    stage = BY_NAME["dsa_in"]
                    for c in range(3):
                        if c < 2:
                            dve.wait_ge(chunk_used, stage.base + c + 1)
                            V.tensor_tensor((z_q, z_kv)[c][:, :, :],
                                            bank[:, lin_bank(stage, c), :].rearrange("p (a t) -> p a t", a=2),
                                            both(rstd[:, 0, :]), ALU.mult).then_inc(bank_read, 1)
                        else:
                            dve.wait_ge(low_bank, 1)
                            V.tensor_tensor(k_idx[:, :], bank[:, lin_bank(stage, 2), 0:SEQ], rstd[:, 0, :], ALU.mult)\
                             .then_inc(bank_read, 1)
                            dve.wait_ge(chunk_used, stage.base + 3)
                            for t in range(QT):
                                ins = V.tensor_scalar(w_idx[:, t, :],
                                                      bank[:, lin_bank(stage, 3), t * IDX_HEADS:(t + 1) * IDX_HEADS],
                                                      rcol[:, t:t + 1], IDX_SCALE, ALU.mult, ALU.mult)
                            ins.then_inc(bank_read, 1)
                        split(stage, 0, c)
                    n_norm[0] += 1
                    dve.wait_ge(squares, n_norm[0])
                    V.tensor_tensor(ssum[:, :, :], sq[:, 0:4:2, :], sq[:, 1:4:2, :], ALU.add).then_inc(sums, 1)
                    for k in range(2):
                        for src, tile in ((z_q, 0), (z_kv, 2)):
                            g = LATENT_GAIN_AT + tile + k
                            n_hi[0] += 1
                            dve.wait_ge(act_hi, n_hi[0])
                            V.scalar_tensor_tensor(alo[:, tile + k, :], src[:, k, :], gains[:, g:g + 1],
                                                   plain(ahi[:, tile + k, :]), ALU.mult, ALU.subtract)\
                             .then_inc(op_ready, 1)
                    inverse_root(2 * SEQ)
                    stage = BY_NAME["dsa_low"]
                    j = 0
                    lows = 1
                    for c in range(4):
                        pairs = 2 if c == 0 else 4
                        for pair in range(pairs):
                            if pair == pairs - 1:
                                dve.wait_ge(chunk_used, stage.base + c + 1)
                            else:
                                lows += 1
                                dve.wait_ge(low_bank, lows)
                            b = bank[:, lin_bank(stage, j), :].rearrange("p (a t) -> p a t", a=2)
                            if c < 3:
                                dst = (q_idx, q1, k1)[c][:, 2 * pair:2 * pair + 2, :]
                                ins = V.tensor_tensor(dst, b, both(rstd[:, 1 if c == 2 else 0, :]), ALU.mult)
                            else:
                                for t in range(QT):
                                    ins = V.tensor_scalar(v1[:, t, pair * 256:(pair + 1) * 256], b[:, t, :],
                                                          rcol[:, t:t + 1], None, ALU.mult)
                            ins.then_inc(bank_read, 1)
                            j += 1
                        split(stage, 0, c)
                        if c == 0:
                            token_scale(3)
                            for h in range(IDX_HEADS):
                                dve.wait_ge(idx_relu, h + 1)
                                if h:
                                    dve.wait_ge(idx_used, h)
                                for t, cols in ((0, slice(0, P)), (1, slice(P, CAUSAL))):
                                    w = w_idx[:, t, h:h + 1]
                                    if h == 0:
                                        ins = V.tensor_scalar(score[:, cols], relu_s[:, 0, cols], w, None, ALU.mult)
                                    else:
                                        ins = V.scalar_tensor_tensor(score[:, cols], relu_s[:, h % 2, cols], w,
                                                                     score[:, cols], ALU.mult, ALU.add)
                                ins.then_inc(idx_used, 1)
                    dve.wait_ge(idx_used, IDX_HEADS)
                    top_keys()
                    dve.wait_ge(bias_landed, 32)
                    attention(1, 1, masked=True)
                    through(BY_NAME["dsa_o"], residual)
                norm_operand(f"ln_mlp_{n}")
                through(BY_NAME[f"up_{n}"], *relu_stage(BY_NAME[f"up_{n}"]))
                through(BY_NAME[f"down_{n}"], residual)
            sum_squares()
            inverse_root()
            own.link(V.tensor_tensor(x[:, :, :], x[:, :, :], rstd[:, 0:1, :].to_broadcast([P, KT, SEQ]), ALU.mult))
            for k in range(KT):
                g = GAIN_AT["final"] + k
                ins = V.tensor_scalar(x[:, k, :], x[:, k, :], gains[:, g:g + 1], None, ALU.mult)
            ins.then_inc(x_done, 1)
            x_count[0] += 1
            dve.wait_ge(x_done, 1)
            norm_operand("mix_pre_0")
            own.link(V.memset(gated[:, :, 0:2], 0.0))
            ch = BY_NAME["conv_ch"]

            def conv_step(i, u, j, b):
                V.tensor_tensor(z[:, :, :], b, both(rstd[:, 0, :]), ALU.mult).then_inc(bank_read, 1)
                dve.wait_ge(bank_read, i * ch.unroll + (ch.bank_base + u + 1))
                V.tensor_tensor(gated[:, bass.ds(j, 1), 2:2 + SEQ], z[:, 0:1, :], z[:, 1:2, :], ALU.mult)\
                 .then_inc(gate_ready, 1)

            def conv_tail(i, u, j, b):
                dve.wait_ge(gate_ready, i * ch.unroll + (u + 1))
                d = conv[:, bass.ds(j, 1), :]
                for tap in range(3):
                    w = gains[:, bass.ds(j * 3 + (CONV_AT + tap), 1)]
                    src = gated[:, bass.ds(j, 1), tap:tap + SEQ]
                    if tap == 0:
                        ins = V.tensor_scalar(d, src, w, None, ALU.mult)
                    else:
                        dve.wait_ge(tap_ready, i * (ch.unroll * 3) + (u * 3 + tap))
                        ins = V.scalar_tensor_tensor(d, src, w, d, ALU.mult, ALU.add)
                    ins.then_inc(tap_ready, 1)
            through(ch, conv_step, conv_tail)
            dve.wait_ge(tap_ready, 3 * KT)
            cb = BY_NAME["conv_b"]
            dve.wait_ge(chunk_used, cb.base)

            def gate_step(i, u, j, b):
                if u:
                    dve.wait_ge(conv_ready, u)
                V.tensor_tensor(z[:, :, :], b, both(rstd[:, 0, :]), ALU.mult).then_inc(bank_read, 1)
                dve.wait_ge(bank_read, i * cb.unroll + (cb.bank_base + u + 1))
                d = conv[:, bass.ds(j * 2, 2), :]
                V.tensor_tensor(d, z[:, :, :], d, ALU.mult).then_inc(conv_ready, 1)
            through(cb, gate_step)
            dve.wait_ge(conv_ready, 4)
            dve.wait_ge(chunk_used, cb.base + cb.chunks)
            own.link(V.tensor_copy(ahi[:, :, :], conv[:, :, :]))
            for k in range(KT):
                V.tensor_tensor(alo[:, k, :], conv[:, k, :], plain(ahi[:, k, :]), ALU.subtract).then_inc(op_ready, 1)
            through(BY_NAME["conv_out"], before_norm)
            dve.wait_ge(bank_read, BY_NAME["gate_up_0"].bank_base)
            add_normed("mix_post_0")
            for n in range(2):
                if n == 1:
                    norm_operand("kv")
                    token_scale(4)
                    V.tensor_tensor(cos_r[:, :], cos_t[:, :], rstd[:, 0, :], ALU.mult)
                    own.link(V.tensor_tensor(sin_r[:, :], sin_t[:, :], rstd[:, 0, :], ALU.mult))
                    through(BY_NAME["dil_k"], *rope_stage(BY_NAME["dil_k"], k3))
                    through(BY_NAME["dil_v"], tokens_into(v3, QW))
                    low_operand(x, GAIN_AT["mix_pre_1"])
                    through(BY_NAME["dil_q"], *rope_stage(BY_NAME["dil_q"], q3))
                    attention(2, NB)
                    through(BY_NAME["dil_o"], before_norm)
                    dve.wait_ge(bank_read, BY_NAME["gate_up_1"].bank_base)
                    add_normed("mix_post_1")
                norm_operand(f"ffn_pre_{n}")
                gu, down = BY_NAME[f"gate_up_{n}"], BY_NAME[f"ffn_down_{n}"]
                through(gu, *swiglu_stage(gu))
                through(down, before_norm)
                dve.wait_ge(bank_read, down.bank_base + down.banks)
                add_normed(f"ffn_post_{n}")


def buckets():
    n = np.arange(SEQ)
    exact = BUCKETS // 2
    large = np.log(np.maximum(n, 1).astype(np.float32) / np.float32(exact)) / np.float32(np.log(MAX_DISTANCE / exact))
    large = exact + (large * np.float32(BUCKETS - exact)).astype(np.int32)
    return np.where(n < exact, n, np.minimum(large, BUCKETS - 1))


def shape_constants():
    consts = np.zeros((P, CONST_COLS), np.float32)
    q = np.arange(P)[:, None]
    j = np.arange(CAUSAL)[None, :]
    dist = np.where(j < P, q - j, P + q - (j - P))
    for g, (window, dilation) in enumerate(BRANCHES):
        seen = (dist >= 0) & (dist <= window) & (dist % dilation == 0)
        consts[:, C_MASK + g * CAUSAL:C_MASK + (g + 1) * CAUSAL] = np.where(seen, 0.0, NEG)
    consts[:, C_CAUSAL:C_IDENT] = np.where(dist >= 0, 0.0, NEG)
    consts[:, C_IDENT:C_IDENT + P] = np.eye(P)
    half = DH // 2
    freq = (10000.0 ** (-np.arange(half, dtype=np.float32).astype(np.float64) / half)).astype(np.float32)
    consts[:, C_FREQ] = np.tile(freq, P // half)
    consts[:, C_SIGN] = np.where(np.arange(P) % DH < half, -1.0, 1.0)
    at_dist = 2 * P - 1 - np.arange(CAUSAL)
    b = buckets()
    onehot = np.zeros((BUCKETS, CAUSAL), np.float32)
    for u in range(CAUSAL):
        if at_dist[u] >= 0:
            onehot[b[at_dist[u]], u] = 1.0
    negmask = np.broadcast_to(np.where(at_dist >= 0, 0.0, NEG).astype(np.float32), (HEADS, CAUSAL))
    return consts, onehot, np.ascontiguousarray(negmask)


def packed(inp):
    stream = np.zeros((CHUNKS, P, CW), np.float32)
    at = [0]

    def put(tiles):
        k, _, n = tiles.shape
        stream[at[0], :, :k * n] = tiles.transpose(1, 0, 2).reshape(P, k * n)
        at[0] += 1

    def by_pairs(w, starts):
        w = w.reshape(-1, P, w.shape[1])
        for a, b in starts:
            put(np.concatenate([w[:, :, a:a + P], w[:, :, b:b + P]], axis=2))

    def across(w, lo, hi):
        by_pairs(w, [(c, c + P) for c in range(lo, hi, 2 * P)])

    def quartered(w, tiles):
        for c in range(0, D, 2 * P):
            for k0, nk in QUARTERS[tiles]:
                by_pairs(w[k0 * P:(k0 + nk) * P], [(c, c + P)])

    def low(w):
        w = w.reshape(2, P, -1)
        put(np.concatenate([w, np.zeros((2, P, 1024 - w.shape[2]), np.float32)], axis=2))

    across(inp["moba_w_qkv"][0], 0, 3 * D)
    across(inp["moba_w_o"][0], 0, D)
    for n in range(2):
        if n == 1:
            w = inp["dsa_w_in"][0]
            across(w, 0, 2 * LORA)
            keys, weights = w[:, 2 * LORA:2 * LORA + DH], w[:, 2 * LORA + DH:]
            tail = np.concatenate([keys, keys, weights, np.zeros((D, P - IDX_HEADS), np.float32)], axis=1)
            across(tail, 0, 2 * P)
            low(inp["dsa_w_qi"][0])
            low(inp["dsa_w_uq"][0])
            low(inp["dsa_w_uk"][0].transpose(2, 0, 1).reshape(LORA, HEADS * DH))
            low(inp["dsa_w_uv"][0].transpose(1, 0, 2).reshape(LORA, HEADS * DH))
            across(inp["dsa_w_o"][0], 0, D)
        across(inp["mlp_w_up"][n], 0, FF)
        quartered(inp["mlp_w_down"][n], HID_TILES)
    by_pairs(inp["conv_w_in_2"][0], [(D + c, 2 * D + c) for c in range(0, D, P)])
    across(inp["conv_w_in_2"][0], 0, D)
    across(inp["conv_w_out_2"][0], 0, D)
    for n in range(2):
        if n == 1:
            across(inp["w_kv_2"], 0, 2 * QW)
            across(inp["w_q_2"][0], 0, QW)
            across(inp["w_o_2"][0], 0, D)
        by_pairs(inp["ffn_w_gate_up_2"][n], [(c, FF2 + c) for c in range(0, FF2, P)])
        quartered(inp["ffn_w_down_2"][n], HID2_TILES)
    assert at[0] == CHUNKS
    return stream


def packed_gains(inp):
    rows = {"ln_attn_0": inp["ln_attn"][0], "ln_attn_1": inp["ln_attn"][1], "ln_mlp_0": inp["ln_mlp"][0],
            "ln_mlp_1": inp["ln_mlp"][1], "final": inp["final_norm"], "kv": inp["kv_norm_2"]}
    for n in range(2):
        rows[f"mix_pre_{n}"] = inp["mix_norm_pre_2"][n]
        rows[f"mix_post_{n}"] = inp["mix_norm_post_2"][n]
        rows[f"ffn_pre_{n}"] = inp["ffn_norm_pre_2"][n]
        rows[f"ffn_post_{n}"] = inp["ffn_norm_post_2"][n]
    cols = [rows[g].reshape(-1, P).T for g in GAINS]
    cols += [inp["dsa_g_q"][0].reshape(-1, P).T, inp["dsa_g_kv"][0].reshape(-1, P).T]
    cols += [inp["conv_w_2"][0].reshape(3, KT, P).transpose(2, 1, 0).reshape(P, KT * 3)]
    return np.ascontiguousarray(np.concatenate(cols, axis=1))


def kernel(**inputs):
    import concourse.bacc as bacc
    from concourse.bass_utils import run_bass_kernel_spmd

    inp = {name: np.asarray(a) for name, a in inputs.items()}
    consts, onehot, negmask = shape_constants()
    arrays = {
        "weight_stream": packed(inp),
        "x_features": np.ascontiguousarray(inp["x"][0].T.reshape(KT, P, SEQ).transpose(1, 0, 2)),
        "gain_columns": packed_gains(inp),
        "bias_table": np.ascontiguousarray(inp["rel_bias"]),
        "token_positions": np.ascontiguousarray(inp["positions_2"]),
        "shape_consts": consts,
        "bucket_onehot": onehot,
        "ahead_mask": negmask,
    }
    nc = bacc.Bacc("TRN2", target_bir_lowering=False, num_devices=1)
    args = [nc.dram_tensor(name, a.shape, mybir.dt.from_np(a.dtype), kind="ExternalInput").ap()
            for name, a in arrays.items()]
    toeplitz = nc.dram_tensor("bias_by_head", (HEADS, P, CAUSAL), F32).ap()
    out = nc.dram_tensor("out_features", (P, KT, SEQ), F32, kind="ExternalOutput").ap()
    build(nc, *args, toeplitz, out)
    r = run_bass_kernel_spmd(nc, [arrays], core_ids=[0])
    got = r.results[0]["out_features"]
    return np.ascontiguousarray(got.transpose(1, 0, 2).reshape(D, SEQ).T)[None]
```

```python
from contextlib import ExitStack

import numpy as np

import concourse.bass as bass
from concourse import mybir

F32 = mybir.dt.float32
F32R = mybir.dt.float32r
I32 = mybir.dt.int32
ALU = mybir.AluOpType
ACT = mybir.ActivationFunctionType
AX = mybir.AxisListType

P = 128
SEQ = 256
QT = SEQ // P
D = 1024
KT = D // P
HEADS = 16
DH = 64
FF = 4096
FF2 = 2816
HID_TILES = FF // P
HID2_TILES = FF2 // P
BUCKETS = 32
MAX_DISTANCE = 128
IDX_HEADS = 8
LORA = 256
TOPK = 64
BRANCHES = ((128, 1), (512, 4), (2048, 16))
NB = len(BRANCHES)
QW = NB * HEADS * DH
EPS = 1e-6
NEG = -1e30
TAKEN = -3e38
SCALE = DH ** -0.5
IDX_SCALE = IDX_HEADS ** -0.5 * DH ** -0.5
CAUSAL = P + SEQ

CW = 2048
RAW_SLOTS = 4
SPLIT_SLOTS = 2
LIN_BANKS = 2

QUARTERS = {HID_TILES: ((0, 8), (8, 8), (16, 8), (24, 8)), HID2_TILES: ((0, 6), (6, 6), (12, 5), (17, 5))}


class Stage:

    def __init__(self, name, kind, chunks, banks, contraction=KT):
        self.name, self.kind, self.chunks, self.banks, self.contraction = name, kind, chunks, banks, contraction
        self.quartered = contraction != KT
        self.unroll = 8 if self.quartered else 4


STAGES = [
    Stage("moba_qk", "scale", 8, 8),
    Stage("moba_v", "token", 4, 4),
    Stage("moba_o", "residual", 4, 4),
    Stage("up_0", "relu", 16, 16),
    Stage("down_0", "residual", 16, 4, HID_TILES),
    Stage("dsa_in", "dsa_in", 3, 4),
    Stage("dsa_low", "dsa_low", 4, 14),
    Stage("dsa_o", "residual", 4, 4),
    Stage("up_1", "relu", 16, 16),
    Stage("down_1", "residual", 16, 4, HID_TILES),
    Stage("conv_ch", "conv", 8, 8),
    Stage("conv_b", "gate", 4, 4),
    Stage("conv_out", "post", 4, 4),
    Stage("gate_up_0", "swiglu", 22, 22),
    Stage("ffn_down_0", "post", 16, 4, HID2_TILES),
    Stage("dil_k", "rope", 12, 12),
    Stage("dil_v", "token", 12, 12),
    Stage("dil_q", "rope", 12, 12),
    Stage("dil_o", "post", 4, 4),
    Stage("gate_up_1", "swiglu", 22, 22),
    Stage("ffn_down_1", "post", 16, 4, HID2_TILES),
]
CHUNKS = 0
_banks = 0
for _n, _s in enumerate(STAGES):
    _s.n, _s.base, _s.bank_base = _n, CHUNKS, _banks
    CHUNKS += _s.chunks
    _banks += _s.banks
BY_NAME = {s.name: s for s in STAGES}


OPERANDS = [("moba_qk", KT), ("moba_o", KT), ("up_0", KT), ("down_0", FF // 256), ("dsa_in", KT), ("dsa_low", 4),
            ("dsa_o", KT), ("up_1", KT), ("down_1", FF // 256), ("conv_ch", KT), ("conv_out", KT // 2), ("gate_up_0", KT),
            ("ffn_down_0", HID2_TILES), ("dil_k", KT), ("dil_q", KT), ("dil_o", KT), ("gate_up_1", KT),
            ("ffn_down_1", HID2_TILES)]
OP_BEFORE = {name: sum(n for _, n in OPERANDS[:m]) for m, (name, _) in enumerate(OPERANDS)}
ATTENTION_FOR = ["moba_o", "dsa_o", "dil_o"]


def banks_before(stage, *kinds):
    return sum(s.banks for s in STAGES[:stage.n] if s.kind in kinds)


def in_loop(eng, stage, step, first=0):
    looped = (stage.chunks - first) // stage.unroll - (stage is STAGES[-1])
    if looped > 1:
        with eng.Fori(0, looped) as i:
            for u in range(first, first + stage.unroll):
                step(i, u)
    else:
        looped = 0
    for c in range(first + looped * stage.unroll, stage.chunks):
        step(0, c)


class Own:

    def __init__(self, eng, sem):
        self.eng, self.sem, self.n = eng, sem, 0

    def link(self, ins):
        self.n += 1
        ins.then_inc(self.sem, 1)
        self.eng.wait_ge(self.sem, self.n)


GAINS = ["ln_attn_0", "ln_mlp_0", "ln_attn_1", "ln_mlp_1", "final", "mix_pre_0", "mix_post_0", "ffn_pre_0",
         "ffn_post_0", "kv", "mix_pre_1", "mix_post_1", "ffn_pre_1", "ffn_post_1"]
GAIN_AT = {g: KT * n for n, g in enumerate(GAINS)}
LATENT_GAIN_AT = KT * len(GAINS)
CONV_AT = LATENT_GAIN_AT + 2 * (LORA // P)
GAIN_COLS = CONV_AT + KT * 3

C_MASK = 0
C_CAUSAL = C_MASK + NB * CAUSAL
C_IDENT = C_CAUSAL + CAUSAL
C_FREQ = C_IDENT + P
C_SIGN = C_FREQ + 1
CONST_COLS = C_SIGN + 1


def build(nc, stream, x_in, gains_in, table_in, pos_in, const_in, onehot_in, negmask_in, toeplitz, out):
    with ExitStack() as ctx:
        ctx.enter_context(nc.allow_non_contiguous_dma("small constants"))
        place = [-(-nc.sbuf_base // 64) * 64]

        def at(name, shape, dt, offset):
            return nc.alloc_sbuf_tensor_at(name, shape, dt, offset=offset)

        def sb(name, shape, dt=F32):
            offset = place[0]
            place[0] += -(-int(np.prod(shape[1:])) * 4 // 32) * 32
            return at(name, shape, dt, offset)

        def sem(name):
            return nc.alloc_semaphore(name)

        raw = sb("raw", [P, RAW_SLOTS, CW])
        whi = sb("whi", [P, SPLIT_SLOTS, CW], F32R)
        wlo = sb("wlo", [P, SPLIT_SLOTS, CW], F32R)
        x = sb("x", [P, KT, SEQ])
        ahi = sb("ahi", [P, KT, SEQ], F32R)
        alo = sb("alo", [P, KT, SEQ], F32R)
        region = place[0]
        place[0] += NB * KT * SEQ * 4 * 3
        bhi = at("bhi", [P, HID_TILES, SEQ], F32R, region)
        blo = at("blo", [P, HID_TILES, SEQ], F32R, region + HID_TILES * SEQ * 4)
        one = KT * SEQ * 4
        qk1 = at("qk1", [P, 2 * KT, SEQ], F32, region)
        q1, k1 = qk1[:, 0:KT, :], qk1[:, KT:2 * KT, :]
        v1 = at("v1", [P, QT, D], F32, region + 2 * one)
        bias = at("bias", [P, HEADS, CAUSAL], F32, region + 3 * one)
        free1 = region + 3 * one + HEADS * CAUSAL * 4
        topmask = at("topmask", [P, CAUSAL], F32, free1)
        q_idx = at("q_idx", [P, 4, SEQ], F32, free1 + 2048)
        k_idx = at("k_idx", [P, SEQ], F32, free1 + 2048 + 4096)
        score = at("score", [P, CAUSAL], F32, free1 + 2048 + 4096 + 1024)
        relu_s = at("relu_s", [P, 2, CAUSAL], F32, free1 + 2048 + 4096 + 1024 + 2048)
        z_q = at("z_q", [P, 2, SEQ], F32, free1 + 13312)
        z_kv = at("z_kv", [P, 2, SEQ], F32, free1 + 13312 + 2048)
        masked_bias = at("masked_bias", [P, 4, CAUSAL], F32, free1 + 17408)
        q3 = at("q3", [P, NB * KT, SEQ], F32, region)
        k3 = at("k3", [P, NB * KT, SEQ], F32, region + NB * one)
        v3 = at("v3", [P, QT, QW], F32, region + 2 * NB * one)
        gated = at("gated", [P, KT, SEQ + 2], F32, region)
        conv = at("conv", [P, KT, SEQ], F32, region + KT * (SEQ + 2) * 4 + 64)
        chi = at("chi", [P, KT, SEQ], F32R, region + 3 * one)
        clo = at("clo", [P, KT, SEQ], F32R, region + 4 * one)
        shared = place[0]
        place[0] += 3 * 2 * NB * SEQ * 4 + 2 * SEQ * 4
        y = at("y", [P, KT, SEQ], F32, shared)
        a2hi = at("a2hi", [P, KT, SEQ], F32R, shared)
        a2lo = at("a2lo", [P, KT, SEQ], F32R, shared + one)
        q_pair = at("q_pair", [P, 2, NB, SEQ], F32, shared)
        k_pair = at("k_pair", [P, 2, NB, SEQ], F32, shared + 2 * NB * SEQ * 4)
        v_pair = at("v_pair", [P, 2, NB * QT, P], F32, shared + 4 * NB * SEQ * 4)
        o_pair = at("o_pair", [P, 2, QT * P], F32, shared + 6 * NB * SEQ * 4)
        logits3 = sb("logits3", [P, 2, NB * CAUSAL])
        logits = at("logits", [P, 4, CAUSAL], F32, place[0] - 2 * NB * CAUSAL * 4)
        pt = sb("pt", [P, NB, CAUSAL])
        z = at("z", [P, 2, SEQ], F32, place[0] - NB * CAUSAL * 4)
        zz = at("zz", [P, 2, SEQ], F32, place[0] - NB * CAUSAL * 4 + 2048)
        ssum = at("ssum", [P, 2, SEQ], F32, place[0] - 2 * NB * CAUSAL * 4)
        std = at("std", [P, 2, SEQ], F32, place[0] - 2 * NB * CAUSAL * 4 + 2048)
        sq = at("sq", [P, 4, SEQ], F32, place[0] - 3 * NB * CAUSAL * 4)
        masks3 = sb("masks3", [P, NB, CAUSAL])
        causal = sb("causal", [P, CAUSAL])
        consts = sb("consts", [P, CONST_COLS - C_IDENT])
        gains = sb("gains", [P, GAIN_COLS])
        rstd = sb("rstd", [P, 2, SEQ])
        rcol = sb("rcol", [P, QT])
        cos_r = sb("cos_r", [P, SEQ])
        sin_r = sb("sin_r", [P, SEQ])
        cos_t = sb("cos_t", [P, SEQ])
        sin_t = sb("sin_t", [P, SEQ])
        ones = sb("ones", [P, P])
        eps = sb("eps", [P, 1])
        w_idx = sb("w_idx", [P, QT, IDX_HEADS])
        neg_max = sb("neg_max", [P, 4, QT])
        row_sum = sb("row_sum", [P, 4, QT])
        inv_sum = sb("inv_sum", [P, 4, QT])
        best = sb("best", [P, QT, 8])
        assert place[0] <= nc.sbuf_usable_end, place[0] - nc.sbuf_usable_end
        onehot = at("onehot", [BUCKETS, CAUSAL], F32, shared)
        table = at("table", [BUCKETS, HEADS], F32, shared + 2048)
        negmask = at("negmask", [HEADS, CAUSAL], F32, shared + 4096)
        by_dist = at("by_dist", [HEADS, CAUSAL], F32, shared + 6144)
        pos_i = at("pos_i", [P, SEQ], I32, shared + 8192)
        angle = at("angle", [P, SEQ], F32, shared + 9216)
        turns = at("turns", [P, SEQ], F32, shared + 10240)
        shifted = at("shifted", [P, SEQ], F32, shared + 11264)
        ident = consts[:, 0:P]

        bank = nc.alloc_psum_tensor("bank", [P, 8, 512], F32)
        S_BANKS, PT_BANKS, O_BANKS = (0, 1, 2, 3), (4, 5), (6, 7)
        STAT = 7

        raw_landed = [sem(f"raw_landed{n}") for n in range(RAW_SLOTS)]
        hi_split = sem("hi_split")
        lo_split = sem("lo_split")
        chunk_used = sem("chunk_used")
        low_bank = sem("low_bank")
        bank_read = sem("bank_read")
        x_landed = sem("x_landed")
        const_landed = sem("const_landed")
        mask_landed = sem("mask_landed")
        table_landed = sem("table_landed")
        dist_stored = sem("dist_stored")
        bias_landed = sem("bias_landed")
        ones_set = sem("ones_set")
        dist_ready = sem("dist_ready")
        dist_done = sem("dist_done")
        act_hi = sem("act_hi")
        op_ready = sem("op_ready")
        squares = sem("squares")
        sums = sem("sums")
        totals = sem("totals")
        roots = sem("roots")
        rstd_ready = sem("rstd_ready")
        col_ready = sem("col_ready")
        rcol_ready = sem("rcol_ready")
        dve_step = sem("dve_step")
        act_step = sem("act_step")
        h_ready = sem("h_ready")
        e_ready = sem("e_ready")
        scaled = sem("scaled")
        y_ready = sem("y_ready")
        yhi_ready = sem("yhi_ready")
        gate_ready = sem("gate_ready")
        tap_ready = sem("tap_ready")
        conv_ready = sem("conv_ready")
        rot_ready = sem("rot_ready")
        rope_cos = sem("rope_cos")
        rope_sin = sem("rope_sin")
        angles = sem("angles")
        sines = sem("sines")
        x_ready = sem("x_ready")
        qk_staged = sem("qk_staged")
        v_staged = sem("v_staged")
        topped = sem("topped")
        topmask_ready = sem("topmask_ready")
        s_ready = sem("s_ready")
        l_ready = sem("l_ready")
        m_ready = sem("m_ready")
        p_ready = sem("p_ready")
        i_ready = sem("i_ready")
        t_ready = sem("t_ready")
        tc_ready = sem("tc_ready")
        o_ready = sem("o_ready")
        on_ready = sem("on_ready")
        ot_ready = sem("ot_ready")
        ohi_ready = sem("ohi_ready")
        idx_ready = sem("idx_ready")
        idx_relu = sem("idx_relu")
        idx_used = sem("idx_used")
        stored = sem("stored")

        def chunk_slot(stage, u):
            return (stage.base + u) % SPLIT_SLOTS

        def lin_bank(stage, local):
            return (stage.bank_base + local) % LIN_BANKS

        def local_bank(stage, i, u):
            return (i * 2 + u // 4) if stage.quartered else i * stage.unroll + u

        def static_bank(stage, u):
            return lin_bank(stage, u // 4 if stage.quartered else u)


        AHEAD = {False: 3, True: 2}

        def in_steps(eng, step, steps, first=8):
            for u in range(first):
                step(0, u)
            with eng.Fori(0, 2) as i:
                for u in range(first, first + 4):
                    step(i, u)
            for u in range(first + 8, steps):
                step(0, u)

        block = ctx.enter_context(nc.Block())

        @block.sync
        def _(sp):
            sp.dma_start(x[:, :, :], x_in).then_inc(x_landed, 16)
            for stage in STAGES:
                width = 6 * 2 * P if stage.contraction == HID2_TILES else CW

                def load(i, u, stage=stage, width=width):
                    g = stage.base + u
                    s = g % RAW_SLOTS
                    c = i * stage.unroll + stage.base + u
                    if g >= RAW_SLOTS:
                        sp.wait_ge(lo_split, i * stage.unroll + (g - RAW_SLOTS + 1))
                    sp.dma_start(raw[:, s, 0:width], stream[c, :, 0:width]).then_inc(raw_landed[s], 16)

                if stage.base == 0:
                    for u in range(4):
                        load(0, u)
                    for u in range(4, stage.chunks):
                        load(0, u)
                else:
                    in_loop(sp, stage, load)
            for j in range(KT // 2):
                sp.wait_ge(x_ready, 4 * (KT // 2) + j + 1)
                sp.dma_start(out[:, 2 * j:2 * j + 2, :], x[:, 2 * j:2 * j + 2, :]).then_inc(stored, 16)
            sp.wait_ge(stored, 16 * (KT // 2))

        @block.tensor
        def _(pe):
            n_stat = [0]
            n_sums = [0]

            def fmm(out_ap, stat, mov, first, last):
                return nc.tensor.matmul(out_ap, stat, mov, start=first, stop=last, skip_group_check=True)

            def features(b, slot, col, a_hi, a_lo, k0, nk, first, last, waits=None, together=1):
                for k in range(nk):
                    if waits is not None and k % together == 0:
                        pe.wait_ge(op_ready, waits + k // together + 1)
                    for n in range(2):
                        c = col(k, n)
                        o = bank[:, b, n * SEQ:(n + 1) * SEQ]
                        w_h, w_l = whi[:, slot, c:c + P], wlo[:, slot, c:c + P]
                        fmm(o, w_h, a_hi[:, k0 + k, :], first and k == 0 and n == 0, False)
                        fmm(o, w_h, a_lo[:, k0 + k, :], False, False)
                        ins = fmm(o, w_l, a_hi[:, k0 + k, :], False, last and k == nk - 1)
                return ins

            def tokens(b, slot, col, width, k0, nk, out_width=SEQ):
                for k in range(nk):
                    c = col(k)
                    for t in range(QT):
                        o = bank[:, b, t * out_width:t * out_width + width]
                        rows = slice(t * P, (t + 1) * P)
                        w_h, w_l = whi[:, slot, c:c + width], wlo[:, slot, c:c + width]
                        fmm(o, ahi[:, k0 + k, rows], w_h, k == 0 and t == 0, False)
                        fmm(o, alo[:, k0 + k, rows], w_h, False, False)
                        ins = fmm(o, ahi[:, k0 + k, rows], w_l, False, k == nk - 1)
                return ins

            def weights_ready(stage, i, u):
                pe.wait_ge(lo_split, i * stage.unroll + (stage.base + u + 1))

            def bank_free(stage, i, local):
                j = stage.bank_base + local
                if j >= LIN_BANKS:
                    per = 2 if stage.quartered else stage.unroll
                    pe.wait_ge(bank_read, i * per + (j - LIN_BANKS + 1))

            def product(stage, operand_base, operand=(ahi, alo), together=1, between=None):
                def step(i, u):
                    weights_ready(stage, i, u)
                    local = u // 4 if stage.quartered else u
                    if not stage.quartered or u % 4 == 0:
                        bank_free(stage, i, local)
                    b, slot = static_bank(stage, u), chunk_slot(stage, u)
                    if stage.quartered:
                        k0, nk = QUARTERS[stage.contraction][u % 4]
                        need = (k0 + nk) // 2 if stage.contraction == HID_TILES else k0 + nk
                        pe.wait_ge(op_ready, operand_base + need)
                        ins = features(b, slot, lambda k, n: (2 * k + n) * P, bhi, blo, k0, nk, u % 4 == 0,
                                       u % 4 == 3)
                    elif stage.kind == "token":
                        ins = tokens(b, slot, lambda k: 2 * k * P, 2 * P, 0, KT)
                    else:
                        ins = features(b, slot, lambda k, n: (2 * k + n) * P, *operand, 0, KT, True, True,
                                       waits=operand_base if u == 0 else None, together=together)
                    ins.then_inc(chunk_used, 1)
                if between is not None:
                    step(0, 0)
                    between()
                in_loop(pe, stage, step, first=0 if between is None else 1)

            def statistics():
                n_stat[0] += 1
                n_sums[0] += KT // 2 - 1
                pe.wait_ge(sums, n_sums[0])
                for t in range(2):
                    ins = nc.tensor.matmul(bank[:, STAT, 0:SEQ], ones[:, :], ssum[:, t, :], start=(t == 0), stop=(t == 1))
                ins.then_inc(totals, 1)

            def latent_statistics():
                n_stat[0] += 1
                n_sums[0] += 1
                pe.wait_ge(sums, n_sums[0])
                nc.tensor.matmul(bank[:, STAT, :], ones[:, :], ssum[:, :, :].rearrange("p a t -> p (a t)"),
                                 start=True, stop=True).then_inc(totals, 1)

            def columns(source):
                pe.wait_ge(rstd_ready, n_stat[0])
                for t in range(QT):
                    ins = nc.tensor.matmul(bank[:, STAT, t:t + 1], rstd[0:1, source, t * P:(t + 1) * P], ones[0:1, 0:1],
                                           start=(t == 0), stop=(t == 1), skip_group_check=True)
                ins.then_inc(col_ready, 1)

            def attention(run, branches):
                base, wide = HEADS * run, branches > 1
                ahead = AHEAD[wide]
                pairs = base // 2
                s_banks, pt_banks = ((0, 1, 2), (3, 4, 5)) if wide else (S_BANKS, PT_BANKS)

                def step(i, u):
                    h = u - ahead
                    if 0 <= h < HEADS:
                        pe.wait_ge(p_ready, i * 4 + (base + h + 1))
                        held = base + h if wide else base + h - 1
                        if held > 0:
                            pe.wait_ge(tc_ready, i * 4 + held)
                        for g in range(branches):
                            b = pt_banks[g] if wide else pt_banks[h % 2]
                            src = logits3[:, h % 2, g * CAUSAL:(g + 1) * CAUSAL] if wide else logits[:, h % 4, :]
                            for c in range(3):
                                cols = slice(c * P, (c + 1) * P)
                                ins = nc.tensor.transpose(bank[:, b, cols], src[:, cols], ident)
                        ins.then_inc(t_ready, 1)
                    if u < HEADS:
                        slot, odd = (u // 2) % 2, u % 2
                        rows = slice(odd * DH, odd * DH + DH)
                        if not odd:
                            pe.wait_ge(qk_staged, i * 4 + (2 * pairs + (u // 2 + 1) * 2))
                        need = base + u if wide else base + u + 1 - len(s_banks)
                        if need > 0:
                            pe.wait_ge(l_ready, i * 4 + need)
                        for g in range(branches):
                            b = s_banks[g] if wide else s_banks[u % 4]
                            nc.tensor.matmul(bank[:, b, 0:P], q_pair[rows, slot, g, 0:P], k_pair[rows, slot, g, 0:P],
                                             start=True, stop=True, skip_group_check=True)
                            ins = nc.tensor.matmul(bank[:, b, P:CAUSAL], q_pair[rows, slot, g, P:SEQ],
                                                   k_pair[rows, slot, g, :], start=True, stop=True, skip_group_check=True)
                        ins.then_inc(s_ready, 1)
                    if 0 <= h < HEADS:
                        b = O_BANKS[(h // 2) % 2]
                        odd = h % 2
                        pe.wait_ge(tc_ready, i * 4 + (base + h + 1))
                        if not odd:
                            pe.wait_ge(v_staged, i * 2 + (pairs + h // 2 + 1))
                        if not odd and h >= 4:
                            pe.wait_ge(op_ready, i * 2 + (OP_BEFORE[ATTENTION_FOR[run]] + h // 2 - 1))
                        for q in range(QT):
                            o = bank[:, b, q * P + odd * DH:q * P + odd * DH + DH]
                            terms = [(g, c) for g in range(branches) for c in range(q + 1)]
                            for n, (g, c) in enumerate(terms):
                                at_col = (q + c) * P
                                src = (pt[:, g, at_col:at_col + P] if wide else pt[:, h % 2, at_col:at_col + P])
                                v = v_pair[:, (h // 2) % 2, g * QT + c, odd * DH:odd * DH + DH]
                                ins = nc.tensor.matmul(o, src, v, start=(n == 0),
                                                       stop=(n == len(terms) - 1), skip_group_check=True)
                        ins.then_inc(o_ready, 1)
                    if h >= 2 and h % 2 == 0:
                        t = h // 2 - 1
                        pe.wait_ge(on_ready, i * 2 + (pairs + t + 1))
                        for q in range(QT):
                            ins = nc.tensor.transpose(bank[:, O_BANKS[t % 2], SEQ + q * P:SEQ + (q + 1) * P],
                                                      o_pair[:, t % 2, q * P:(q + 1) * P], ident)
                        ins.then_inc(ot_ready, 1)

                in_steps(pe, step, HEADS + ahead + 2)

            def bias_by_distance():
                pe.wait_ge(table_landed, 48)
                nc.tensor.matmul(bank[0:HEADS, 2, 0:CAUSAL], table[:, :], onehot[:, :], start=True, stop=True)\
                  .then_inc(dist_ready, 1)

            def low_rank():
                stage = BY_NAME["dsa_low"]
                j = 0
                for c in range(4):
                    weights_ready(stage, 0, c)
                    for pair in range(2 if c == 0 else 4):
                        if pair == 0 and c == 0:
                            pe.wait_ge(op_ready, OP_BEFORE["dsa_low"] + 4)
                        bank_free(stage, 0, j)
                        b, slot = lin_bank(stage, j), chunk_slot(stage, c)
                        if c == 3:
                            ins = tokens(b, slot, lambda k: k * 1024 + pair * 256, 256, 2, 2)
                        else:
                            ins = features(b, slot, lambda k, n: k * 1024 + pair * 256 + n * P, ahi, alo,
                                           2 if c == 2 else 0, 2, True, True)
                        last = pair == (1 if c == 0 else 3)
                        ins.then_inc(chunk_used if last else low_bank, 1)
                        j += 1
                    if c == 0:
                        columns(1)
                        index_scores()

            def index_scores():
                stage = BY_NAME["dsa_low"]
                pe.wait_ge(bank_read, stage.bank_base + 2)
                for h in range(IDX_HEADS):
                    rows = slice((h % 2) * DH, (h % 2) * DH + DH)
                    b = 2 + h % 4
                    if h >= 4:
                        pe.wait_ge(idx_relu, h - 3)
                    nc.tensor.matmul(bank[:, b, 0:P], q_idx[rows, h // 2, 0:P], k_idx[rows, 0:P],
                                     start=True, stop=True, skip_group_check=True)
                    nc.tensor.matmul(bank[:, b, P:CAUSAL], q_idx[rows, h // 2, P:SEQ], k_idx[rows, :],
                                     start=True, stop=True, skip_group_check=True).then_inc(idx_ready, 1)

            def dsa_in():
                stage = BY_NAME["dsa_in"]
                for c in range(2):
                    weights_ready(stage, 0, c)
                    bank_free(stage, 0, c)
                    features(lin_bank(stage, c), chunk_slot(stage, c), lambda k, n: (2 * k + n) * P, ahi, alo, 0, KT,
                             True, True, waits=OP_BEFORE["dsa_in"] if c == 0 else None).then_inc(chunk_used, 1)
                    if c == 0:
                        statistics()
                weights_ready(stage, 0, 2)
                bank_free(stage, 0, 2)
                slot, b = chunk_slot(stage, 2), lin_bank(stage, 2)
                for k in range(KT):
                    c = 2 * k * P
                    fmm(bank[:, b, 0:SEQ], whi[:, slot, c:c + P], ahi[:, k, :], k == 0, False)
                    fmm(bank[:, b, 0:SEQ], whi[:, slot, c:c + P], alo[:, k, :], False, False)
                    ins = fmm(bank[:, b, 0:SEQ], wlo[:, slot, c:c + P], ahi[:, k, :], False, k == KT - 1)
                ins.then_inc(low_bank, 1)
                columns(0)
                bank_free(stage, 0, 3)
                tokens(lin_bank(stage, 3), slot, lambda k: (2 * k + 1) * P, IDX_HEADS, 0, KT, IDX_HEADS)\
                    .then_inc(chunk_used, 1)

            def first_norm():
                pe.wait_ge(ones_set, 2)
                statistics()
                bias_by_distance()

            product(BY_NAME["moba_qk"], OP_BEFORE["moba_qk"], between=first_norm)
            columns(0)
            product(BY_NAME["moba_v"], 0)
            attention(0, 1)
            product(BY_NAME["moba_o"], OP_BEFORE["moba_o"])
            for n in range(2):
                if n == 1:
                    dsa_in()
                    latent_statistics()
                    low_rank()
                    attention(1, 1)
                    product(BY_NAME["dsa_o"], OP_BEFORE["dsa_o"])
                product(BY_NAME[f"up_{n}"], OP_BEFORE[f"up_{n}"], (a2hi, a2lo), between=statistics)
                product(BY_NAME[f"down_{n}"], OP_BEFORE[f"down_{n}"])
            statistics()
            product(BY_NAME["conv_ch"], OP_BEFORE["conv_ch"], between=statistics)
            product(BY_NAME["conv_b"], OP_BEFORE["conv_ch"])
            product(BY_NAME["conv_out"], OP_BEFORE["conv_out"], (chi, clo), together=2)
            statistics()
            for n in range(2):
                if n == 1:
                    product(BY_NAME["dil_k"], OP_BEFORE["dil_k"], between=statistics)
                    columns(0)
                    product(BY_NAME["dil_v"], 0)
                    product(BY_NAME["dil_q"], OP_BEFORE["dil_q"], (a2hi, a2lo))
                    attention(2, NB)
                    product(BY_NAME["dil_o"], OP_BEFORE["dil_o"])
                    statistics()
                product(BY_NAME[f"gate_up_{n}"], OP_BEFORE[f"gate_up_{n}"], between=statistics)
                product(BY_NAME[f"ffn_down_{n}"], OP_BEFORE[f"ffn_down_{n}"])
                statistics()

        @block.scalar
        def _(act):
            n_sq, n_sums, n_norm, n_x = [0], [0], [0], [0]

            def split(stage, i, u):
                g = stage.base + u + SPLIT_SLOTS
                if stage is STAGES[-1] and isinstance(i, int) and i * stage.unroll + g >= CHUNKS:
                    return
                per = stage.unroll // RAW_SLOTS
                s = g % RAW_SLOTS
                act.wait_ge(raw_landed[s], (i * per + (g // RAW_SLOTS + 1)) * 16)
                act.wait_ge(chunk_used, i * stage.unroll + (g - 1))
                nc.scalar.activation(whi[:, g % SPLIT_SLOTS, :], raw[:, s, :], ACT.Copy).then_inc(hi_split, 1)

            def first_split(g):
                act.wait_ge(raw_landed[g], 16)
                nc.scalar.activation(whi[:, g, :], raw[:, g, :], ACT.Copy).then_inc(hi_split, 1)

            def square(src, j):
                if j == 2:
                    act.wait_ge(sums, n_sums[0] + 1)
                nc.scalar.activation(sq[:, 2 * (j % 2):2 * (j % 2) + 2, :], src[:, 2 * j:2 * j + 2, :], ACT.Square)\
                  .then_inc(squares, 1)
                n_sq[0] += 1
                if j == KT // 2 - 1:
                    n_sums[0] += KT // 2 - 1

            def root(over, width=SEQ):
                n_norm[0] += 1
                act.wait_ge(totals, n_norm[0])
                nc.scalar.activation(std[:, :, :].rearrange("p a t -> p (a t)")[:, 0:width], bank[:, STAT, 0:width],
                                     ACT.Sqrt, bias=eps[:, 0:1], scale=1.0 / over).then_inc(roots, 1)

            def high_operand(dst, gain, j):
                for k in (2 * j, 2 * j + 1):
                    nc.scalar.activation(dst[:, k, :], x[:, k, :], ACT.Copy,
                                         scale=gains[:, gain + k:gain + k + 1]).then_inc(act_hi, 1)

            def norm_operand(gain):
                for j in range(KT // 2):
                    n_x[0] += 1
                    act.wait_ge(x_ready, n_x[0])
                    high_operand(ahi, GAIN_AT[gain], j)
                    square(x, j)
                root(D)

            def through(stage, step=None):
                def body(i, u):
                    split(stage, i, u)
                    if step is not None:
                        step(i, u)
                in_loop(act, stage, body)

            def through_into_norm(stage, pair):
                for u in range(stage.chunks):
                    last = u == stage.chunks - 1
                    if not last:
                        split(stage, 0, u)
                    if not stage.quartered or u % 4 == 3:
                        j = u // 4 if stage.quartered else u
                        act.wait_ge(bank_read, stage.bank_base + j + 1)
                        pair(j)
                    if last:
                        split(stage, 0, u)
                root(D)

            def into_operand(dst, gain):
                def pair(j):
                    high_operand(dst, GAIN_AT[gain], j)
                    square(x, j)
                return pair

            def scaled_for_norm(src, gain):
                def pair(j):
                    square(src, j)
                    if src is y:
                        act.wait_ge(squares, n_sq[0])
                    for k in (2 * j, 2 * j + 1):
                        g = GAIN_AT[gain] + k
                        ins = nc.scalar.activation(y[:, k, :], src[:, k, :], ACT.Copy, scale=gains[:, g:g + 1])
                    ins.then_inc(scaled, 1)
                return pair

            def relu_stage(stage):
                before = banks_before(stage, "relu", "swiglu")

                def step(i, u):
                    j = i * stage.unroll + u
                    act.wait_ge(bank_read, i * stage.unroll + (stage.bank_base + u + 1))
                    nc.scalar.activation(zz[:, :, :], z[:, :, :], ACT.Square).then_inc(e_ready, 1)
                    act.wait_ge(e_ready, i * stage.unroll + (before + u + 1))
                    nc.scalar.activation(bhi[:, bass.ds(j * 2, 2), :], zz[:, :, :], ACT.Copy).then_inc(h_ready, 1)
                through(stage, step)

            def swiglu_stage(stage):
                before = banks_before(stage, "relu", "swiglu")

                def step(i, u):
                    act.wait_ge(bank_read, i * stage.unroll + (stage.bank_base + u + 1))
                    nc.scalar.activation(zz[:, 0, :], z[:, 0, :], ACT.Silu).then_inc(h_ready, 1)
                through(stage, step)

            def rope_stage(stage):
                before = banks_before(stage, "rope")

                def step(i, u):
                    b = static_bank(stage, u)
                    act.wait_ge(rope_cos, i * stage.unroll + (before + u + 1))
                    act.wait_ge(bank_read, i * stage.unroll + (stage.bank_base + u))
                    for d in range(4):
                        s = d ^ 1
                        ins = nc.scalar.activation(zz[d * 32:(d + 1) * 32, :, :].rearrange("p a t -> p (a t)"),
                                                   bank[s * 32:(s + 1) * 32, b, :], ACT.Copy)
                    ins.then_inc(rot_ready, 1)
                through(stage, step)

            def attention(run, branches):
                base, wide = HEADS * run, branches > 1
                ahead = AHEAD[wide]

                def step(i, u):
                    h = u - ahead
                    if h >= 3 and h % 2 == 1:
                        t = (h - 3) // 2
                        act.wait_ge(ot_ready, i * 2 + (base // 2 + t + 1))
                        nc.scalar.activation(ahi[:, bass.ds(i * 2 + t, 1), :],
                                             bank[:, O_BANKS[t % 2]:O_BANKS[t % 2] + 1, SEQ:2 * SEQ], ACT.Copy)\
                          .then_inc(ohi_ready, 1)
                    if 0 <= h < HEADS:
                        act.wait_ge(t_ready, i * 4 + (base + h + 1))
                        held = base + h if wide else base + h - 1
                        if held > 0:
                            act.wait_ge(o_ready, i * 4 + held)
                        if wide:
                            ins = nc.scalar.activation(pt[:, :, :], bank[:, 3:6, 0:CAUSAL], ACT.Copy)
                        else:
                            ins = nc.scalar.activation(pt[:, h % 2, :], bank[:, PT_BANKS[h % 2], 0:CAUSAL], ACT.Copy)
                        ins.then_inc(tc_ready, 1)
                    if u < HEADS:
                        s = u % 4
                        act.wait_ge(m_ready, i * 4 + (base + u + 1))
                        if wide:
                            l = logits3[:, u % 2, :].rearrange("p (g c) -> p g c", g=NB)
                            first, second = l[:, :, 0:P], l[:, :, P:CAUSAL]
                        else:
                            first, second = logits[:, s, 0:P], logits[:, s, P:CAUSAL]
                        nc.scalar.activation(first, first, ACT.Exp, bias=neg_max[:, s, 0:1],
                                             accum_out=row_sum[:, s, 0:1])
                        nc.scalar.activation(second, second, ACT.Exp, bias=neg_max[:, s, 1:2],
                                             accum_out=row_sum[:, s, 1:2]).then_inc(p_ready, 1)

                in_steps(act, step, HEADS + ahead + 2)

            act.dma_start(pos_i[:, :], bass.AP(tensor=pos_in.tensor, offset=0, ap=[[0, P], [1, SEQ]]))\
               .then_inc(const_landed, 16)
            act.dma_start(consts[:, :], const_in[:, C_IDENT:CONST_COLS]).then_inc(const_landed, 16)
            act.dma_start(gains[:, :], gains_in).then_inc(const_landed, 16)
            act.dma_start(masks3[:, :, :], const_in[:, 0:C_CAUSAL].rearrange("p (g c) -> p g c", g=NB))\
               .then_inc(mask_landed, 16)
            act.dma_start(causal[:, :], const_in[:, C_CAUSAL:C_IDENT]).then_inc(mask_landed, 16)
            act.wait_ge(x_landed, 16)
            act.wait_ge(const_landed, 48)
            for j in range(KT // 2):
                high_operand(ahi, GAIN_AT["ln_attn_0"], j)
            first_split(0)
            for j in range(KT // 2):
                square(x, j)
            first_split(1)
            act.wait_ge(ones_set, 2)
            root(D)
            for n, dst in enumerate((sin_t, cos_t)):
                act.wait_ge(angles, n + 1)
                nc.scalar.activation(dst[:, :], angle[:, :] if n == 0 else shifted[:, :], ACT.Sin).then_inc(sines, 1)
            through(BY_NAME["moba_qk"])
            through(BY_NAME["moba_v"])
            attention(0, 1)
            through_into_norm(BY_NAME["moba_o"], into_operand(a2hi, "ln_mlp_0"))
            relu_stage(BY_NAME["up_0"])
            through_into_norm(BY_NAME["down_0"], into_operand(ahi, "ln_attn_1"))
            through(BY_NAME["dsa_in"])
            act.wait_ge(bank_read, BY_NAME["dsa_low"].bank_base)
            nc.scalar.activation(sq[:, 0:2, :], z_q[:, :, :], ACT.Square)
            nc.scalar.activation(sq[:, 2:4, :], z_kv[:, :, :], ACT.Square).then_inc(squares, 1)
            n_sq[0] += 1
            n_sums[0] += 1
            for k in range(2):
                for src, at_tile in ((z_q, 0), (z_kv, 2)):
                    g = LATENT_GAIN_AT + at_tile + k
                    nc.scalar.activation(ahi[:, at_tile + k, :], src[:, k, :], ACT.Copy,
                                         scale=gains[:, g:g + 1]).then_inc(act_hi, 1)
            root(LORA, 2 * SEQ)
            for u in range(4):
                split(BY_NAME["dsa_low"], 0, u)
                if u == 0:
                    for h in range(IDX_HEADS):
                        act.wait_ge(idx_ready, h + 1)
                        if h >= 2:
                            act.wait_ge(idx_used, h - 1)
                        nc.scalar.activation(relu_s[:, h % 2, :], bank[:, 2 + h % 4, 0:CAUSAL], ACT.Relu)\
                          .then_inc(idx_relu, 1)
            attention(1, 1)
            through_into_norm(BY_NAME["dsa_o"], into_operand(a2hi, "ln_mlp_1"))
            relu_stage(BY_NAME["up_1"])
            through_into_norm(BY_NAME["down_1"], scaled_for_norm(x, "final"))
            norm_operand("mix_pre_0")
            through(BY_NAME["conv_ch"])

            def gate_high(i, u):
                act.wait_ge(conv_ready, u + 1)
                nc.scalar.activation(chi[:, 2 * u:2 * u + 2, :], conv[:, 2 * u:2 * u + 2, :], ACT.Copy).then_inc(act_hi, 1)
            through(BY_NAME["conv_b"], gate_high)
            through_into_norm(BY_NAME["conv_out"], scaled_for_norm(y, "mix_post_0"))
            norm_operand("ffn_pre_0")
            swiglu_stage(BY_NAME["gate_up_0"])
            through_into_norm(BY_NAME["ffn_down_0"], scaled_for_norm(y, "ffn_post_0"))
            norm_operand("kv")
            rope_stage(BY_NAME["dil_k"])
            for j in range(KT // 2):
                high_operand(a2hi, GAIN_AT["mix_pre_1"], j)
            through(BY_NAME["dil_v"])
            rope_stage(BY_NAME["dil_q"])
            attention(2, NB)
            through_into_norm(BY_NAME["dil_o"], scaled_for_norm(y, "mix_post_1"))
            norm_operand("ffn_pre_1")
            swiglu_stage(BY_NAME["gate_up_1"])
            through_into_norm(BY_NAME["ffn_down_1"], scaled_for_norm(y, "ffn_post_1"))

        @block.gpsimd
        def _(pool):
            G = nc.gpsimd

            def store_bias():
                whole = by_dist[:, :]
                for lo, hi, offset in ((0, P, 2 * P - 1), (P, CAUSAL, P - 1)):
                    src = bass.AP(tensor=whole.tensor, offset=offset, ap=[list(whole.ap[0]), [-1, P], [1, hi - lo]])
                    pool.dma_start(toeplitz[:, :, lo:hi], src).then_inc(dist_stored, 16)

            def load_bias():
                pool.dma_start(bias[:, :, :], toeplitz.rearrange("h p c -> p h c")).then_inc(bias_landed, 16)

            def attention(run, branches, masked=False):
                base, wide = HEADS * run, branches > 1
                if wide:
                    q_of, k_of = (a[:, :, :].rearrange("p (g k) t -> p g k t", g=NB) for a in (q3, k3))
                else:
                    q_of, k_of = q1.unsqueeze(1), k1.unsqueeze(1)

                def stage_qk(i, t):
                    slot = t % 2
                    for src, dst in ((q_of, q_pair), (k_of, k_pair)):
                        G.tensor_copy(dst[:, slot, 0:branches, :].unsqueeze(2), src[:, :, bass.ds(i * 2 + t, 1), :])\
                         .then_inc(qk_staged, 1)

                def step(i, u):
                    if masked and u < HEADS:
                        if u >= 4:
                            pool.wait_ge(l_ready, i * 4 + (base + u - 3))
                        G.tensor_tensor(masked_bias[:, u % 4, :], bias[:, bass.ds(i * 4 + u, 1), :].squeeze(1),
                                        topmask[:, :], ALU.add).then_inc(topped, 1)
                    if u % 2 and u < HEADS - 1:
                        t = u // 2
                        if base + 2 * t > 0:
                            pool.wait_ge(s_ready, i * 4 + (base + 2 * t))
                        stage_qk(i, t + 1)

                stage_qk(0, 0)
                if masked:
                    pool.wait_ge(topmask_ready, 1)
                in_steps(pool, step, HEADS, first=4)

            pool.dma_start(table[:, :], table_in).then_inc(table_landed, 16)
            pool.dma_start(onehot[:, :], onehot_in).then_inc(table_landed, 16)
            pool.dma_start(negmask[:, :], negmask_in).then_inc(table_landed, 16)
            pool.wait_ge(dist_done, 1)
            store_bias()
            pool.wait_ge(dist_stored, 32)
            load_bias()
            pool.wait_ge(bank_read, BY_NAME["moba_o"].bank_base)
            attention(0, 1)
            pool.wait_ge(bank_read, BY_NAME["dsa_in"].bank_base)
            load_bias()
            pool.wait_ge(bias_landed, 32)
            pool.wait_ge(bank_read, BY_NAME["dsa_o"].bank_base)
            attention(1, 1, masked=True)
            pool.wait_ge(bank_read, BY_NAME["dil_o"].bank_base)
            attention(2, NB)

        @block.vector
        def _(dve):
            own = Own(dve, dve_step)
            n_sq, n_sums, n_norm, n_hi, n_x = [0], [0], [0], [0], [0]
            V = nc.vector

            def plain(ap):
                return ap.bitcast(F32)

            def split(stage, i, u):
                g = stage.base + u + SPLIT_SLOTS
                if stage is STAGES[-1] and isinstance(i, int) and i * stage.unroll + g >= CHUNKS:
                    return
                dve.wait_ge(hi_split, i * stage.unroll + (g + 1))
                s = g % SPLIT_SLOTS
                V.tensor_tensor(wlo[:, s, :], raw[:, g % RAW_SLOTS, :], plain(whi[:, s, :]), ALU.subtract)\
                 .then_inc(lo_split, 1)

            def first_split(g):
                dve.wait_ge(hi_split, g + 1)
                V.tensor_tensor(wlo[:, g, :], raw[:, g, :], plain(whi[:, g, :]), ALU.subtract).then_inc(lo_split, 1)

            def add_squares(j):
                if j == 0:
                    return
                if j == 1:
                    n_sq[0] += 1
                n_sq[0] += 1
                dve.wait_ge(squares, n_sq[0])
                if j == 1:
                    a = sq[:, 0:2, :]
                else:
                    dve.wait_ge(sums, n_sums[0])
                    a = ssum[:, :, :]
                V.tensor_tensor(ssum[:, :, :], a, sq[:, 2 * (j % 2):2 * (j % 2) + 2, :], ALU.add).then_inc(sums, 1)
                n_sums[0] += 1

            def inverse_root(width=SEQ):
                n_norm[0] += 1
                dve.wait_ge(roots, n_norm[0])
                V.reciprocal(rstd[:, :, :].rearrange("p a t -> p (a t)")[:, 0:width],
                             std[:, :, :].rearrange("p a t -> p (a t)")[:, 0:width]).then_inc(rstd_ready, 1)
                dve.wait_ge(rstd_ready, n_norm[0])

            def low_operand(hi, lo, gain, j):
                for k in (2 * j, 2 * j + 1):
                    n_hi[0] += 1
                    dve.wait_ge(act_hi, n_hi[0])
                    V.scalar_tensor_tensor(lo[:, k, :], x[:, k, :], gains[:, gain + k:gain + k + 1],
                                           plain(hi[:, k, :]), ALU.mult, ALU.subtract).then_inc(op_ready, 1)

            def token_scale(n):
                dve.wait_ge(col_ready, n)
                V.tensor_copy(rcol[:, :], bank[:, STAT, 0:QT]).then_inc(rcol_ready, 1)
                dve.wait_ge(rcol_ready, n)

            def both(ap):
                return ap.unsqueeze(1).to_broadcast([P, 2, SEQ])

            def through(stage, step, tail=None):
                def body(i, u):
                    done = not stage.quartered or u % 4 == 3
                    if done:
                        dve.wait_ge(chunk_used, i * stage.unroll + (stage.base + u + 1))
                        local = u // 4 if stage.quartered else u
                        per = 2 if stage.quartered else stage.unroll
                        b = bank[:, lin_bank(stage, local), :].rearrange("p (a t) -> p a t", a=2)
                        step(i, u, i * per + local, b)
                    split(stage, i, u)
                    if done and tail is not None:
                        tail(i, u, i * per + local, b)
                in_loop(dve, stage, body)

            def through_into_norm(stage, pair, tail):
                for u in range(stage.chunks):
                    done = not stage.quartered or u % 4 == 3
                    last = u == stage.chunks - 1
                    j = u // 4 if stage.quartered else u
                    if done:
                        dve.wait_ge(chunk_used, stage.base + u + 1)
                        pair(0, u, j, bank[:, lin_bank(stage, j), :].rearrange("p (a t) -> p a t", a=2))
                    if not last:
                        split(stage, 0, u)
                    if done:
                        tail(j)
                    if last:
                        split(stage, 0, u)
                inverse_root()

            def into_operand(hi, lo, gain):
                def tail(j):
                    low_operand(hi, lo, GAIN_AT[gain], j)
                    add_squares(j)
                return tail

            def scaled_into(dst):
                def step(i, u, j, b):
                    V.tensor_tensor(dst[:, bass.ds(j * 2, 2), :], b, both(rstd[:, 0, :]), ALU.mult).then_inc(bank_read, 1)
                return step

            def tokens_into(v, width):
                def step(i, u, j, b):
                    for t in range(QT):
                        ins = V.tensor_scalar(v[:, t, bass.ds(j * 256, 256)], b[:, t, :], rcol[:, t:t + 1], None, ALU.mult)
                    ins.then_inc(bank_read, 1)
                return step

            def residual(i, u, j, b):
                d = x[:, bass.ds(j * 2, 2), :]
                V.tensor_tensor(d, b, d, ALU.add).then_inc(bank_read, 1)

            def before_norm(i, u, j, b):
                V.tensor_copy(y[:, bass.ds(j * 2, 2), :], b).then_inc(bank_read, 1)

            def relu_stage(stage):
                before = banks_before(stage, "relu", "swiglu")

                def step(i, u, j, b):
                    V.scalar_tensor_tensor(z[:, :, :], b, 0.0, both(rstd[:, 0, :]), ALU.max, ALU.mult)\
                     .then_inc(bank_read, 1)

                def tail(i, u, j, b):
                    dve.wait_ge(h_ready, i * stage.unroll + (before + u + 1))
                    V.tensor_tensor(blo[:, bass.ds(j * 2, 2), :], zz[:, :, :], plain(bhi[:, bass.ds(j * 2, 2), :]),
                                    ALU.subtract).then_inc(op_ready, 1)
                return step, tail

            def swiglu_stage(stage):
                before = banks_before(stage, "relu", "swiglu")
                first = banks_before(stage, "swiglu")
                operands = OP_BEFORE[STAGES[stage.n + 1].name]

                def step(i, u, j, b):
                    dve.wait_ge(op_ready, i * stage.unroll + (operands + u))
                    V.tensor_tensor(z[:, :, :], b, both(rstd[:, 0, :]), ALU.mult).then_inc(bank_read, 1)

                def tail(i, u, j, b):
                    n = i * stage.unroll + (first + u + 1)
                    dve.wait_ge(h_ready, i * stage.unroll + (before + u + 1))
                    V.tensor_tensor(zz[:, 1:2, :], zz[:, 0:1, :], z[:, 1:2, :], ALU.mult).then_inc(y_ready, 1)
                    dve.wait_ge(y_ready, n)
                    V.tensor_copy(bhi[:, bass.ds(j, 1), :], zz[:, 1:2, :]).then_inc(yhi_ready, 1)
                    dve.wait_ge(yhi_ready, n)
                    V.tensor_tensor(blo[:, bass.ds(j, 1), :], zz[:, 1:2, :], plain(bhi[:, bass.ds(j, 1), :]),
                                    ALU.subtract).then_inc(op_ready, 1)
                return step, tail

            def rope_stage(stage, dst):
                before = banks_before(stage, "rope")

                def step(i, u, j, b):
                    dve.wait_ge(bank_read, i * stage.unroll + (stage.bank_base + u))
                    V.tensor_tensor(z[:, :, :], b, both(cos_r[:, :]), ALU.mult).then_inc(rope_cos, 1)

                def tail(i, u, j, b):
                    n = i * stage.unroll + (before + u + 1)
                    dve.wait_ge(rot_ready, n)
                    V.tensor_tensor(zz[:, :, :], zz[:, :, :], both(sin_r[:, :]), ALU.mult).then_inc(rope_sin, 1)
                    dve.wait_ge(rope_sin, n)
                    dve.wait_ge(rope_cos, n)
                    V.tensor_tensor(dst[:, bass.ds(j * 2, 2), :], z[:, :, :], zz[:, :, :], ALU.add).then_inc(bank_read, 1)
                return step, tail

            def attention(run, branches, masked=False):
                base, wide = HEADS * run, branches > 1
                ahead = AHEAD[wide]
                pairs = base // 2

                if wide:
                    v_of = v3[:, :, :].rearrange("p q (g n) -> p g q n", g=NB)
                else:
                    v_of = v1[:, :, :].unsqueeze(1)

                def stage_v(i, t):
                    dst = v_pair[:, t % 2, 0:branches * QT, :].rearrange("p (g q) n -> p g q n", q=QT)
                    V.tensor_copy(dst, v_of[:, :, :, bass.ds((i * 2 + t) * P, P)]).then_inc(v_staged, 1)

                for t in range(2):
                    stage_v(0, t)

                def step(i, u):
                    s = u % 4
                    if u < HEADS:
                        dve.wait_ge(s_ready, i * 4 + (base + u + 1))
                        if wide:
                            l = logits3[:, u % 2, :].rearrange("p (g c) -> p g c", g=NB)
                            V.scalar_tensor_tensor(l, bank[:, 0:3, 0:CAUSAL], SCALE, masks3[:, :, :],
                                                   ALU.mult, ALU.add).then_inc(l_ready, 1)
                            first, second, axes = l[:, :, 0:P], l[:, :, P:CAUSAL], AX.XY
                        else:
                            l = logits[:, s, :]
                            if masked:
                                dve.wait_ge(topped, i * 4 + (u + 1))
                                b = masked_bias[:, s, :]
                            else:
                                b = bias[:, bass.ds(i * 4 + u, 1), :].squeeze(1)
                            V.scalar_tensor_tensor(l, bank[:, S_BANKS[s], 0:CAUSAL], SCALE, b,
                                                   ALU.mult, ALU.add).then_inc(l_ready, 1)
                            first, second, axes = l[:, 0:P], l[:, P:CAUSAL], AX.X
                        dve.wait_ge(l_ready, i * 4 + (base + u + 1))
                        V.tensor_reduce(neg_max[:, s, 0:1], first, axes, ALU.max, negate=True)
                        V.tensor_reduce(neg_max[:, s, 1:2], second, axes, ALU.max, negate=True).then_inc(m_ready, 1)
                    if 1 <= u <= HEADS:
                        dve.wait_ge(p_ready, i * 4 + (base + u))
                        V.reciprocal(inv_sum[:, (u - 1) % 4, :], row_sum[:, (u - 1) % 4, :]).then_inc(i_ready, 1)
                    h = u - ahead
                    if h >= 3 and h % 2 == 1:
                        t = (h - 3) // 2
                        dve.wait_ge(ohi_ready, i * 2 + (pairs + t + 1))
                        V.tensor_tensor(alo[:, bass.ds(i * 2 + t, 1), :],
                                        bank[:, O_BANKS[t % 2]:O_BANKS[t % 2] + 1, SEQ:2 * SEQ],
                                        plain(ahi[:, bass.ds(i * 2 + t, 1), :]), ALU.subtract).then_inc(op_ready, 1)
                    if 1 <= h < HEADS and h % 2 == 1:
                        t = h // 2
                        dve.wait_ge(o_ready, i * 4 + (base + h + 1))
                        dve.wait_ge(i_ready, i * 4 + (base + h + 1))
                        if t >= 2:
                            dve.wait_ge(ot_ready, i * 2 + (pairs + t - 1))
                        inv = inv_sum[:, (h - 1) % 4:(h - 1) % 4 + 2, :].rearrange("p h q -> p q h")
                        V.tensor_tensor(o_pair[:, t % 2, :].rearrange("p (q h d) -> p q h d", q=QT, h=2),
                                        bank[:, O_BANKS[t % 2], 0:SEQ].rearrange("p (q h d) -> p q h d", q=QT, h=2),
                                        inv.unsqueeze(3).to_broadcast([P, QT, 2, DH]), ALU.mult).then_inc(on_ready, 1)
                        if h < HEADS - 4:
                            stage_v(i, t + 2)

                in_steps(dve, step, HEADS + ahead + 2, first=ahead + 5)

            def normed(j, add):
                n_x[0] += 1
                dve.wait_ge(scaled, n_x[0])
                tiles = slice(2 * j, 2 * j + 2)
                if add:
                    own.link(V.tensor_tensor(y[:, tiles, :], y[:, tiles, :], both(rstd[:, 0, :]), ALU.mult))
                    V.tensor_tensor(x[:, tiles, :], x[:, tiles, :], y[:, tiles, :], ALU.add).then_inc(x_ready, 1)
                else:
                    V.tensor_tensor(x[:, tiles, :], y[:, tiles, :], both(rstd[:, 0, :]), ALU.mult).then_inc(x_ready, 1)

            def normed_operand(gain, add=True):
                for j in range(KT // 2 + 1):
                    if j < KT // 2:
                        normed(j, add)
                    if j:
                        low_operand(ahi, alo, GAIN_AT[gain], j - 1)
                        add_squares(j - 1)
                inverse_root()

            def top_keys():
                own.link(V.tensor_tensor(score[:, :], score[:, :], causal[:, :], ALU.add))
                halves = ((0, slice(0, P)), (1, slice(P, CAUSAL)))
                for _ in range(TOPK // 8):
                    for t, cols in halves:
                        ins = V.max(best[:, t, :], score[:, cols])
                    own.link(ins)
                    for t, cols in halves:
                        ins = V.match_replace(score[:, cols], best[:, t, :], score[:, cols], TAKEN)
                    own.link(ins)
                V.tensor_scalar(topmask[:, :], score[:, :], TAKEN / 2, NEG, ALU.is_gt, ALU.mult).then_inc(topmask_ready, 1)

            V.memset(ones[:, :], 1.0).then_inc(ones_set, 1)
            V.memset(eps[:, :], EPS).then_inc(ones_set, 1)
            dve.wait_ge(const_landed, 48)
            own.link(V.tensor_copy(angle[:, :], pos_i[:, :]))
            own.link(V.tensor_scalar(angle[:, :], angle[:, :], consts[:, C_FREQ - C_IDENT:C_FREQ - C_IDENT + 1], None,
                                     ALU.mult))
            magic = 12582912.0
            own.link(V.tensor_scalar(turns[:, :], angle[:, :], 1.0 / (2 * np.pi), magic, ALU.mult, ALU.add))
            own.link(V.tensor_scalar(turns[:, :], turns[:, :], -magic, None, ALU.add))
            two_pi = 2 * np.pi
            part1 = 6.28125
            part2 = float(np.round((two_pi - part1) * 2 ** 21) / 2 ** 21)
            part3 = float(two_pi - part1 - part2)
            for part in (part1, part2, part3):
                own.link(V.scalar_tensor_tensor(angle[:, :], turns[:, :], -part, angle[:, :], ALU.mult, ALU.add))
            edge = 3.1415925
            own.link(V.tensor_scalar(shifted[:, :], angle[:, :], float(np.pi / 2), None, ALU.add))
            own.link(V.tensor_scalar(turns[:, :], shifted[:, :], float(np.pi), -two_pi, ALU.is_gt, ALU.mult))
            own.link(V.tensor_tensor(shifted[:, :], shifted[:, :], turns[:, :], ALU.add))
            V.tensor_scalar(angle[:, :], angle[:, :], -edge, edge, ALU.max, ALU.min).then_inc(angles, 1)
            V.tensor_scalar(shifted[:, :], shifted[:, :], -edge, edge, ALU.max, ALU.min).then_inc(angles, 1)
            dve.wait_ge(x_landed, 16)
            for j in range(KT // 2):
                low_operand(ahi, alo, GAIN_AT["ln_attn_0"], j)
            first_split(0)
            for j in range(KT // 2):
                add_squares(j)
            first_split(1)
            inverse_root()
            dve.wait_ge(dist_ready, 1)
            V.tensor_tensor(by_dist[:, :], bank[0:HEADS, 2, 0:CAUSAL], negmask[:, :], ALU.add).then_inc(dist_done, 1)
            through(BY_NAME["moba_qk"], scaled_into(qk1))
            dve.wait_ge(sines, 2)
            own.link(V.tensor_scalar(sin_t[:, :], sin_t[:, :], consts[:, C_SIGN - C_IDENT:C_SIGN - C_IDENT + 1], None,
                                     ALU.mult))
            token_scale(1)
            through(BY_NAME["moba_v"], tokens_into(v1, D))
            dve.wait_ge(bias_landed, 16)
            attention(0, 1)
            through_into_norm(BY_NAME["moba_o"], residual, into_operand(a2hi, a2lo, "ln_mlp_0"))
            for n in range(2):
                if n == 1:
                    stage = BY_NAME["dsa_in"]
                    for c in range(3):
                        if c < 2:
                            dve.wait_ge(chunk_used, stage.base + c + 1)
                            V.tensor_tensor((z_q, z_kv)[c][:, :, :],
                                            bank[:, lin_bank(stage, c), :].rearrange("p (a t) -> p a t", a=2),
                                            both(rstd[:, 0, :]), ALU.mult).then_inc(bank_read, 1)
                        else:
                            dve.wait_ge(low_bank, 1)
                            V.tensor_tensor(k_idx[:, :], bank[:, lin_bank(stage, 2), 0:SEQ], rstd[:, 0, :], ALU.mult)\
                             .then_inc(bank_read, 1)
                            token_scale(2)
                            dve.wait_ge(chunk_used, stage.base + 3)
                            for t in range(QT):
                                ins = V.tensor_scalar(w_idx[:, t, :],
                                                      bank[:, lin_bank(stage, 3), t * IDX_HEADS:(t + 1) * IDX_HEADS],
                                                      rcol[:, t:t + 1], IDX_SCALE, ALU.mult, ALU.mult)
                            ins.then_inc(bank_read, 1)
                        split(stage, 0, c)
                    n_sq[0] += 1
                    dve.wait_ge(squares, n_sq[0])
                    n_sums[0] += 1
                    V.tensor_tensor(ssum[:, :, :], sq[:, 0:4:2, :], sq[:, 1:4:2, :], ALU.add).then_inc(sums, 1)
                    for k in range(2):
                        for src, tile in ((z_q, 0), (z_kv, 2)):
                            g = LATENT_GAIN_AT + tile + k
                            n_hi[0] += 1
                            dve.wait_ge(act_hi, n_hi[0])
                            V.scalar_tensor_tensor(alo[:, tile + k, :], src[:, k, :], gains[:, g:g + 1],
                                                   plain(ahi[:, tile + k, :]), ALU.mult, ALU.subtract)\
                             .then_inc(op_ready, 1)
                    inverse_root(2 * SEQ)
                    stage = BY_NAME["dsa_low"]
                    j = 0
                    lows = 1
                    for c in range(4):
                        pairs = 2 if c == 0 else 4
                        for pair in range(pairs):
                            if pair == pairs - 1:
                                dve.wait_ge(chunk_used, stage.base + c + 1)
                            else:
                                lows += 1
                                dve.wait_ge(low_bank, lows)
                            b = bank[:, lin_bank(stage, j), :].rearrange("p (a t) -> p a t", a=2)
                            if c < 3:
                                dst = (q_idx, q1, k1)[c][:, 2 * pair:2 * pair + 2, :]
                                ins = V.tensor_tensor(dst, b, both(rstd[:, 1 if c == 2 else 0, :]), ALU.mult)
                            else:
                                for t in range(QT):
                                    ins = V.tensor_scalar(v1[:, t, pair * 256:(pair + 1) * 256], b[:, t, :],
                                                          rcol[:, t:t + 1], None, ALU.mult)
                            ins.then_inc(bank_read, 1)
                            j += 1
                        split(stage, 0, c)
                        if c == 0:
                            token_scale(3)
                            for h in range(IDX_HEADS):
                                dve.wait_ge(idx_relu, h + 1)
                                if h:
                                    dve.wait_ge(idx_used, h)
                                for t, cols in ((0, slice(0, P)), (1, slice(P, CAUSAL))):
                                    w = w_idx[:, t, h:h + 1]
                                    if h == 0:
                                        ins = V.tensor_scalar(score[:, cols], relu_s[:, 0, cols], w, None, ALU.mult)
                                    else:
                                        ins = V.scalar_tensor_tensor(score[:, cols], relu_s[:, h % 2, cols], w,
                                                                     score[:, cols], ALU.mult, ALU.add)
                                ins.then_inc(idx_used, 1)
                    dve.wait_ge(idx_used, IDX_HEADS)
                    dve.wait_ge(mask_landed, 32)
                    top_keys()
                    dve.wait_ge(bias_landed, 32)
                    attention(1, 1, masked=True)
                    through_into_norm(BY_NAME["dsa_o"], residual, into_operand(a2hi, a2lo, "ln_mlp_1"))
                through(BY_NAME[f"up_{n}"], *relu_stage(BY_NAME[f"up_{n}"]))
                through_into_norm(BY_NAME[f"down_{n}"], residual,
                                  into_operand(ahi, alo, "ln_attn_1") if n == 0 else add_squares)
            normed_operand("mix_pre_0", add=False)
            own.link(V.memset(gated[:, :, 0:2], 0.0))
            ch = BY_NAME["conv_ch"]

            def conv_step(i, u, j, b):
                V.tensor_tensor(z[:, :, :], b, both(rstd[:, 0, :]), ALU.mult).then_inc(bank_read, 1)
                dve.wait_ge(bank_read, i * ch.unroll + (ch.bank_base + u + 1))
                V.tensor_tensor(gated[:, bass.ds(j, 1), 2:2 + SEQ], z[:, 0:1, :], z[:, 1:2, :], ALU.mult)\
                 .then_inc(gate_ready, 1)

            def conv_tail(i, u, j, b):
                dve.wait_ge(gate_ready, i * ch.unroll + (u + 1))
                d = conv[:, bass.ds(j, 1), :]
                for tap in range(3):
                    w = gains[:, bass.ds(j * 3 + (CONV_AT + tap), 1)]
                    src = gated[:, bass.ds(j, 1), tap:tap + SEQ]
                    if tap == 0:
                        ins = V.tensor_scalar(d, src, w, None, ALU.mult)
                    else:
                        dve.wait_ge(tap_ready, i * (ch.unroll * 3) + (u * 3 + tap))
                        ins = V.scalar_tensor_tensor(d, src, w, d, ALU.mult, ALU.add)
                    ins.then_inc(tap_ready, 1)
            through(ch, conv_step, conv_tail)
            dve.wait_ge(tap_ready, 3 * KT)
            cb = BY_NAME["conv_b"]
            dve.wait_ge(chunk_used, cb.base)

            def gate_step(i, u, j, b):
                if u:
                    dve.wait_ge(conv_ready, u)
                V.tensor_tensor(z[:, :, :], b, both(rstd[:, 0, :]), ALU.mult).then_inc(bank_read, 1)
                dve.wait_ge(bank_read, i * cb.unroll + (cb.bank_base + u + 1))
                d = conv[:, bass.ds(j * 2, 2), :]
                V.tensor_tensor(d, z[:, :, :], d, ALU.mult).then_inc(conv_ready, 1)

            def gate_tail(i, u, j, b):
                n_hi[0] += 1
                dve.wait_ge(act_hi, n_hi[0])
                V.tensor_tensor(clo[:, 2 * u:2 * u + 2, :], conv[:, 2 * u:2 * u + 2, :],
                                plain(chi[:, 2 * u:2 * u + 2, :]), ALU.subtract).then_inc(op_ready, 1)
            through(cb, gate_step, gate_tail)
            through_into_norm(BY_NAME["conv_out"], before_norm, add_squares)
            normed_operand("ffn_pre_0")
            for n in range(2):
                if n == 1:
                    V.tensor_tensor(cos_r[:, :], cos_t[:, :], rstd[:, 0, :], ALU.mult)
                    own.link(V.tensor_tensor(sin_r[:, :], sin_t[:, :], rstd[:, 0, :], ALU.mult))
                    through(BY_NAME["dil_k"], *rope_stage(BY_NAME["dil_k"], k3))
                    token_scale(4)
                    for j in range(KT // 2):
                        low_operand(a2hi, a2lo, GAIN_AT["mix_pre_1"], j)
                    through(BY_NAME["dil_v"], tokens_into(v3, QW))
                    through(BY_NAME["dil_q"], *rope_stage(BY_NAME["dil_q"], q3))
                    attention(2, NB)
                    through_into_norm(BY_NAME["dil_o"], before_norm, add_squares)
                    normed_operand("ffn_pre_1")
                gu, down = BY_NAME[f"gate_up_{n}"], BY_NAME[f"ffn_down_{n}"]
                through(gu, *swiglu_stage(gu))
                through_into_norm(down, before_norm, add_squares)
                if n == 0:
                    normed_operand("kv")
            for j in range(KT // 2):
                normed(j, True)


def buckets():
    n = np.arange(SEQ)
    exact = BUCKETS // 2
    large = np.log(np.maximum(n, 1).astype(np.float32) / np.float32(exact)) / np.float32(np.log(MAX_DISTANCE / exact))
    large = exact + (large * np.float32(BUCKETS - exact)).astype(np.int32)
    return np.where(n < exact, n, np.minimum(large, BUCKETS - 1))


def shape_constants():
    consts = np.zeros((P, CONST_COLS), np.float32)
    q = np.arange(P)[:, None]
    j = np.arange(CAUSAL)[None, :]
    dist = np.where(j < P, q - j, P + q - (j - P))
    for g, (window, dilation) in enumerate(BRANCHES):
        seen = (dist >= 0) & (dist <= window) & (dist % dilation == 0)
        consts[:, C_MASK + g * CAUSAL:C_MASK + (g + 1) * CAUSAL] = np.where(seen, 0.0, NEG)
    consts[:, C_CAUSAL:C_IDENT] = np.where(dist >= 0, 0.0, NEG)
    consts[:, C_IDENT:C_IDENT + P] = np.eye(P)
    half = DH // 2
    freq = (10000.0 ** (-np.arange(half, dtype=np.float32).astype(np.float64) / half)).astype(np.float32)
    consts[:, C_FREQ] = np.tile(freq, P // half)
    consts[:, C_SIGN] = np.where(np.arange(P) % DH < half, -1.0, 1.0)
    at_dist = 2 * P - 1 - np.arange(CAUSAL)
    b = buckets()
    onehot = np.zeros((BUCKETS, CAUSAL), np.float32)
    for u in range(CAUSAL):
        if at_dist[u] >= 0:
            onehot[b[at_dist[u]], u] = 1.0
    negmask = np.broadcast_to(np.where(at_dist >= 0, 0.0, NEG).astype(np.float32), (HEADS, CAUSAL))
    return consts, onehot, np.ascontiguousarray(negmask)


def packed(inp):
    stream = np.zeros((CHUNKS, P, CW), np.float32)
    at = [0]

    def put(tiles):
        k, _, n = tiles.shape
        stream[at[0], :, :k * n] = tiles.transpose(1, 0, 2).reshape(P, k * n)
        at[0] += 1

    def by_pairs(w, starts):
        w = w.reshape(-1, P, w.shape[1])
        for a, b in starts:
            put(np.concatenate([w[:, :, a:a + P], w[:, :, b:b + P]], axis=2))

    def across(w, lo, hi):
        by_pairs(w, [(c, c + P) for c in range(lo, hi, 2 * P)])

    def quartered(w, tiles):
        for c in range(0, D, 2 * P):
            for k0, nk in QUARTERS[tiles]:
                by_pairs(w[k0 * P:(k0 + nk) * P], [(c, c + P)])

    def low(w):
        w = w.reshape(2, P, -1)
        put(np.concatenate([w, np.zeros((2, P, 1024 - w.shape[2]), np.float32)], axis=2))

    across(inp["moba_w_qkv"][0], 0, 3 * D)
    across(inp["moba_w_o"][0], 0, D)
    for n in range(2):
        if n == 1:
            w = inp["dsa_w_in"][0]
            across(w, 0, 2 * LORA)
            keys, weights = w[:, 2 * LORA:2 * LORA + DH], w[:, 2 * LORA + DH:]
            tail = np.concatenate([keys, keys, weights, np.zeros((D, P - IDX_HEADS), np.float32)], axis=1)
            across(tail, 0, 2 * P)
            low(inp["dsa_w_qi"][0])
            low(inp["dsa_w_uq"][0])
            low(inp["dsa_w_uk"][0].transpose(2, 0, 1).reshape(LORA, HEADS * DH))
            low(inp["dsa_w_uv"][0].transpose(1, 0, 2).reshape(LORA, HEADS * DH))
            across(inp["dsa_w_o"][0], 0, D)
        across(inp["mlp_w_up"][n], 0, FF)
        quartered(inp["mlp_w_down"][n], HID_TILES)
    by_pairs(inp["conv_w_in_2"][0], [(D + c, 2 * D + c) for c in range(0, D, P)])
    across(inp["conv_w_in_2"][0], 0, D)
    across(inp["conv_w_out_2"][0], 0, D)
    for n in range(2):
        if n == 1:
            across(inp["w_kv_2"], 0, 2 * QW)
            across(inp["w_q_2"][0], 0, QW)
            across(inp["w_o_2"][0], 0, D)
        by_pairs(inp["ffn_w_gate_up_2"][n], [(c, FF2 + c) for c in range(0, FF2, P)])
        quartered(inp["ffn_w_down_2"][n], HID2_TILES)
    assert at[0] == CHUNKS
    return stream


def packed_gains(inp):
    rows = {"ln_attn_0": inp["ln_attn"][0], "ln_attn_1": inp["ln_attn"][1], "ln_mlp_0": inp["ln_mlp"][0],
            "ln_mlp_1": inp["ln_mlp"][1], "final": inp["final_norm"], "kv": inp["kv_norm_2"]}
    for n in range(2):
        rows[f"mix_pre_{n}"] = inp["mix_norm_pre_2"][n]
        rows[f"mix_post_{n}"] = inp["mix_norm_post_2"][n]
        rows[f"ffn_pre_{n}"] = inp["ffn_norm_pre_2"][n]
        rows[f"ffn_post_{n}"] = inp["ffn_norm_post_2"][n]
    cols = [rows[g].reshape(-1, P).T for g in GAINS]
    cols += [inp["dsa_g_q"][0].reshape(-1, P).T, inp["dsa_g_kv"][0].reshape(-1, P).T]
    cols += [inp["conv_w_2"][0].reshape(3, KT, P).transpose(2, 1, 0).reshape(P, KT * 3)]
    return np.ascontiguousarray(np.concatenate(cols, axis=1))


def kernel(**inputs):
    import concourse.bacc as bacc
    from concourse.bass_utils import run_bass_kernel_spmd

    inp = {name: np.asarray(a) for name, a in inputs.items()}
    consts, onehot, negmask = shape_constants()
    arrays = {
        "weight_stream": packed(inp),
        "x_features": np.ascontiguousarray(inp["x"][0].T.reshape(KT, P, SEQ).transpose(1, 0, 2)),
        "gain_columns": packed_gains(inp),
        "bias_table": np.ascontiguousarray(inp["rel_bias"]),
        "token_positions": np.ascontiguousarray(inp["positions_2"]),
        "shape_consts": consts,
        "bucket_onehot": onehot,
        "ahead_mask": negmask,
    }
    nc = bacc.Bacc("TRN2", target_bir_lowering=False, num_devices=1)
    args = [nc.dram_tensor(name, a.shape, mybir.dt.from_np(a.dtype), kind="ExternalInput").ap()
            for name, a in arrays.items()]
    toeplitz = nc.dram_tensor("bias_by_head", (HEADS, P, CAUSAL), F32).ap()
    out = nc.dram_tensor("out_features", (P, KT, SEQ), F32, kind="ExternalOutput").ap()
    build(nc, *args, toeplitz, out)
    r = run_bass_kernel_spmd(nc, [arrays], core_ids=[0])
    got = r.results[0]["out_features"]
    return np.ascontiguousarray(got.transpose(1, 0, 2).reshape(D, SEQ).T)[None]
```

```python
from contextlib import ExitStack

import numpy as np

import concourse.bass as bass
from concourse import mybir

F32 = mybir.dt.float32
F32R = mybir.dt.float32r
I32 = mybir.dt.int32
ALU = mybir.AluOpType
ACT = mybir.ActivationFunctionType
AX = mybir.AxisListType

P = 128
SEQ = 256
QT = SEQ // P
D = 1024
KT = D // P
HEADS = 16
DH = 64
FF = 4096
FF2 = 2816
HID_TILES = FF // P
HID2_TILES = FF2 // P
BUCKETS = 32
MAX_DISTANCE = 128
IDX_HEADS = 8
LORA = 256
TOPK = 64
BRANCHES = ((128, 1), (512, 4), (2048, 16))
NB = len(BRANCHES)
QW = NB * HEADS * DH
EPS = 1e-6
NEG = -1e30
TAKEN = -3e38
SCALE = DH ** -0.5
IDX_SCALE = IDX_HEADS ** -0.5 * DH ** -0.5
CAUSAL = P + SEQ

CW = 2048
RAW_SLOTS = 4
SPLIT_SLOTS = 2
LIN_BANKS = 2

QUARTERS = {HID_TILES: ((0, 8), (8, 8), (16, 8), (24, 8)), HID2_TILES: ((0, 6), (6, 6), (12, 5), (17, 5))}

HID2_WIDTH = max(n for _, n in QUARTERS[HID2_TILES]) * 2 * P


class Stage:

    def __init__(self, name, kind, chunks, banks, contraction=KT):
        self.name, self.kind, self.chunks, self.banks, self.contraction = name, kind, chunks, banks, contraction
        self.quartered = contraction != KT
        self.unroll = 8 if self.quartered else 4


STAGES = [
    Stage("moba_qk", "scale", 8, 8),
    Stage("moba_v", "token", 4, 4),
    Stage("moba_o", "residual", 4, 4),
    Stage("up_0", "relu", 16, 16),
    Stage("down_0", "residual", 16, 4, HID_TILES),
    Stage("dsa_in", "dsa_in", 3, 4),
    Stage("dsa_low", "dsa_low", 4, 14),
    Stage("dsa_o", "residual", 4, 4),
    Stage("up_1", "relu", 16, 16),
    Stage("down_1", "residual", 16, 4, HID_TILES),
    Stage("conv_ch", "conv", 8, 8),
    Stage("conv_b", "gate", 4, 4),
    Stage("conv_out", "post", 4, 4),
    Stage("gate_up_0", "swiglu", 22, 22),
    Stage("ffn_down_0", "post", 16, 4, HID2_TILES),
    Stage("dil_k", "rope", 12, 12),
    Stage("dil_q", "rope", 12, 12),
    Stage("dil_v", "token", 12, 12),
    Stage("dil_o", "post", 4, 4),
    Stage("gate_up_1", "swiglu", 22, 22),
    Stage("ffn_down_1", "post", 16, 4, HID2_TILES),
]
CHUNKS = 0
_banks = 0
for _n, _s in enumerate(STAGES):
    _s.n, _s.base, _s.bank_base = _n, CHUNKS, _banks
    CHUNKS += _s.chunks
    _banks += _s.banks
BY_NAME = {s.name: s for s in STAGES}


OPERANDS = [("moba_qk", KT), ("moba_o", KT), ("up_0", KT), ("down_0", FF // 256), ("dsa_in", KT), ("dsa_low", 4),
            ("dsa_o", KT), ("up_1", KT), ("down_1", FF // 256), ("conv_ch", KT), ("conv_out", KT // 2), ("gate_up_0", KT),
            ("ffn_down_0", HID2_TILES), ("dil_k", KT), ("dil_q", KT), ("dil_o", KT), ("gate_up_1", KT),
            ("ffn_down_1", HID2_TILES)]
OP_BEFORE = {name: sum(n for _, n in OPERANDS[:m]) for m, (name, _) in enumerate(OPERANDS)}
ATTENTION_FOR = ["moba_o", "dsa_o", "dil_o"]


def banks_before(stage, *kinds):
    return sum(s.banks for s in STAGES[:stage.n] if s.kind in kinds)


def in_loop(eng, stage, step, first=0, peeled=False):
    looped = (stage.chunks - first) // stage.unroll - (peeled or stage is STAGES[-1])
    if looped > 1:
        with eng.Fori(0, looped) as i:
            for u in range(first, first + stage.unroll):
                step(i, u)
    else:
        looped = 0
    for c in range(first + looped * stage.unroll, stage.chunks):
        step(0, c)


class Own:

    def __init__(self, eng, sem):
        self.eng, self.sem, self.n = eng, sem, 0

    def count(self, ins):
        self.n += 1
        ins.then_inc(self.sem, 1)
        return self.n

    def link(self, ins):
        self.eng.wait_ge(self.sem, self.count(ins))


GAINS = ["ln_attn_0", "ln_mlp_0", "ln_attn_1", "ln_mlp_1", "final", "mix_pre_0", "mix_post_0", "ffn_pre_0",
         "ffn_post_0", "kv", "mix_pre_1", "mix_post_1", "ffn_pre_1", "ffn_post_1"]
GAIN_AT = {g: KT * n for n, g in enumerate(GAINS)}
LATENT_GAIN_AT = KT * len(GAINS)
CONV_AT = LATENT_GAIN_AT + 2 * (LORA // P)
GAIN_COLS = CONV_AT + KT * 3

C_MASK = 0
C_CAUSAL = C_MASK + NB * CAUSAL
C_IDENT = C_CAUSAL + CAUSAL
C_FREQ = C_IDENT + P
C_SIGN = C_FREQ + 1
CONST_COLS = C_SIGN + 1


def build(nc, stream, x_in, gains_in, table_in, pos_in, const_in, onehot_in, negmask_in, toeplitz, out):
    with ExitStack() as ctx:
        ctx.enter_context(nc.allow_non_contiguous_dma("small constants"))
        place = [-(-nc.sbuf_base // 64) * 64]

        def at(name, shape, dt, offset):
            return nc.alloc_sbuf_tensor_at(name, shape, dt, offset=offset)

        def sb(name, shape, dt=F32):
            offset = place[0]
            place[0] += -(-int(np.prod(shape[1:])) * 4 // 32) * 32
            return at(name, shape, dt, offset)

        def sem(name):
            return nc.alloc_semaphore(name)

        raw = sb("raw", [P, RAW_SLOTS, CW])
        whi = sb("whi", [P, SPLIT_SLOTS, CW], F32R)
        wlo = sb("wlo", [P, SPLIT_SLOTS, CW], F32R)
        x = sb("x", [P, KT, SEQ])
        ahi = sb("ahi", [P, KT, SEQ], F32R)
        alo = sb("alo", [P, KT, SEQ], F32R)
        region = place[0]
        place[0] += NB * KT * SEQ * 4 * 3
        bhi = at("bhi", [P, HID_TILES, SEQ], F32R, region)
        blo = at("blo", [P, HID_TILES, SEQ], F32R, region + HID_TILES * SEQ * 4)
        one = KT * SEQ * 4
        qk1 = at("qk1", [P, 2 * KT, SEQ], F32, region)
        q1, k1 = qk1[:, 0:KT, :], qk1[:, KT:2 * KT, :]
        v1 = at("v1", [P, QT, D], F32, region + 2 * one)
        bias = at("bias", [P, HEADS, CAUSAL], F32, region + 3 * one)
        free1 = region + 3 * one + HEADS * CAUSAL * 4
        topmask = at("topmask", [P, CAUSAL], F32, free1)
        q_idx = at("q_idx", [P, 4, SEQ], F32, free1 + 2048)
        k_idx = at("k_idx", [P, SEQ], F32, free1 + 2048 + 4096)
        score = at("score", [P, CAUSAL], F32, free1 + 2048 + 4096 + 1024)
        w_rows = at("w_rows", [IDX_HEADS, SEQ], F32, free1 + 2048 + 4096 + 1024 + 2048)
        z_q = at("z_q", [P, 2, SEQ], F32, free1 + 13312)
        z_kv = at("z_kv", [P, 2, SEQ], F32, free1 + 13312 + 2048)
        masked_bias = at("masked_bias", [P, 4, CAUSAL], F32, free1 + 17408)
        q3 = at("q3", [P, NB * KT, SEQ], F32, region)
        k3 = at("k3", [P, NB * KT, SEQ], F32, region + NB * one)
        v3 = at("v3", [P, QT, QW], F32, region + 2 * NB * one)
        gated = at("gated", [P, KT, SEQ + 2], F32, region)
        conv = at("conv", [P, KT, SEQ], F32, region + KT * (SEQ + 2) * 4 + 64)
        chi = at("chi", [P, KT, SEQ], F32R, region + 3 * one)
        clo = at("clo", [P, KT, SEQ], F32R, region + 4 * one)
        shared = place[0]
        place[0] += 3 * 2 * NB * SEQ * 4 + 2 * SEQ * 4
        y = at("y", [P, KT, SEQ], F32, shared)
        a2hi = at("a2hi", [P, KT, SEQ], F32R, shared)
        a2lo = at("a2lo", [P, KT, SEQ], F32R, shared + one)
        q_pair = at("q_pair", [P, 2, NB, SEQ], F32, shared)
        k_pair = at("k_pair", [P, 2, NB, SEQ], F32, shared + 2 * NB * SEQ * 4)
        v_pair = at("v_pair", [P, 2, NB * QT, P], F32, shared + 4 * NB * SEQ * 4)
        relu_s = at("relu_s", [P, IDX_HEADS, CAUSAL], F32, shared)
        o_pair = at("o_pair", [P, 2, QT * P], F32, shared + 6 * NB * SEQ * 4)
        logits3 = sb("logits3", [P, 2, NB * CAUSAL])
        logits = at("logits", [P, 4, CAUSAL], F32, place[0] - 2 * NB * CAUSAL * 4)
        pt = sb("pt", [P, NB, CAUSAL])
        z = at("z", [P, 2, SEQ], F32, place[0] - NB * CAUSAL * 4)
        zz = at("zz", [P, 2, SEQ], F32, place[0] - NB * CAUSAL * 4 + 2048)
        ssum = at("ssum", [P, 2, SEQ], F32, place[0] - 2 * NB * CAUSAL * 4)
        std = at("std", [P, 2, SEQ], F32, place[0] - 2 * NB * CAUSAL * 4 + 2048)
        sq = at("sq", [P, 4, SEQ], F32, place[0] - 3 * NB * CAUSAL * 4)
        masks3 = sb("masks3", [P, NB, CAUSAL])
        causal = sb("causal", [P, CAUSAL])
        consts = sb("consts", [P, CONST_COLS - C_IDENT])
        gains = sb("gains", [P, GAIN_COLS])
        rstd = sb("rstd", [P, 2, SEQ])
        root_col = sb("root_col", [P, QT])
        scratch = sb("scratch", [P, 1])
        rcol = sb("rcol", [P, QT])
        cos_r = sb("cos_r", [P, SEQ])
        sin_r = sb("sin_r", [P, SEQ])
        cos_t = sb("cos_t", [P, SEQ])
        sin_t = sb("sin_t", [P, SEQ])
        ones = sb("ones", [P, P])
        eps = sb("eps", [P, 1])
        w_idx = sb("w_idx", [P, QT, IDX_HEADS])
        neg_max = sb("neg_max", [P, 4, QT])
        row_sum = sb("row_sum", [P, 4, QT])
        inv_sum = sb("inv_sum", [P, 4, QT])
        best = sb("best", [P, QT, 8])
        assert place[0] <= nc.sbuf_usable_end, place[0] - nc.sbuf_usable_end
        onehot = at("onehot", [BUCKETS, CAUSAL], F32, shared)
        table = at("table", [BUCKETS, HEADS], F32, shared + 2048)
        negmask = at("negmask", [HEADS, CAUSAL], F32, shared + 4096)
        by_dist = at("by_dist", [HEADS, CAUSAL], F32, shared + 6144)
        pos_i = at("pos_i", [P, SEQ], I32, shared + 8192)
        angle = at("angle", [P, SEQ], F32, shared + 9216)
        turns = at("turns", [P, SEQ], F32, shared + 10240)
        shifted = at("shifted", [P, SEQ], F32, shared + 11264)
        ident = consts[:, 0:P]

        bank = nc.alloc_psum_tensor("bank", [P, 8, 512], F32)
        S_BANKS, PT_BANKS, O_BANKS = (2, 3, 0, 1), (4, 5), (6, 7)
        IDX_BANKS = (2, 3, 4, 5, 7)
        STAT = 7

        raw_landed = [sem(f"raw_landed{n}") for n in range(RAW_SLOTS)]
        half_landed = sem("half_landed")
        half_hi = sem("half_hi")
        half_lo = sem("half_lo")
        hi_split = sem("hi_split")
        lo_split = sem("lo_split")
        chunk_used = sem("chunk_used")
        low_bank = sem("low_bank")
        bank_read = sem("bank_read")
        gains_landed = sem("gains_landed")
        x_landed = [sem(f"x_landed{half}") for half in range(2)]
        const_landed = sem("const_landed")
        mask_landed = sem("mask_landed")
        table_landed = sem("table_landed")
        dist_stored = sem("dist_stored")
        bias_landed = sem("bias_landed")
        ones_set = sem("ones_set")
        dist_ready = sem("dist_ready")
        dist_done = sem("dist_done")
        act_hi = sem("act_hi")
        op_ready = sem("op_ready")
        squares = sem("squares")
        sums = sem("sums")
        totals = sem("totals")
        roots = sem("roots")
        inverse_col = sem("inverse_col")
        spread = sem("spread")
        rstd_ready = sem("rstd_ready")
        col_ready = sem("col_ready")
        rcol_ready = sem("rcol_ready")
        dve_step = sem("dve_step")
        h_ready = sem("h_ready")
        relu_squared = sem("relu_squared")
        scaled = sem("scaled")
        y_ready = sem("y_ready")
        yhi_ready = sem("yhi_ready")
        gate_ready = sem("gate_ready")
        tap_ready = sem("tap_ready")
        conv_ready = sem("conv_ready")
        rope_cos = sem("rope_cos")
        rope_sin = sem("rope_sin")
        roped = sem("roped")
        angles = sem("angles")
        sines = sem("sines")
        x_ready = sem("x_ready")
        qk_staged = sem("qk_staged")
        first_q = sem("first_q")
        first_k = sem("first_k")
        v_staged = sem("v_staged")
        topped = sem("topped")
        topmask_ready = sem("topmask_ready")
        s_ready = sem("s_ready")
        l_ready = sem("l_ready")
        m_ready = sem("m_ready")
        p_ready = sem("p_ready")
        i_ready = sem("i_ready")
        t_ready = sem("t_ready")
        tc_ready = sem("tc_ready")
        o_ready = sem("o_ready")
        on_ready = sem("on_ready")
        ot_ready = sem("ot_ready")
        ohi_ready = sem("ohi_ready")
        latent_ready = sem("latent_ready")
        w_turned = sem("w_turned")
        idx_ready = sem("idx_ready")
        idx_relu = sem("idx_relu")
        idx_used = sem("idx_used")
        stored = sem("stored")

        def chunk_slot(stage, u):
            return (stage.base + u) % SPLIT_SLOTS

        def split_width(stage, u):
            after = [s for s in STAGES if s.base <= stage.base + u + SPLIT_SLOTS][-1]
            return HID2_WIDTH if stage.quartered and after.contraction == HID2_TILES else CW

        def lin_bank(stage, local):
            return (stage.bank_base + local) % LIN_BANKS

        def local_bank(stage, i, u):
            return (i * 2 + u // 4) if stage.quartered else i * stage.unroll + u

        def static_bank(stage, u):
            return lin_bank(stage, u // 4 if stage.quartered else u)


        AHEAD = {False: 3, True: 2}
        ROPED = 1 + BY_NAME["dil_k"].banks + BY_NAME["dil_q"].banks
        BUSY = {"first steps": 6, "step": 2, "wide start": 8, "norm": 16}
        BEGUN = 6
        HOLD = HEADS

        def in_steps(eng, step, steps, first=8):
            for u in range(first):
                step(0, u)
            with eng.Fori(0, 2) as i:
                for u in range(first, first + 4):
                    step(i, u)
            for u in range(first + 8, steps):
                step(0, u)

        block = ctx.enter_context(nc.Block())

        @block.sync
        def _(sp):
            sp.dma_start(pos_i[:, :], bass.AP(tensor=pos_in.tensor, offset=0, ap=[[0, P], [1, SEQ]]))\
              .then_inc(const_landed, 16)
            sp.dma_start(consts[:, :], const_in[:, C_IDENT:CONST_COLS]).then_inc(const_landed, 16)
            sp.dma_start(gains[:, :], gains_in).then_inc(gains_landed, 16)
            for half in range(2):
                tiles = slice(half * KT // 2, (half + 1) * KT // 2)
                sp.dma_start(x[:, tiles, :], x_in[:, tiles, :]).then_inc(x_landed[half], 16)
            for stage in STAGES:
                width = HID2_WIDTH if stage.contraction == HID2_TILES else CW

                def load(i, u, stage=stage, width=width):
                    g = stage.base + u
                    s = g % RAW_SLOTS
                    c = i * stage.unroll + stage.base + u
                    if g >= RAW_SLOTS:
                        sp.wait_ge(lo_split, i * stage.unroll + (g - RAW_SLOTS + 1))
                    lo = 0
                    if g == 0:
                        lo = CW // 2
                        sp.dma_start(raw[:, 0, 0:lo], stream[0, :, 0:lo]).then_inc(half_landed, 16)
                    sp.dma_start(raw[:, s, lo:width], stream[c, :, lo:width]).then_inc(raw_landed[s], 16)

                if stage.base == 0:
                    for u in range(4):
                        load(0, u)
                    for u in range(4, stage.chunks):
                        load(0, u)
                else:
                    in_loop(sp, stage, load)
            for j in range(KT // 2):
                sp.wait_ge(x_ready, 4 * (KT // 2) + j + 1)
                sp.dma_start(out[:, 2 * j:2 * j + 2, :], x[:, 2 * j:2 * j + 2, :]).then_inc(stored, 16)
            sp.wait_ge(stored, 16 * (KT // 2))

        @block.tensor
        def _(pe):
            n_stat = [0]
            n_sums = [0]
            n_spread = [0]

            def fmm(out_ap, stat, mov, first, last):
                return nc.tensor.matmul(out_ap, stat, mov, start=first, stop=last, skip_group_check=True)

            def features(b, slot, col, a_hi, a_lo, k0, nk, first, last, waits=None, together=1):
                for k in range(nk):
                    if waits is not None and k % together == 0:
                        pe.wait_ge(op_ready, waits + k // together + 1)
                    for n in range(2):
                        c = col(k, n)
                        o = bank[:, b, n * SEQ:(n + 1) * SEQ]
                        w_h, w_l = whi[:, slot, c:c + P], wlo[:, slot, c:c + P]
                        fmm(o, w_h, a_hi[:, k0 + k, :], first and k == 0 and n == 0, False)
                        fmm(o, w_h, a_lo[:, k0 + k, :], False, False)
                        ins = fmm(o, w_l, a_hi[:, k0 + k, :], False, last and k == nk - 1)
                return ins

            def tokens(b, slot, col, width, k0, nk, out_width=SEQ):
                for k in range(nk):
                    c = col(k)
                    for t in range(QT):
                        o = bank[:, b, t * out_width:t * out_width + width]
                        rows = slice(t * P, (t + 1) * P)
                        w_h, w_l = whi[:, slot, c:c + width], wlo[:, slot, c:c + width]
                        fmm(o, ahi[:, k0 + k, rows], w_h, k == 0 and t == 0, False)
                        fmm(o, alo[:, k0 + k, rows], w_h, False, False)
                        ins = fmm(o, ahi[:, k0 + k, rows], w_l, False, k == nk - 1)
                return ins

            def weights_ready(stage, i, u):
                pe.wait_ge(lo_split, i * stage.unroll + (stage.base + u + 1))

            def bank_free(stage, i, local):
                j = stage.bank_base + local
                if j >= LIN_BANKS:
                    per = 2 if stage.quartered else stage.unroll
                    pe.wait_ge(bank_read, i * per + (j - LIN_BANKS + 1))

            def part(stage, k0, nk, operand=(ahi, alo)):
                base = OP_BEFORE[stage.name]
                return features(lin_bank(stage, 0), chunk_slot(stage, 0), lambda k, n: (2 * (k0 + k) + n) * P, *operand,
                                k0, nk, k0 == 0, k0 + nk == KT, waits=base + k0)

            def product(stage, operand_base, operand=(ahi, alo), together=1, between=None, begun=0):
                def step(i, u):
                    if stage.base + u == 0:
                        pe.wait_ge(half_lo, 1)
                    else:
                        weights_ready(stage, i, u)
                    local = u // 4 if stage.quartered else u
                    if begun and u == 0:
                        part(stage, begun, KT - begun).then_inc(chunk_used, 1)
                        return
                    if not stage.quartered or u % 4 == 0:
                        bank_free(stage, i, local)
                    b, slot = static_bank(stage, u), chunk_slot(stage, u)
                    if stage.quartered:
                        k0, nk = QUARTERS[stage.contraction][u % 4]
                        need = (k0 + nk) // 2 if stage.contraction == HID_TILES else k0 + nk
                        pe.wait_ge(op_ready, operand_base + need)
                        ins = features(b, slot, lambda k, n: (2 * k + n) * P, bhi, blo, k0, nk, u % 4 == 0,
                                       u % 4 == 3)
                    elif stage.kind == "token":
                        ins = tokens(b, slot, lambda k: 2 * k * P, 2 * P, 0, KT)
                    elif stage.base + u == 0:
                        half = KT // 2
                        part(stage, 0, half)
                        weights_ready(stage, 0, 0)
                        ins = part(stage, half, half)
                    else:
                        ins = features(b, slot, lambda k, n: (2 * k + n) * P, *operand, 0, KT, True, True,
                                       waits=operand_base if u == 0 else None, together=together)
                    ins.then_inc(chunk_used, 1)
                if between is not None:
                    step(0, 0)
                    between()
                in_loop(pe, stage, step, first=0 if between is None else 1)

            def statistics():
                n_stat[0] += 1
                n_sums[0] += KT // 2 - 1
                pe.wait_ge(sums, n_sums[0])
                for t in range(2):
                    ins = nc.tensor.matmul(bank[:, STAT, 0:SEQ], ones[:, :], ssum[:, t, :], start=(t == 0), stop=(t == 1))
                ins.then_inc(totals, 1)

            def awaited_statistics():
                n_stat[0] += 1
                n_sums[0] += KT // 2 - 1
                n_spread[0] += 1
                pe.wait_ge(sums, n_sums[0])
                for q in range(QT):
                    for t in range(2):
                        ins = nc.tensor.matmul(bank[:, STAT, q:q + 1], ssum[:, t, q * P:(q + 1) * P], ones[:, 0:1],
                                               start=(q == 0 and t == 0), stop=(t == 1), skip_group_check=True)
                ins.then_inc(totals, 1)
                pe.wait_ge(inverse_col, n_spread[0])
                for q in range(QT):
                    ins = nc.tensor.matmul(bank[:, STAT, SEQ + q * P:SEQ + (q + 1) * P],
                                           rcol[:, q:q + 1].to_broadcast([P, P]), ident, start=True, stop=True,
                                           skip_group_check=True)
                ins.then_inc(spread, 1)

            def latent_statistics():
                n_stat[0] += 1
                n_sums[0] += 1
                pe.wait_ge(sums, n_sums[0])
                nc.tensor.matmul(bank[:, STAT, :], ones[:, :], ssum[:, :, :].rearrange("p a t -> p (a t)"),
                                 start=True, stop=True).then_inc(totals, 1)

            def columns(source):
                pe.wait_ge(rstd_ready, n_stat[0])
                for t in range(QT):
                    ins = nc.tensor.matmul(bank[:, STAT, t:t + 1], rstd[0:1, source, t * P:(t + 1) * P], ones[0:1, 0:1],
                                           start=(t == 0), stop=(t == 1), skip_group_check=True)
                ins.then_inc(col_ready, 1)

            def busy(b, n):
                for _ in range(n):
                    nc.tensor.matmul(bank[:, b, 0:P], ones[:, :], ones[:, :], start=True, stop=True, skip_group_check=True)

            def attention(run, branches, after):
                base, wide = HEADS * run, branches > 1
                ahead = AHEAD[wide]
                pairs = base // 2
                s_banks, pt_banks = ((0, 1, 2), (3, 4, 5)) if wide else (S_BANKS, PT_BANKS)

                def step(i, u):
                    h, r = u - ahead, u - ahead + 1
                    if HEADS < u <= HEADS + BEGUN // 2:
                        if u == HEADS + 1:
                            weights_ready(after, 0, 0)
                            pe.wait_ge(l_ready, base + HEADS)
                        part(after, 2 * (u - HEADS - 1), 2)
                    if wide and u in (1, 2):
                        busy(O_BANKS[1], BUSY["wide start"])
                    if u < HEADS:
                        slot, odd = (u // 2) % 2, u % 2
                        rows = slice(odd * DH, odd * DH + DH)
                        if not odd:
                            if u == 0:
                                pe.wait_ge(first_q, run + 1)
                                pe.wait_ge(first_k, run + 1)
                            else:
                                pe.wait_ge(qk_staged, i * 4 + (run * (HEADS - 2) + u))
                        if u == (0 if wide else 2):
                            pe.wait_ge(bank_read, after.bank_base)
                        need = base + u if wide else base + u + 1 - len(s_banks)
                        if need > 0:
                            pe.wait_ge(l_ready, i * 4 + need)
                        if not wide:
                            busy(s_banks[u % 4], BUSY["step" if u >= 2 else "first steps"])
                        for g in range(branches):
                            b = s_banks[g] if wide else s_banks[u % 4]
                            nc.tensor.matmul(bank[:, b, 0:P], q_pair[rows, slot, g, 0:P], k_pair[rows, slot, g, 0:P],
                                             start=True, stop=True, skip_group_check=True)
                            ins = nc.tensor.matmul(bank[:, b, P:CAUSAL], q_pair[rows, slot, g, P:SEQ],
                                                   k_pair[rows, slot, g, :], start=True, stop=True, skip_group_check=True)
                        ins.then_inc(s_ready, 1)
                    if 0 <= h < HEADS:
                        b = O_BANKS[(h // 2) % 2]
                        odd = h % 2
                        pe.wait_ge(tc_ready, i * 4 + (base + h + 1))
                        if not odd:
                            pe.wait_ge(v_staged, i * 2 + (pairs + h // 2 + 1))
                        if not odd and h >= 4:
                            pe.wait_ge(op_ready, i * 2 + (OP_BEFORE[ATTENTION_FOR[run]] + h // 2 - 1))
                        for q in range(QT):
                            o = bank[:, b, q * P + odd * DH:q * P + odd * DH + DH]
                            terms = [(g, c) for g in range(branches) for c in range(q + 1)]
                            for n, (g, c) in enumerate(terms):
                                at_col = (q + c) * P
                                src = (pt[:, g, at_col:at_col + P] if wide else pt[:, h % 2, at_col:at_col + P])
                                v = v_pair[:, (h // 2) % 2, g * QT + c, odd * DH:odd * DH + DH]
                                ins = nc.tensor.matmul(o, src, v, start=(n == 0),
                                                       stop=(n == len(terms) - 1), skip_group_check=True)
                        ins.then_inc(o_ready, 1)
                    if h >= 2 and h % 2 == 0:
                        t = h // 2 - 1
                        pe.wait_ge(on_ready, i * 2 + (pairs + t + 1))
                        for q in range(QT):
                            ins = nc.tensor.transpose(bank[:, O_BANKS[t % 2], SEQ + q * P:SEQ + (q + 1) * P],
                                                      o_pair[:, t % 2, q * P:(q + 1) * P], ident)
                        ins.then_inc(ot_ready, 1)
                    if 0 <= r < HEADS:
                        pe.wait_ge(p_ready, i * 4 + (base + r + 1))
                        held = base + r if wide else base + r - 1
                        if held > 0:
                            pe.wait_ge(tc_ready, i * 4 + held)
                        for g in range(branches):
                            b = pt_banks[g] if wide else pt_banks[r % 2]
                            src = logits3[:, r % 2, g * CAUSAL:(g + 1) * CAUSAL] if wide else logits[:, r % 4, :]
                            for c in range(3):
                                cols = slice(c * P, (c + 1) * P)
                                ins = nc.tensor.transpose(bank[:, b, cols], src[:, cols], ident)
                        ins.then_inc(t_ready, 1)

                in_steps(pe, step, HEADS + ahead + 2)

            def bias_by_distance():
                pe.wait_ge(table_landed, 48)
                nc.tensor.matmul(bank[0:HEADS, 2, 0:CAUSAL], table[:, :], onehot[:, :], start=True, stop=True)\
                  .then_inc(dist_ready, 1)

            def low_rank():
                stage = BY_NAME["dsa_low"]
                j = 0
                for c in range(4):
                    weights_ready(stage, 0, c)
                    for pair in range(2 if c == 0 else 4):
                        if pair == 0 and c in (0, 2):
                            pe.wait_ge(op_ready, OP_BEFORE["dsa_low"] + (2 if c == 0 else 4))
                        bank_free(stage, 0, j)
                        b, slot = lin_bank(stage, j), chunk_slot(stage, c)
                        if c == 3:
                            ins = tokens(b, slot, lambda k: k * 1024 + pair * 256, 256, 2, 2)
                        else:
                            ins = features(b, slot, lambda k, n: k * 1024 + pair * 256 + n * P, ahi, alo,
                                           2 if c == 2 else 0, 2, True, True)
                        last = pair == (1 if c == 0 else 3)
                        ins.then_inc(chunk_used if last else low_bank, 1)
                        j += 1
                    if c == 0:
                        turn_index_weights()
                        index_scores()

            def index_scores():
                stage = BY_NAME["dsa_low"]
                pe.wait_ge(bank_read, stage.bank_base + 2)
                for h in range(IDX_HEADS):
                    rows = slice((h % 2) * DH, (h % 2) * DH + DH)
                    b = IDX_BANKS[h % len(IDX_BANKS)]
                    if h >= len(IDX_BANKS):
                        pe.wait_ge(idx_relu, h + 1 - len(IDX_BANKS))
                    nc.tensor.matmul(bank[:, b, 0:P], q_idx[rows, h // 2, 0:P], k_idx[rows, 0:P],
                                     start=True, stop=True, skip_group_check=True)
                    nc.tensor.matmul(bank[:, b, P:CAUSAL], q_idx[rows, h // 2, P:SEQ], k_idx[rows, :],
                                     start=True, stop=True, skip_group_check=True).then_inc(idx_ready, 1)

            def dsa_in():
                stage = BY_NAME["dsa_in"]
                for c in range(2):
                    weights_ready(stage, 0, c)
                    bank_free(stage, 0, c)
                    features(lin_bank(stage, c), chunk_slot(stage, c), lambda k, n: (2 * k + n) * P, ahi, alo, 0, KT,
                             True, True, waits=OP_BEFORE["dsa_in"] if c == 0 else None).then_inc(chunk_used, 1)
                    if c == 0:
                        statistics()
                weights_ready(stage, 0, 2)
                bank_free(stage, 0, 2)
                slot, b = chunk_slot(stage, 2), lin_bank(stage, 2)
                for k in range(KT):
                    c = 2 * k * P
                    fmm(bank[:, b, 0:SEQ], whi[:, slot, c:c + P], ahi[:, k, :], k == 0, False)
                    fmm(bank[:, b, 0:SEQ], whi[:, slot, c:c + P], alo[:, k, :], False, False)
                    ins = fmm(bank[:, b, 0:SEQ], wlo[:, slot, c:c + P], ahi[:, k, :], False, k == KT - 1)
                ins.then_inc(low_bank, 1)
                latent_statistics()
                bank_free(stage, 0, 3)
                b = lin_bank(stage, 3)
                for k in range(KT):
                    c = (2 * k + 1) * P
                    o = bank[0:IDX_HEADS, b, 0:SEQ]
                    fmm(o, whi[:, slot, c:c + IDX_HEADS], ahi[:, k, :], k == 0, False)
                    fmm(o, whi[:, slot, c:c + IDX_HEADS], alo[:, k, :], False, False)
                    ins = fmm(o, wlo[:, slot, c:c + IDX_HEADS], ahi[:, k, :], False, k == KT - 1)
                ins.then_inc(chunk_used, 1)
                busy(O_BANKS[0], BUSY["norm"])

            def turn_index_weights():
                pe.wait_ge(bank_read, BY_NAME["dsa_low"].bank_base)
                for t in range(QT):
                    ins = nc.tensor.transpose(bank[:, O_BANKS[0], t * IDX_HEADS:(t + 1) * IDX_HEADS],
                                              w_rows[:, t * P:(t + 1) * P], ident[0:IDX_HEADS, 0:IDX_HEADS])
                ins.then_inc(w_turned, 1)

            def first_norm():
                pe.wait_ge(ones_set, 2)
                statistics()
                bias_by_distance()

            product(BY_NAME["moba_qk"], OP_BEFORE["moba_qk"], between=first_norm)
            columns(0)
            product(BY_NAME["moba_v"], 0)
            attention(0, 1, BY_NAME["moba_o"])
            product(BY_NAME["moba_o"], OP_BEFORE["moba_o"], begun=BEGUN)
            for n in range(2):
                if n == 1:
                    dsa_in()
                    low_rank()
                    attention(1, 1, BY_NAME["dsa_o"])
                    product(BY_NAME["dsa_o"], OP_BEFORE["dsa_o"], begun=BEGUN)
                product(BY_NAME[f"up_{n}"], OP_BEFORE[f"up_{n}"], (a2hi, a2lo), between=statistics)
                product(BY_NAME[f"down_{n}"], OP_BEFORE[f"down_{n}"])
            awaited_statistics()
            busy(O_BANKS[0], BUSY["norm"])
            product(BY_NAME["conv_ch"], OP_BEFORE["conv_ch"], between=statistics)
            product(BY_NAME["conv_b"], OP_BEFORE["conv_ch"])
            product(BY_NAME["conv_out"], OP_BEFORE["conv_out"], (chi, clo), together=2)
            awaited_statistics()
            busy(O_BANKS[0], BUSY["norm"])
            for n in range(2):
                if n == 1:
                    product(BY_NAME["dil_k"], OP_BEFORE["dil_k"], between=statistics)
                    columns(0)
                    product(BY_NAME["dil_q"], OP_BEFORE["dil_q"], (a2hi, a2lo))
                    product(BY_NAME["dil_v"], 0)
                    attention(2, NB, BY_NAME["dil_o"])
                    product(BY_NAME["dil_o"], OP_BEFORE["dil_o"], begun=BEGUN)
                    awaited_statistics()
                    busy(O_BANKS[0], BUSY["norm"])
                product(BY_NAME[f"gate_up_{n}"], OP_BEFORE[f"gate_up_{n}"], between=statistics)
                product(BY_NAME[f"ffn_down_{n}"], OP_BEFORE[f"ffn_down_{n}"])
                awaited_statistics()
                if n == 0:
                    busy(O_BANKS[0], BUSY["norm"])

        @block.scalar
        def _(act):
            n_sq, n_sums, n_norm, n_x = [0], [0], [0], [0]

            def split(stage, i, u):
                g = stage.base + u + SPLIT_SLOTS
                if stage is STAGES[-1] and isinstance(i, int) and i * stage.unroll + g >= CHUNKS:
                    return
                per = stage.unroll // RAW_SLOTS
                s = g % RAW_SLOTS
                act.wait_ge(raw_landed[s], (i * per + (g // RAW_SLOTS + 1)) * 16)
                act.wait_ge(chunk_used, i * stage.unroll + (g - 1))
                w = split_width(stage, u)
                nc.scalar.activation(whi[:, g % SPLIT_SLOTS, 0:w], raw[:, s, 0:w], ACT.Copy).then_inc(hi_split, 1)

            def first_split(g, lo=0, hi=CW, landed=None, done=hi_split):
                act.wait_ge(raw_landed[g] if landed is None else landed, 16)
                nc.scalar.activation(whi[:, g, lo:hi], raw[:, g, lo:hi], ACT.Copy).then_inc(done, 1)

            def square(src, j):
                if j == 2:
                    act.wait_ge(sums, n_sums[0] + 1)
                nc.scalar.activation(sq[:, 2 * (j % 2):2 * (j % 2) + 2, :], src[:, 2 * j:2 * j + 2, :], ACT.Square)\
                  .then_inc(squares, 1)
                n_sq[0] += 1
                if j == KT // 2 - 1:
                    n_sums[0] += KT // 2 - 1

            def token_root():
                n_norm[0] += 1
                act.wait_ge(totals, n_norm[0])
                nc.scalar.activation(root_col[:, :], bank[:, STAT, 0:QT], ACT.Sqrt, bias=eps[:, 0:1], scale=1.0 / D)\
                  .then_inc(roots, 1)

            def root(over, width=SEQ):
                n_norm[0] += 1
                act.wait_ge(totals, n_norm[0])
                nc.scalar.activation(std[:, :, :].rearrange("p a t -> p (a t)")[:, 0:width], bank[:, STAT, 0:width],
                                     ACT.Sqrt, bias=eps[:, 0:1], scale=1.0 / over).then_inc(roots, 1)

            def high_tile(dst, gain, k):
                nc.scalar.activation(dst[:, k, :], x[:, k, :], ACT.Copy,
                                     scale=gains[:, gain + k:gain + k + 1]).then_inc(act_hi, 1)

            def high_operand(dst, gain, j):
                for k in (2 * j, 2 * j + 1):
                    high_tile(dst, gain, k)

            def norm_operand(gain):
                for j in range(KT // 2):
                    n_x[0] += 1
                    act.wait_ge(x_ready, n_x[0])
                    high_operand(ahi, GAIN_AT[gain], j)
                    square(x, j)
                root(D)

            def through(stage, step=None, held=False, also=None):
                def body(i, u):
                    if not (held and isinstance(i, int) and u == stage.chunks - 1):
                        split(stage, i, u)
                    if step is not None:
                        step(i, u)
                if also is not None:
                    for k in range(KT):
                        body(0, k)
                        also(k)
                in_loop(act, stage, body, first=0 if also is None else KT, peeled=held)

            def through_into_norm(stage, pair, waited=False):
                for u in range(stage.chunks):
                    last = u == stage.chunks - 1
                    if not last:
                        split(stage, 0, u)
                    if not stage.quartered or u % 4 == 3:
                        j = u // 4 if stage.quartered else u
                        if last and waited:
                            nc.scalar.activation(scratch[:, :], eps[:, :], ACT.Sqrt)
                        act.wait_ge(bank_read, stage.bank_base + j + 1)
                        pair(j)
                    if last and waited:
                        token_root()
                    if last:
                        split(stage, 0, u)
                if not waited:
                    root(D)

            def into_operand(dst, gain):
                def pair(j):
                    high_operand(dst, GAIN_AT[gain], j)
                    square(x, j)
                return pair

            def scaled_for_norm(src, gain):
                def pair(j):
                    square(src, j)
                    if src is y:
                        act.wait_ge(squares, n_sq[0])
                    for k in (2 * j, 2 * j + 1):
                        g = GAIN_AT[gain] + k
                        ins = nc.scalar.activation(y[:, k, :], src[:, k, :], ACT.Copy, scale=gains[:, g:g + 1])
                    ins.then_inc(scaled, 1)
                return pair

            def relu_stage(stage):
                before = banks_before(stage, "relu", "swiglu")

                def step(i, u):
                    j = i * stage.unroll + u
                    act.wait_ge(bank_read, i * stage.unroll + (stage.bank_base + u + 1))
                    nc.scalar.activation(zz[:, :, :], z[:, :, :], ACT.Square).then_inc(relu_squared, 1)
                    act.wait_ge(relu_squared, i * stage.unroll + (before + u + 1))
                    nc.scalar.activation(bhi[:, bass.ds(j * 2, 2), :], zz[:, :, :], ACT.Copy).then_inc(h_ready, 1)
                through(stage, step)

            def swiglu_stage(stage):
                def step(i, u):
                    act.wait_ge(bank_read, i * stage.unroll + (stage.bank_base + u + 1))
                    nc.scalar.activation(zz[:, 0, :], z[:, 0, :], ACT.Silu).then_inc(h_ready, 1)
                through(stage, step)

            def rope_stage(stage, also=None):
                before = banks_before(stage, "rope")

                def step(i, u):
                    b = static_bank(stage, u)
                    act.wait_ge(rope_cos, i * stage.unroll + (before + u + 1))
                    act.wait_ge(roped, i * stage.unroll + (before + u + 1))
                    for d in range(4):
                        s = d ^ 1
                        ins = nc.scalar.activation(zz[d * 32:(d + 1) * 32, :, :].rearrange("p a t -> p (a t)"),
                                                   bank[s * 32:(s + 1) * 32, b, :], ACT.Copy)
                    ins.then_inc(bank_read, 1)
                through(stage, step, also=also)

            def stage_first_k(branches):
                k_of = k3[:, :, :].rearrange("p (g k) t -> p g k t", g=NB) if branches > 1 else k1.unsqueeze(1)
                nc.scalar.activation(k_pair[:, 0, 0:branches, :], k_of[:, :, 0, :], ACT.Copy).then_inc(first_k, 1)

            def attention(run, branches, last):
                base, wide = HEADS * run, branches > 1
                ahead = AHEAD[wide]

                def step(i, u):
                    h, r = u - ahead, u - ahead + 1
                    if h >= 3 and h % 2 == 1:
                        t = (h - 3) // 2
                        act.wait_ge(ot_ready, i * 2 + (base // 2 + t + 1))
                        nc.scalar.activation(ahi[:, bass.ds(i * 2 + t, 1), :],
                                             bank[:, O_BANKS[t % 2]:O_BANKS[t % 2] + 1, SEQ:2 * SEQ], ACT.Copy)\
                          .then_inc(ohi_ready, 1)
                    if 0 <= r < HEADS:
                        act.wait_ge(t_ready, i * 4 + (base + r + 1))
                        held = base + r if wide else base + r - 1
                        if held > 0:
                            act.wait_ge(o_ready, i * 4 + held)
                        if wide:
                            ins = nc.scalar.activation(pt[:, :, :], bank[:, 3:6, 0:CAUSAL], ACT.Copy)
                        else:
                            ins = nc.scalar.activation(pt[:, r % 2, :], bank[:, PT_BANKS[r % 2], 0:CAUSAL], ACT.Copy)
                        ins.then_inc(tc_ready, 1)
                    if u < HEADS:
                        s = u % 4
                        act.wait_ge(m_ready, i * 4 + (base + u + 1))
                        if wide:
                            l = logits3[:, u % 2, :].rearrange("p (g c) -> p g c", g=NB)
                            first, second = l[:, :, 0:P], l[:, :, P:CAUSAL]
                        else:
                            first, second = logits[:, s, 0:P], logits[:, s, P:CAUSAL]
                        nc.scalar.activation(first, first, ACT.Exp, bias=neg_max[:, s, 0:1],
                                             accum_out=row_sum[:, s, 0:1])
                        nc.scalar.activation(second, second, ACT.Exp, bias=neg_max[:, s, 1:2],
                                             accum_out=row_sum[:, s, 1:2]).then_inc(p_ready, 1)
                    if u == HOLD:
                        split(last, 0, last.chunks - 1)

                in_steps(act, step, HEADS + ahead + 2)

            act.wait_ge(gains_landed, 16)
            for j in range(KT // 2):
                if j % 2 == 0:
                    act.wait_ge(x_landed[j // 2], 16)
                high_operand(ahi, GAIN_AT["ln_attn_0"], j)
            first_split(0, 0, CW // 2, half_landed, half_hi)
            first_split(0, CW // 2)
            for j in range(KT // 2):
                square(x, j)
            first_split(1)
            act.dma_start(masks3[:, :, :], const_in[:, 0:C_CAUSAL].rearrange("p (g c) -> p g c", g=NB))\
               .then_inc(mask_landed, 16)
            act.dma_start(causal[:, :], const_in[:, C_CAUSAL:C_IDENT]).then_inc(mask_landed, 16)
            for n, dst in enumerate((sin_t, cos_t)):
                act.wait_ge(angles, n + 1)
                nc.scalar.activation(dst[:, :], angle[:, :] if n == 0 else shifted[:, :], ACT.Sin).then_inc(sines, 1)
            act.wait_ge(ones_set, 2)
            root(D)
            through(BY_NAME["moba_qk"])
            act.wait_ge(bank_read, BY_NAME["moba_v"].bank_base)
            act.wait_ge(dist_stored, 32)
            stage_first_k(1)
            through(BY_NAME["moba_v"], held=True)
            attention(0, 1, BY_NAME["moba_v"])
            through_into_norm(BY_NAME["moba_o"], into_operand(a2hi, "ln_mlp_0"))
            relu_stage(BY_NAME["up_0"])
            through_into_norm(BY_NAME["down_0"], into_operand(ahi, "ln_attn_1"))
            dsa_in, dsa_low = BY_NAME["dsa_in"], BY_NAME["dsa_low"]
            for c, latent in enumerate((z_q, z_kv)):
                act.wait_ge(bank_read, dsa_in.bank_base + c + 1)
                nc.scalar.activation(sq[:, 2 * c:2 * c + 2, :], latent[:, :, :], ACT.Square).then_inc(squares, 1)
                n_sq[0] += 1
                split(dsa_in, 0, c)
            n_sums[0] += 1
            root(LORA, 2 * SEQ)
            for c, latent in enumerate((z_q, z_kv)):
                act.wait_ge(latent_ready, c + 1)
                for k in range(2):
                    g = LATENT_GAIN_AT + 2 * c + k
                    nc.scalar.activation(ahi[:, 2 * c + k, :], latent[:, k, :], ACT.Copy, scale=gains[:, g:g + 1])\
                      .then_inc(act_hi, 1)
            split(dsa_in, 0, 2)
            lows, j = 1, 0
            for c in range(4):
                pairs = 2 if c == 0 else 4
                for pair in range(pairs):
                    if pair == pairs - 1:
                        act.wait_ge(chunk_used, dsa_low.base + c + 1)
                    else:
                        lows += 1
                        act.wait_ge(low_bank, lows)
                    b = bank[:, lin_bank(dsa_low, j), :].rearrange("p (a t) -> p a t", a=2)
                    dst = v1[:, :, pair * 256:(pair + 1) * 256] if c == 3 else \
                        (q_idx, q1, k1)[c][:, 2 * pair:2 * pair + 2, :]
                    nc.scalar.activation(dst, b, ACT.Copy).then_inc(bank_read, 1)
                    j += 1
                if c == 0:
                    for h in range(IDX_HEADS):
                        act.wait_ge(idx_ready, h + 1)
                        nc.scalar.activation(relu_s[:, h, :], bank[:, IDX_BANKS[h % len(IDX_BANKS)], 0:CAUSAL], ACT.Relu).then_inc(idx_relu, 1)
                if c < 3:
                    split(dsa_low, 0, c)
            act.wait_ge(idx_used, IDX_HEADS)
            act.wait_ge(bank_read, BY_NAME["dsa_o"].bank_base)
            stage_first_k(1)
            attention(1, 1, dsa_low)
            through_into_norm(BY_NAME["dsa_o"], into_operand(a2hi, "ln_mlp_1"))
            relu_stage(BY_NAME["up_1"])
            through_into_norm(BY_NAME["down_1"], scaled_for_norm(x, "final"), waited=True)
            norm_operand("mix_pre_0")
            through(BY_NAME["conv_ch"])

            def gate_high(i, u):
                act.wait_ge(conv_ready, u + 1)
                nc.scalar.activation(chi[:, 2 * u:2 * u + 2, :], conv[:, 2 * u:2 * u + 2, :], ACT.Copy).then_inc(act_hi, 1)
            through(BY_NAME["conv_b"], gate_high)
            through_into_norm(BY_NAME["conv_out"], scaled_for_norm(y, "mix_post_0"), waited=True)
            norm_operand("ffn_pre_0")
            swiglu_stage(BY_NAME["gate_up_0"])
            through_into_norm(BY_NAME["ffn_down_0"], scaled_for_norm(y, "ffn_post_0"), waited=True)
            norm_operand("kv")
            rope_stage(BY_NAME["dil_k"], lambda k: high_tile(a2hi, GAIN_AT["mix_pre_1"], k))
            rope_stage(BY_NAME["dil_q"])
            act.wait_ge(chunk_used, BY_NAME["dil_v"].base)
            stage_first_k(NB)
            through(BY_NAME["dil_v"], held=True)
            attention(2, NB, BY_NAME["dil_v"])
            through_into_norm(BY_NAME["dil_o"], scaled_for_norm(y, "mix_post_1"), waited=True)
            norm_operand("ffn_pre_1")
            swiglu_stage(BY_NAME["gate_up_1"])
            through_into_norm(BY_NAME["ffn_down_1"], scaled_for_norm(y, "ffn_post_1"), waited=True)

        @block.gpsimd
        def _(pool):
            G = nc.gpsimd

            def store_bias():
                whole = by_dist[:, :]
                for lo, hi, offset in ((0, P, 2 * P - 1), (P, CAUSAL, P - 1)):
                    src = bass.AP(tensor=whole.tensor, offset=offset, ap=[list(whole.ap[0]), [-1, P], [1, hi - lo]])
                    pool.dma_start(toeplitz[:, :, lo:hi], src).then_inc(dist_stored, 16)

            def load_bias():
                pool.dma_start(bias[:, :, :], toeplitz.rearrange("h p c -> p h c")).then_inc(bias_landed, 16)

            def attention(run, branches, masked=False):
                base, wide = HEADS * run, branches > 1
                if wide:
                    q_of, k_of = (a[:, :, :].rearrange("p (g k) t -> p g k t", g=NB) for a in (q3, k3))
                else:
                    q_of, k_of = q1.unsqueeze(1), k1.unsqueeze(1)

                def stage_qk(i, t):
                    slot = t % 2
                    for src, dst in ((q_of, q_pair), (k_of, k_pair)):
                        G.tensor_copy(dst[:, slot, 0:branches, :].unsqueeze(2), src[:, :, bass.ds(i * 2 + t, 1), :])\
                         .then_inc(qk_staged, 1)

                def step(i, u):
                    if masked and u < HEADS:
                        if u >= 4:
                            pool.wait_ge(l_ready, i * 4 + (base + u - 3))
                        G.tensor_tensor(masked_bias[:, u % 4, :], bias[:, bass.ds(i * 4 + u, 1), :].squeeze(1),
                                        topmask[:, :], ALU.add).then_inc(topped, 1)
                    if u % 2 and u < HEADS - 1:
                        t = u // 2
                        if base + 2 * t > 0:
                            pool.wait_ge(s_ready, i * 4 + (base + 2 * t))
                        stage_qk(i, t + 1)

                if masked:
                    pool.wait_ge(topmask_ready, 1)
                in_steps(pool, step, HEADS, first=4)

            pool.dma_start(table[:, :], table_in).then_inc(table_landed, 16)
            pool.dma_start(onehot[:, :], onehot_in).then_inc(table_landed, 16)
            pool.dma_start(negmask[:, :], negmask_in).then_inc(table_landed, 16)
            pool.wait_ge(dist_done, 1)
            store_bias()
            pool.wait_ge(dist_stored, 32)
            load_bias()
            pool.wait_ge(bank_read, BY_NAME["moba_v"].bank_base)
            attention(0, 1)
            pool.wait_ge(bank_read, BY_NAME["dsa_in"].bank_base)
            load_bias()
            pool.wait_ge(bias_landed, 32)
            pool.wait_ge(bank_read, BY_NAME["dsa_o"].bank_base)
            attention(1, 1, masked=True)
            pool.wait_ge(roped, ROPED)
            pool.wait_ge(chunk_used, BY_NAME["dil_v"].base)
            attention(2, NB)

        @block.vector
        def _(dve):
            own = Own(dve, dve_step)
            n_sq, n_sums, n_norm, n_hi, n_x, n_col = [0], [0], [0], [0], [0], [0]
            V = nc.vector

            def plain(ap):
                return ap.bitcast(F32)

            def split(stage, i, u):
                g = stage.base + u + SPLIT_SLOTS
                if stage is STAGES[-1] and isinstance(i, int) and i * stage.unroll + g >= CHUNKS:
                    return
                dve.wait_ge(hi_split, i * stage.unroll + (g + 1))
                s = g % SPLIT_SLOTS
                w = split_width(stage, u)
                V.tensor_tensor(wlo[:, s, 0:w], raw[:, g % RAW_SLOTS, 0:w], plain(whi[:, s, 0:w]), ALU.subtract)\
                 .then_inc(lo_split, 1)

            def first_split(g, lo=0, hi=CW, landed=None, done=lo_split):
                if landed is None:
                    dve.wait_ge(hi_split, g + 1)
                else:
                    dve.wait_ge(landed, 1)
                V.tensor_tensor(wlo[:, g, lo:hi], raw[:, g, lo:hi], plain(whi[:, g, lo:hi]), ALU.subtract)\
                 .then_inc(done, 1)

            def add_squares(j):
                if j == 0:
                    return
                if j == 1:
                    n_sq[0] += 1
                n_sq[0] += 1
                dve.wait_ge(squares, n_sq[0])
                if j == 1:
                    a = sq[:, 0:2, :]
                else:
                    dve.wait_ge(sums, n_sums[0])
                    a = ssum[:, :, :]
                V.tensor_tensor(ssum[:, :, :], a, sq[:, 2 * (j % 2):2 * (j % 2) + 2, :], ALU.add).then_inc(sums, 1)
                n_sums[0] += 1

            def inverse_root():
                n_norm[0] += 1
                dve.wait_ge(roots, n_norm[0])
                V.reciprocal(rstd[:, 0, :], std[:, 0, :]).then_inc(rstd_ready, 1)
                dve.wait_ge(rstd_ready, n_norm[0])

            def low_tile(hi, lo, gain, k):
                n_hi[0] += 1
                dve.wait_ge(act_hi, n_hi[0])
                V.scalar_tensor_tensor(lo[:, k, :], x[:, k, :], gains[:, gain + k:gain + k + 1],
                                       plain(hi[:, k, :]), ALU.mult, ALU.subtract).then_inc(op_ready, 1)

            def low_operand(hi, lo, gain, j):
                for k in (2 * j, 2 * j + 1):
                    low_tile(hi, lo, gain, k)

            def inverse_root_spread():
                n_norm[0] += 1
                dve.wait_ge(roots, n_norm[0])
                n_col[0] += 1
                V.reciprocal(rcol[:, :], root_col[:, :]).then_inc(inverse_col, 1)
                dve.wait_ge(spread, n_col[0])
                V.tensor_copy(rstd[:, 0, :], bank[:, STAT, SEQ:2 * SEQ]).then_inc(rstd_ready, 1)
                dve.wait_ge(rstd_ready, n_norm[0])

            def token_scale(n):
                dve.wait_ge(col_ready, n)
                V.tensor_copy(rcol[:, :], bank[:, STAT, 0:QT]).then_inc(rcol_ready, 1)
                dve.wait_ge(rcol_ready, n)

            def both(ap):
                return ap.unsqueeze(1).to_broadcast([P, 2, SEQ])

            def through(stage, step, tail=None, held=False, also=None):
                def body(i, u):
                    done = not stage.quartered or u % 4 == 3
                    if done:
                        dve.wait_ge(chunk_used, i * stage.unroll + (stage.base + u + 1))
                        local = u // 4 if stage.quartered else u
                        per = 2 if stage.quartered else stage.unroll
                        b = bank[:, lin_bank(stage, local), :].rearrange("p (a t) -> p a t", a=2)
                        step(i, u, i * per + local, b)
                    if not (held and isinstance(i, int) and u == stage.chunks - 1):
                        split(stage, i, u)
                    if done and tail is not None:
                        tail(i, u, i * per + local, b)
                if also is not None:
                    for k in range(KT):
                        body(0, k)
                        also(k)
                in_loop(dve, stage, body, first=0 if also is None else KT, peeled=held)

            def through_into_norm(stage, pair, tail, waited=False):
                for u in range(stage.chunks):
                    done = not stage.quartered or u % 4 == 3
                    last = u == stage.chunks - 1
                    j = u // 4 if stage.quartered else u
                    if done:
                        dve.wait_ge(chunk_used, stage.base + u + 1)
                        pair(0, u, j, bank[:, lin_bank(stage, j), :].rearrange("p (a t) -> p a t", a=2))
                    if not last:
                        split(stage, 0, u)
                    if done:
                        tail(j)
                    if last and not waited:
                        split(stage, 0, u)
                if waited:
                    inverse_root_spread()
                else:
                    inverse_root()

            def into_operand(hi, lo, gain):
                def tail(j):
                    low_operand(hi, lo, GAIN_AT[gain], j)
                    add_squares(j)
                return tail

            def scaled_into(dst):
                def step(i, u, j, b):
                    V.tensor_tensor(dst[:, bass.ds(j * 2, 2), :], b, both(rstd[:, 0, :]), ALU.mult).then_inc(bank_read, 1)
                return step

            def tokens_into(v, width):
                def step(i, u, j, b):
                    for t in range(QT):
                        ins = V.tensor_scalar(v[:, t, bass.ds(j * 256, 256)], b[:, t, :], rcol[:, t:t + 1], None, ALU.mult)
                    ins.then_inc(bank_read, 1)
                return step

            def residual(i, u, j, b):
                d = x[:, bass.ds(j * 2, 2), :]
                V.tensor_tensor(d, b, d, ALU.add).then_inc(bank_read, 1)

            def before_norm(i, u, j, b):
                V.tensor_copy(y[:, bass.ds(j * 2, 2), :], b).then_inc(bank_read, 1)

            def relu_stage(stage):
                before = banks_before(stage, "relu", "swiglu")

                def step(i, u, j, b):
                    V.scalar_tensor_tensor(z[:, :, :], b, 0.0, both(rstd[:, 0, :]), ALU.max, ALU.mult)\
                     .then_inc(bank_read, 1)

                def tail(i, u, j, b):
                    dve.wait_ge(h_ready, i * stage.unroll + (before + u + 1))
                    V.tensor_tensor(blo[:, bass.ds(j * 2, 2), :], zz[:, :, :], plain(bhi[:, bass.ds(j * 2, 2), :]),
                                    ALU.subtract).then_inc(op_ready, 1)
                return step, tail

            def swiglu_stage(stage):
                before = banks_before(stage, "relu", "swiglu")
                first = banks_before(stage, "swiglu")
                operands = OP_BEFORE[STAGES[stage.n + 1].name]

                def step(i, u, j, b):
                    dve.wait_ge(op_ready, i * stage.unroll + (operands + u))
                    V.tensor_tensor(z[:, :, :], b, both(rstd[:, 0, :]), ALU.mult).then_inc(bank_read, 1)

                def tail(i, u, j, b):
                    n = i * stage.unroll + (first + u + 1)
                    dve.wait_ge(h_ready, i * stage.unroll + (before + u + 1))
                    V.tensor_tensor(zz[:, 1:2, :], zz[:, 0:1, :], z[:, 1:2, :], ALU.mult).then_inc(y_ready, 1)
                    dve.wait_ge(y_ready, n)
                    V.tensor_copy(bhi[:, bass.ds(j, 1), :], zz[:, 1:2, :]).then_inc(yhi_ready, 1)
                    dve.wait_ge(yhi_ready, n)
                    V.tensor_tensor(blo[:, bass.ds(j, 1), :], zz[:, 1:2, :], plain(bhi[:, bass.ds(j, 1), :]),
                                    ALU.subtract).then_inc(op_ready, 1)
                return step, tail

            def rope_stage(stage, dst):
                before = banks_before(stage, "rope")

                def step(i, u, j, b):
                    dve.wait_ge(roped, i * stage.unroll + (before + u + 1))
                    V.tensor_tensor(z[:, :, :], b, both(cos_r[:, :]), ALU.mult).then_inc(rope_cos, 1)

                def tail(i, u, j, b):
                    n = i * stage.unroll + (before + u + 1)
                    dve.wait_ge(bank_read, i * stage.unroll + (stage.bank_base + u + 1))
                    V.tensor_tensor(zz[:, :, :], zz[:, :, :], both(sin_r[:, :]), ALU.mult).then_inc(rope_sin, 1)
                    dve.wait_ge(rope_sin, n)
                    dve.wait_ge(rope_cos, n)
                    V.tensor_tensor(dst[:, bass.ds(j * 2, 2), :], z[:, :, :], zz[:, :, :], ALU.add).then_inc(roped, 1)
                return step, tail

            def stage_first_q(branches):
                q_of = q3[:, :, :].rearrange("p (g k) t -> p g k t", g=NB) if branches > 1 else q1.unsqueeze(1)
                V.tensor_copy(q_pair[:, 0, 0:branches, :], q_of[:, :, 0, :]).then_inc(first_q, 1)

            def attention(run, branches, last, masked=False):
                base, wide = HEADS * run, branches > 1
                ahead = AHEAD[wide]
                pairs = base // 2

                if wide:
                    v_of = v3[:, :, :].rearrange("p q (g n) -> p g q n", g=NB)
                else:
                    v_of = v1[:, :, :].unsqueeze(1)

                def stage_v(i, t):
                    dst = v_pair[:, t % 2, 0:branches * QT, :].rearrange("p (g q) n -> p g q n", q=QT)
                    V.tensor_copy(dst, v_of[:, :, :, bass.ds((i * 2 + t) * P, P)]).then_inc(v_staged, 1)

                for t in range(2):
                    stage_v(0, t)

                def step(i, u):
                    s = u % 4
                    if u < HEADS:
                        dve.wait_ge(s_ready, i * 4 + (base + u + 1))
                        if wide:
                            l = logits3[:, u % 2, :].rearrange("p (g c) -> p g c", g=NB)
                            V.scalar_tensor_tensor(l, bank[:, 0:3, 0:CAUSAL], SCALE, masks3[:, :, :],
                                                   ALU.mult, ALU.add).then_inc(l_ready, 1)
                            first, second, axes = l[:, :, 0:P], l[:, :, P:CAUSAL], AX.XY
                        else:
                            l = logits[:, s, :]
                            if masked:
                                dve.wait_ge(topped, i * 4 + (u + 1))
                                b = masked_bias[:, s, :]
                            else:
                                b = bias[:, bass.ds(i * 4 + u, 1), :].squeeze(1)
                            V.scalar_tensor_tensor(l, bank[:, S_BANKS[s], 0:CAUSAL], SCALE, b,
                                                   ALU.mult, ALU.add).then_inc(l_ready, 1)
                            first, second, axes = l[:, 0:P], l[:, P:CAUSAL], AX.X
                        dve.wait_ge(l_ready, i * 4 + (base + u + 1))
                        V.tensor_reduce(neg_max[:, s, 0:1], first, axes, ALU.max, negate=True)
                        V.tensor_reduce(neg_max[:, s, 1:2], second, axes, ALU.max, negate=True).then_inc(m_ready, 1)
                    if 1 <= u <= HEADS:
                        dve.wait_ge(p_ready, i * 4 + (base + u))
                        V.reciprocal(inv_sum[:, (u - 1) % 4, :], row_sum[:, (u - 1) % 4, :]).then_inc(i_ready, 1)
                    h = u - ahead
                    if h >= 3 and h % 2 == 1:
                        t = (h - 3) // 2
                        dve.wait_ge(ohi_ready, i * 2 + (pairs + t + 1))
                        V.tensor_tensor(alo[:, bass.ds(i * 2 + t, 1), :],
                                        bank[:, O_BANKS[t % 2]:O_BANKS[t % 2] + 1, SEQ:2 * SEQ],
                                        plain(ahi[:, bass.ds(i * 2 + t, 1), :]), ALU.subtract).then_inc(op_ready, 1)
                    if 1 <= h < HEADS and h % 2 == 1:
                        t = h // 2
                        dve.wait_ge(o_ready, i * 4 + (base + h + 1))
                        dve.wait_ge(i_ready, i * 4 + (base + h + 1))
                        if t >= 2:
                            dve.wait_ge(ot_ready, i * 2 + (pairs + t - 1))
                        inv = inv_sum[:, (h - 1) % 4:(h - 1) % 4 + 2, :].rearrange("p h q -> p q h")
                        V.tensor_tensor(o_pair[:, t % 2, :].rearrange("p (q h d) -> p q h d", q=QT, h=2),
                                        bank[:, O_BANKS[t % 2], 0:SEQ].rearrange("p (q h d) -> p q h d", q=QT, h=2),
                                        inv.unsqueeze(3).to_broadcast([P, QT, 2, DH]), ALU.mult).then_inc(on_ready, 1)
                        if h < HEADS - 4:
                            stage_v(i, t + 2)
                    if u == HOLD:
                        split(last, 0, last.chunks - 1)

                in_steps(dve, step, HEADS + ahead + 2, first=ahead + 5)

            def normed(j, add):
                n_x[0] += 1
                dve.wait_ge(scaled, n_x[0])
                tiles = slice(2 * j, 2 * j + 2)
                if add:
                    own.link(V.tensor_tensor(y[:, tiles, :], y[:, tiles, :], both(rstd[:, 0, :]), ALU.mult))
                    V.tensor_tensor(x[:, tiles, :], x[:, tiles, :], y[:, tiles, :], ALU.add).then_inc(x_ready, 1)
                else:
                    V.tensor_tensor(x[:, tiles, :], y[:, tiles, :], both(rstd[:, 0, :]), ALU.mult).then_inc(x_ready, 1)

            def normed_operand(stage, gain, add=True):
                for j in range(KT // 2 + 1):
                    if j < KT // 2:
                        normed(j, add)
                    if j:
                        low_operand(ahi, alo, GAIN_AT[gain], j - 1)
                        add_squares(j - 1)
                split(stage, 0, stage.chunks - 1)
                inverse_root()

            def top_keys(splits, stage):
                own.link(V.tensor_tensor(score[:, :], score[:, :], causal[:, :], ALU.add))
                halves = ((0, slice(0, P)), (1, slice(P, CAUSAL)))
                done = [own.n, own.n]
                for n in range(TOPK // 8):
                    if n in splits:
                        split(stage, 0, splits[n])
                    for t, cols in halves:
                        dve.wait_ge(own.sem, done[t])
                        done[t] = own.count(V.max(best[:, t, :], score[:, cols]))
                    for t, cols in halves:
                        dve.wait_ge(own.sem, done[t])
                        done[t] = own.count(V.match_replace(score[:, cols], best[:, t, :], score[:, cols], TAKEN))
                dve.wait_ge(own.sem, own.n)
                V.tensor_scalar(topmask[:, :], score[:, :], TAKEN / 2, NEG, ALU.is_gt, ALU.mult).then_inc(topmask_ready, 1)

            V.memset(ones[:, :], 1.0).then_inc(ones_set, 1)
            V.memset(eps[:, :], EPS).then_inc(ones_set, 1)
            dve.wait_ge(const_landed, 32)
            own.link(V.tensor_copy(angle[:, :], pos_i[:, :]))
            own.link(V.tensor_scalar(angle[:, :], angle[:, :], consts[:, C_FREQ - C_IDENT:C_FREQ - C_IDENT + 1], None,
                                     ALU.mult))
            magic = 12582912.0
            own.link(V.tensor_scalar(turns[:, :], angle[:, :], 1.0 / (2 * np.pi), magic, ALU.mult, ALU.add))
            own.link(V.tensor_scalar(turns[:, :], turns[:, :], -magic, None, ALU.add))
            two_pi = 2 * np.pi
            part1 = 6.28125
            part2 = float(np.round((two_pi - part1) * 2 ** 21) / 2 ** 21)
            part3 = float(two_pi - part1 - part2)
            for part in (part1, part2, part3):
                own.link(V.scalar_tensor_tensor(angle[:, :], turns[:, :], -part, angle[:, :], ALU.mult, ALU.add))
            edge = 3.1415925
            own.link(V.tensor_scalar(shifted[:, :], angle[:, :], float(np.pi / 2), None, ALU.add))
            own.link(V.tensor_scalar(turns[:, :], shifted[:, :], float(np.pi), -two_pi, ALU.is_gt, ALU.mult))
            own.link(V.tensor_tensor(shifted[:, :], shifted[:, :], turns[:, :], ALU.add))
            V.tensor_scalar(angle[:, :], angle[:, :], -edge, edge, ALU.max, ALU.min).then_inc(angles, 1)
            V.tensor_scalar(shifted[:, :], shifted[:, :], -edge, edge, ALU.max, ALU.min).then_inc(angles, 1)
            dve.wait_ge(gains_landed, 16)
            for j in range(KT // 2):
                if j % 2 == 0:
                    dve.wait_ge(x_landed[j // 2], 16)
                low_operand(ahi, alo, GAIN_AT["ln_attn_0"], j)
            first_split(0, 0, CW // 2, half_hi, half_lo)
            first_split(0, CW // 2)
            for j in range(KT // 2):
                add_squares(j)
            first_split(1)
            inverse_root()
            dve.wait_ge(dist_ready, 1)
            V.tensor_tensor(by_dist[:, :], bank[0:HEADS, 2, 0:CAUSAL], negmask[:, :], ALU.add).then_inc(dist_done, 1)
            through(BY_NAME["moba_qk"], scaled_into(qk1))
            dve.wait_ge(sines, 2)
            own.link(V.tensor_scalar(sin_t[:, :], sin_t[:, :], consts[:, C_SIGN - C_IDENT:C_SIGN - C_IDENT + 1], None,
                                     ALU.mult))
            token_scale(1)
            dve.wait_ge(bank_read, BY_NAME["moba_v"].bank_base)
            dve.wait_ge(dist_stored, 32)
            stage_first_q(1)
            through(BY_NAME["moba_v"], tokens_into(v1, D), held=True)
            dve.wait_ge(bias_landed, 16)
            attention(0, 1, BY_NAME["moba_v"])
            through_into_norm(BY_NAME["moba_o"], residual, into_operand(a2hi, a2lo, "ln_mlp_0"))
            for n in range(2):
                if n == 1:
                    stage = BY_NAME["dsa_in"]
                    latents = (z_q, z_kv)
                    for c in range(2):
                        dve.wait_ge(chunk_used, stage.base + c + 1)
                        V.tensor_tensor(latents[c][:, :, :],
                                        bank[:, lin_bank(stage, c), :].rearrange("p (a t) -> p a t", a=2),
                                        both(rstd[:, 0, :]), ALU.mult).then_inc(bank_read, 1)
                        if c == 0:
                            split(stage, 0, c)
                    n_sq[0] += 2
                    dve.wait_ge(squares, n_sq[0])
                    n_sums[0] += 1
                    V.tensor_tensor(ssum[:, :, :], sq[:, 0:4:2, :], sq[:, 1:4:2, :], ALU.add).then_inc(sums, 1)
                    dve.wait_ge(low_bank, 1)
                    V.tensor_tensor(k_idx[:, :], bank[:, lin_bank(stage, 2), 0:SEQ], rstd[:, 0, :], ALU.mult)\
                     .then_inc(bank_read, 1)
                    split(stage, 0, 1)
                    dve.wait_ge(chunk_used, stage.base + 3)
                    V.scalar_tensor_tensor(w_rows[:, :], bank[0:IDX_HEADS, lin_bank(stage, 3), 0:SEQ], IDX_SCALE,
                                           rstd[0:IDX_HEADS, 0, :], ALU.mult, ALU.mult).then_inc(bank_read, 1)
                    dve.wait_ge(bank_read, stage.bank_base + 4)
                    inverse_root()
                    for c in range(2):
                        V.tensor_tensor(latents[c][:, :, :], latents[c][:, :, :], both(rstd[:, c, :]), ALU.mult)\
                         .then_inc(latent_ready, 1)
                        if c == 0:
                            own.link(V.reciprocal(rstd[:, 1, :], std[:, 1, :]))
                        else:
                            dve.wait_ge(latent_ready, 2)
                        for k in range(2):
                            g = LATENT_GAIN_AT + 2 * c + k
                            n_hi[0] += 1
                            dve.wait_ge(act_hi, n_hi[0])
                            V.scalar_tensor_tensor(alo[:, 2 * c + k, :], latents[c][:, k, :], gains[:, g:g + 1],
                                                   plain(ahi[:, 2 * c + k, :]), ALU.mult, ALU.subtract)\
                             .then_inc(op_ready, 1)
                    split(stage, 0, 2)
                    stage = BY_NAME["dsa_low"]
                    dve.wait_ge(w_turned, 1)
                    own.link(V.tensor_copy(w_idx[:, :, :].rearrange("p t h -> p (t h)"),
                                           bank[:, O_BANKS[0], 0:QT * IDX_HEADS]))
                    for h in range(IDX_HEADS):
                        dve.wait_ge(idx_relu, h + 1)
                        for t, cols in ((0, slice(0, P)), (1, slice(P, CAUSAL))):
                            w = w_idx[:, t, h:h + 1]
                            if h and t == 0:
                                dve.wait_ge(own.sem, own.n)
                            elif h:
                                dve.wait_ge(idx_used, h)
                            if h == 0:
                                ins = V.tensor_scalar(score[:, cols], relu_s[:, 0, cols], w, None, ALU.mult)
                            else:
                                ins = V.scalar_tensor_tensor(score[:, cols], relu_s[:, h, cols], w,
                                                             score[:, cols], ALU.mult, ALU.add)
                            if t == 0:
                                own.count(ins)
                            else:
                                ins.then_inc(idx_used, 1)
                    dve.wait_ge(idx_used, IDX_HEADS)
                    split(stage, 0, 0)
                    dve.wait_ge(mask_landed, 32)
                    top_keys({0: 1, 4: 2}, stage)
                    dve.wait_ge(bank_read, BY_NAME["dsa_o"].bank_base)
                    dve.wait_ge(bias_landed, 32)
                    stage_first_q(1)
                    attention(1, 1, BY_NAME["dsa_low"], masked=True)
                    through_into_norm(BY_NAME["dsa_o"], residual, into_operand(a2hi, a2lo, "ln_mlp_1"))
                through(BY_NAME[f"up_{n}"], *relu_stage(BY_NAME[f"up_{n}"]))
                through_into_norm(BY_NAME[f"down_{n}"], residual,
                                  into_operand(ahi, alo, "ln_attn_1") if n == 0 else add_squares, waited=n == 1)
            normed_operand(BY_NAME["down_1"], "mix_pre_0", add=False)
            own.link(V.memset(gated[:, :, 0:2], 0.0))
            ch = BY_NAME["conv_ch"]

            def conv_step(i, u, j, b):
                V.tensor_tensor(z[:, :, :], b, both(rstd[:, 0, :]), ALU.mult).then_inc(bank_read, 1)
                dve.wait_ge(bank_read, i * ch.unroll + (ch.bank_base + u + 1))
                V.tensor_tensor(gated[:, bass.ds(j, 1), 2:2 + SEQ], z[:, 0:1, :], z[:, 1:2, :], ALU.mult)\
                 .then_inc(gate_ready, 1)

            def conv_tail(i, u, j, b):
                dve.wait_ge(gate_ready, i * ch.unroll + (u + 1))
                d = conv[:, bass.ds(j, 1), :]
                for tap in range(3):
                    w = gains[:, bass.ds(j * 3 + (CONV_AT + tap), 1)]
                    src = gated[:, bass.ds(j, 1), tap:tap + SEQ]
                    if tap == 0:
                        ins = V.tensor_scalar(d, src, w, None, ALU.mult)
                    else:
                        dve.wait_ge(tap_ready, i * (ch.unroll * 3) + (u * 3 + tap))
                        ins = V.scalar_tensor_tensor(d, src, w, d, ALU.mult, ALU.add)
                    ins.then_inc(tap_ready, 1)
            through(ch, conv_step, conv_tail)
            dve.wait_ge(tap_ready, 3 * KT)
            cb = BY_NAME["conv_b"]
            dve.wait_ge(chunk_used, cb.base)

            def gate_step(i, u, j, b):
                if u:
                    dve.wait_ge(conv_ready, u)
                V.tensor_tensor(z[:, :, :], b, both(rstd[:, 0, :]), ALU.mult).then_inc(bank_read, 1)
                dve.wait_ge(bank_read, i * cb.unroll + (cb.bank_base + u + 1))
                d = conv[:, bass.ds(j * 2, 2), :]
                V.tensor_tensor(d, z[:, :, :], d, ALU.mult).then_inc(conv_ready, 1)

            def gate_tail(i, u, j, b):
                n_hi[0] += 1
                dve.wait_ge(act_hi, n_hi[0])
                V.tensor_tensor(clo[:, 2 * u:2 * u + 2, :], conv[:, 2 * u:2 * u + 2, :],
                                plain(chi[:, 2 * u:2 * u + 2, :]), ALU.subtract).then_inc(op_ready, 1)
            through(cb, gate_step, gate_tail)
            through_into_norm(BY_NAME["conv_out"], before_norm, add_squares, waited=True)
            normed_operand(BY_NAME["conv_out"], "ffn_pre_0")
            for n in range(2):
                if n == 1:
                    V.tensor_tensor(cos_r[:, :], cos_t[:, :], rstd[:, 0, :], ALU.mult).then_inc(roped, 1)
                    own.link(V.tensor_tensor(sin_r[:, :], sin_t[:, :], rstd[:, 0, :], ALU.mult))
                    through(BY_NAME["dil_k"], *rope_stage(BY_NAME["dil_k"], k3),
                            also=lambda k: low_tile(a2hi, a2lo, GAIN_AT["mix_pre_1"], k))
                    through(BY_NAME["dil_q"], *rope_stage(BY_NAME["dil_q"], q3))
                    token_scale(2)
                    dve.wait_ge(roped, ROPED)
                    stage_first_q(NB)
                    through(BY_NAME["dil_v"], tokens_into(v3, QW), held=True)
                    dve.wait_ge(bank_read, BY_NAME["dil_o"].bank_base)
                    attention(2, NB, BY_NAME["dil_v"])
                    through_into_norm(BY_NAME["dil_o"], before_norm, add_squares, waited=True)
                    normed_operand(BY_NAME["dil_o"], "ffn_pre_1")
                gu, down = BY_NAME[f"gate_up_{n}"], BY_NAME[f"ffn_down_{n}"]
                through(gu, *swiglu_stage(gu))
                through_into_norm(down, before_norm, add_squares, waited=True)
                if n == 0:
                    normed_operand(BY_NAME["ffn_down_0"], "kv")
            for j in range(KT // 2):
                normed(j, True)


def buckets():
    n = np.arange(SEQ)
    exact = BUCKETS // 2
    large = np.log(np.maximum(n, 1).astype(np.float32) / np.float32(exact)) / np.float32(np.log(MAX_DISTANCE / exact))
    large = exact + (large * np.float32(BUCKETS - exact)).astype(np.int32)
    return np.where(n < exact, n, np.minimum(large, BUCKETS - 1))


def shape_constants():
    consts = np.zeros((P, CONST_COLS), np.float32)
    q = np.arange(P)[:, None]
    j = np.arange(CAUSAL)[None, :]
    dist = np.where(j < P, q - j, P + q - (j - P))
    for g, (window, dilation) in enumerate(BRANCHES):
        seen = (dist >= 0) & (dist <= window) & (dist % dilation == 0)
        consts[:, C_MASK + g * CAUSAL:C_MASK + (g + 1) * CAUSAL] = np.where(seen, 0.0, NEG)
    consts[:, C_CAUSAL:C_IDENT] = np.where(dist >= 0, 0.0, NEG)
    consts[:, C_IDENT:C_IDENT + P] = np.eye(P)
    half = DH // 2
    freq = (10000.0 ** (-np.arange(half, dtype=np.float32).astype(np.float64) / half)).astype(np.float32)
    consts[:, C_FREQ] = np.tile(freq, P // half)
    consts[:, C_SIGN] = np.where(np.arange(P) % DH < half, -1.0, 1.0)
    at_dist = 2 * P - 1 - np.arange(CAUSAL)
    b = buckets()
    onehot = np.zeros((BUCKETS, CAUSAL), np.float32)
    for u in range(CAUSAL):
        if at_dist[u] >= 0:
            onehot[b[at_dist[u]], u] = 1.0
    negmask = np.broadcast_to(np.where(at_dist >= 0, 0.0, NEG).astype(np.float32), (HEADS, CAUSAL))
    return consts, onehot, np.ascontiguousarray(negmask)


def packed(inp):
    stream = np.zeros((CHUNKS, P, CW), np.float32)
    at = [0]

    def put(tiles):
        k, _, n = tiles.shape
        stream[at[0], :, :k * n] = tiles.transpose(1, 0, 2).reshape(P, k * n)
        at[0] += 1

    def by_pairs(w, starts):
        w = w.reshape(-1, P, w.shape[1])
        for a, b in starts:
            put(np.concatenate([w[:, :, a:a + P], w[:, :, b:b + P]], axis=2))

    def across(w, lo, hi):
        by_pairs(w, [(c, c + P) for c in range(lo, hi, 2 * P)])

    def quartered(w, tiles):
        for c in range(0, D, 2 * P):
            for k0, nk in QUARTERS[tiles]:
                by_pairs(w[k0 * P:(k0 + nk) * P], [(c, c + P)])

    def low(w):
        w = w.reshape(2, P, -1)
        put(np.concatenate([w, np.zeros((2, P, 1024 - w.shape[2]), np.float32)], axis=2))

    across(inp["moba_w_qkv"][0], 0, 3 * D)
    across(inp["moba_w_o"][0], 0, D)
    for n in range(2):
        if n == 1:
            w = inp["dsa_w_in"][0]
            across(w, 0, 2 * LORA)
            keys, weights = w[:, 2 * LORA:2 * LORA + DH], w[:, 2 * LORA + DH:]
            tail = np.concatenate([keys, keys, weights, np.zeros((D, P - IDX_HEADS), np.float32)], axis=1)
            across(tail, 0, 2 * P)
            low(inp["dsa_w_qi"][0])
            low(inp["dsa_w_uq"][0])
            low(inp["dsa_w_uk"][0].transpose(2, 0, 1).reshape(LORA, HEADS * DH))
            low(inp["dsa_w_uv"][0].transpose(1, 0, 2).reshape(LORA, HEADS * DH))
            across(inp["dsa_w_o"][0], 0, D)
        across(inp["mlp_w_up"][n], 0, FF)
        quartered(inp["mlp_w_down"][n], HID_TILES)
    by_pairs(inp["conv_w_in_2"][0], [(D + c, 2 * D + c) for c in range(0, D, P)])
    across(inp["conv_w_in_2"][0], 0, D)
    across(inp["conv_w_out_2"][0], 0, D)
    for n in range(2):
        if n == 1:
            across(inp["w_kv_2"], 0, QW)
            across(inp["w_q_2"][0], 0, QW)
            across(inp["w_kv_2"], QW, 2 * QW)
            across(inp["w_o_2"][0], 0, D)
        by_pairs(inp["ffn_w_gate_up_2"][n], [(c, FF2 + c) for c in range(0, FF2, P)])
        quartered(inp["ffn_w_down_2"][n], HID2_TILES)
    assert at[0] == CHUNKS
    return stream


def packed_gains(inp):
    rows = {"ln_attn_0": inp["ln_attn"][0], "ln_attn_1": inp["ln_attn"][1], "ln_mlp_0": inp["ln_mlp"][0],
            "ln_mlp_1": inp["ln_mlp"][1], "final": inp["final_norm"], "kv": inp["kv_norm_2"]}
    for n in range(2):
        rows[f"mix_pre_{n}"] = inp["mix_norm_pre_2"][n]
        rows[f"mix_post_{n}"] = inp["mix_norm_post_2"][n]
        rows[f"ffn_pre_{n}"] = inp["ffn_norm_pre_2"][n]
        rows[f"ffn_post_{n}"] = inp["ffn_norm_post_2"][n]
    cols = [rows[g].reshape(-1, P).T for g in GAINS]
    cols += [inp["dsa_g_q"][0].reshape(-1, P).T, inp["dsa_g_kv"][0].reshape(-1, P).T]
    cols += [inp["conv_w_2"][0].reshape(3, KT, P).transpose(2, 1, 0).reshape(P, KT * 3)]
    return np.ascontiguousarray(np.concatenate(cols, axis=1))


def kernel(**inputs):
    import concourse.bacc as bacc
    from concourse.bass_utils import run_bass_kernel_spmd

    inp = {name: np.asarray(a) for name, a in inputs.items()}
    consts, onehot, negmask = shape_constants()
    arrays = {
        "weight_stream": packed(inp),
        "x_features": np.ascontiguousarray(inp["x"][0].T.reshape(KT, P, SEQ).transpose(1, 0, 2)),
        "gain_columns": packed_gains(inp),
        "bias_table": np.ascontiguousarray(inp["rel_bias"]),
        "token_positions": np.ascontiguousarray(inp["positions_2"]),
        "shape_consts": consts,
        "bucket_onehot": onehot,
        "ahead_mask": negmask,
    }
    nc = bacc.Bacc("TRN2", target_bir_lowering=False, num_devices=1)
    args = [nc.dram_tensor(name, a.shape, mybir.dt.from_np(a.dtype), kind="ExternalInput").ap()
            for name, a in arrays.items()]
    toeplitz = nc.dram_tensor("bias_by_head", (HEADS, P, CAUSAL), F32).ap()
    out = nc.dram_tensor("out_features", (P, KT, SEQ), F32, kind="ExternalOutput").ap()
    build(nc, *args, toeplitz, out)
    r = run_bass_kernel_spmd(nc, [arrays], core_ids=[0])
    got = r.results[0]["out_features"]
    return np.ascontiguousarray(got.transpose(1, 0, 2).reshape(D, SEQ).T)[None]
```
